# Optimizing a Trainium2 kernel written in Bass

```python
import math
import jax
import jax.numpy as jnp
from jax import lax
import numpy as np

D_MODEL = 2048
BATCH = 1
SEQ = 256
DEPTH = 2

MIX_WIDTH = D_MODEL
SWA_WIDTH = MIX_WIDTH // 2
DN_WIDTH = MIX_WIDTH - SWA_WIDTH
HEAD_DIM = 64
N_Q_HEADS = SWA_WIDTH // HEAD_DIM
KV_GROUP = 8
N_KV_HEADS = N_Q_HEADS // KV_GROUP
WINDOW = 128
BLOCK = 128
ROPE_THETA = 10000.0
DN_HEAD_DIM = 128
DN_HEADS = DN_WIDTH // DN_HEAD_DIM
CONV_WIDTH = 4
CHUNK = 64
N_EXPERTS = 16
N_GROUPS = 4
EXPERTS_PER_GROUP = N_EXPERTS // N_GROUPS
TOP_K = 2
D_EXPERT = D_MODEL // 4
ALPHA = (2 * DEPTH) ** 0.25
BETA_INIT = (8 * DEPTH) ** -0.25
LN_EPS = 1e-5
RMS_EPS = 1e-6
SWA_KV_DIM = N_KV_HEADS * HEAD_DIM
DN_QKV_DIM = 3 * DN_WIDTH
PROJ_SIZES = (SWA_WIDTH, SWA_KV_DIM, SWA_KV_DIM, DN_QKV_DIM, DN_WIDTH, DN_HEADS, DN_HEADS)
PROJ_DIM = sum(PROJ_SIZES)

kernel_name = "hymba_swa_sink_gdn_grouped_moe_deepnorm"

def layer_norm(x, g, b):
    xf = x.astype(jnp.float32)
    mu = jnp.mean(xf, axis=-1, keepdims=True)
    xc = xf - mu
    var = jnp.mean(xc * xc, axis=-1, keepdims=True)
    return (xc * lax.rsqrt(var + LN_EPS) * g.astype(jnp.float32) + b.astype(jnp.float32)).astype(x.dtype)

def rope_tables(positions):
    inv_freq = 1.0 / (ROPE_THETA ** (jnp.arange(0, HEAD_DIM, 2, dtype=jnp.float32) / HEAD_DIM))
    ang = positions.astype(jnp.float32)[..., None] * inv_freq
    return jnp.cos(ang), jnp.sin(ang)

def apply_rope(x, cos, sin):
    xf = x.astype(jnp.float32)
    x1, x2 = jnp.split(xf, 2, axis=-1)
    c = cos[:, :, None, :]
    s = sin[:, :, None, :]
    return jnp.concatenate([x1 * c - x2 * s, x2 * c + x1 * s], axis=-1).astype(x.dtype)

def sliding_window_attention(q, k, v, sinks):
    B, S = q.shape[0], q.shape[1]
    nb = S // BLOCK
    qb = q.reshape(B, nb, BLOCK, N_KV_HEADS, KV_GROUP, HEAD_DIM)
    pad = ((0, 0), (BLOCK, 0), (0, 0), (0, 0))
    kp = jnp.pad(k, pad).reshape(B, nb + 1, BLOCK, N_KV_HEADS, HEAD_DIM)
    vp = jnp.pad(v, pad).reshape(B, nb + 1, BLOCK, N_KV_HEADS, HEAD_DIM)
    kb = jnp.concatenate([kp[:, :-1], kp[:, 1:]], axis=2)
    vb = jnp.concatenate([vp[:, :-1], vp[:, 1:]], axis=2)
    s = jnp.einsum('bnqhgd,bnkhd->bnhgqk', qb, kb).astype(jnp.float32) * (HEAD_DIM ** -0.5)
    qpos = jnp.arange(BLOCK)[:, None] + BLOCK
    kpos = jnp.arange(2 * BLOCK)[None, :]
    rel = qpos - kpos
    band = (rel >= 0) & (rel < WINDOW)
    not_pad = (jnp.arange(nb)[:, None, None] > 0) | (kpos >= BLOCK)[None]
    valid = band[None] & not_pad
    s = jnp.where(valid[None, :, None, None], s, -jnp.inf)
    sink = jnp.broadcast_to(
        sinks.astype(jnp.float32).reshape(N_KV_HEADS, KV_GROUP)[None, None, :, :, None, None],
        s.shape[:-1] + (1,))
    p = jax.nn.softmax(jnp.concatenate([s, sink], axis=-1), axis=-1)[..., :-1]
    o = jnp.einsum('bnhgqk,bnkhd->bnqhgd', p.astype(v.dtype), vb)
    return o.reshape(B, S, N_Q_HEADS * HEAD_DIM)

def causal_depthwise_conv(x, w):
    C = x.shape[-1]
    return lax.conv_general_dilated(
        x, w[:, None, :].astype(x.dtype), window_strides=(1,),
        padding=[(CONV_WIDTH - 1, 0)], dimension_numbers=('NWC', 'WIO', 'NWC'),
        feature_group_count=C)

def l2norm(x):
    return x * lax.rsqrt(jnp.sum(x * x, axis=-1, keepdims=True) + RMS_EPS)

def gated_delta_rule(q, k, v, g, beta):
    B, S, H, DK = q.shape
    DV = v.shape[-1]
    n = S // CHUNK

    def chunk(t):
        return t.reshape(B, n, CHUNK, H, -1).transpose(0, 3, 1, 2, 4)

    q, k, v = chunk(q), chunk(k), chunk(v)
    g = g.reshape(B, n, CHUNK, H).transpose(0, 3, 1, 2)
    beta = beta.reshape(B, n, CHUNK, H).transpose(0, 3, 1, 2)
    gc = jnp.cumsum(g, axis=-1)
    idx = jnp.arange(CHUNK)
    causal = idx[:, None] >= idx[None, :]
    strict = idx[:, None] > idx[None, :]
    decay = jnp.exp(jnp.where(causal, gc[..., :, None] - gc[..., None, :], -jnp.inf))
    kb = k * beta[..., None]
    vb = v * beta[..., None]
    L = jnp.where(strict, jnp.einsum('bhncd,bhnsd->bhncs', kb, k) * decay, 0.0)
    eye = jnp.eye(CHUNK, dtype=L.dtype)
    T = lax.linalg.triangular_solve(eye + L, jnp.broadcast_to(eye, L.shape),
                                    left_side=True, lower=True, unit_diagonal=True)
    u = jnp.einsum('bhncs,bhnsv->bhncv', T, vb)
    w = jnp.einsum('bhncs,bhnsk->bhnck', T, kb * jnp.exp(gc)[..., None])
    a_qk = jnp.where(causal, jnp.einsum('bhncd,bhnsd->bhncs', q, k) * decay, 0.0)
    qg = q * jnp.exp(gc)[..., None]
    kd = k * jnp.exp(gc[..., -1:] - gc)[..., None]
    glast = jnp.exp(gc[..., -1])
    xs = tuple(jnp.moveaxis(t, 2, 0) for t in (u, w, a_qk, qg, kd, glast))

    def step(state, inp):
        u_i, w_i, a_i, qg_i, kd_i, gl_i = inp
        v_new = u_i - jnp.einsum('bhck,bhkv->bhcv', w_i, state)
        o_i = jnp.einsum('bhck,bhkv->bhcv', qg_i, state) + jnp.einsum('bhcs,bhsv->bhcv', a_i, v_new)
        state = state * gl_i[..., None, None] + jnp.einsum('bhck,bhcv->bhkv', kd_i, v_new)
        return state, o_i

    s0 = jnp.zeros((B, H, DK, DV), jnp.float32)
    _, o = lax.scan(step, s0, xs)
    return o.transpose(1, 0, 3, 2, 4).reshape(B, S, H, DV)

def hybrid_mixer(h, w_in, sinks, conv_w, a_log, dt_bias, dn_norm_w, w_out, cos, sin):
    B, S, _ = h.shape
    proj = h @ w_in
    cuts = []
    off = 0
    for size in PROJ_SIZES[:-1]:
        off += size
        cuts.append(off)
    sq, sk, sv, dn_qkv, dn_z, dn_a, dn_b = jnp.split(proj, cuts, axis=-1)

    sq = apply_rope(sq.reshape(B, S, N_Q_HEADS, HEAD_DIM), cos, sin)
    sk = apply_rope(sk.reshape(B, S, N_KV_HEADS, HEAD_DIM), cos, sin)
    sv = sv.reshape(B, S, N_KV_HEADS, HEAD_DIM)
    attn_out = sliding_window_attention(sq, sk, sv, sinks)

    dn_qkv = jax.nn.silu(causal_depthwise_conv(dn_qkv, conv_w)).astype(jnp.float32)
    dq, dk, dv = jnp.split(dn_qkv, 3, axis=-1)
    dq = l2norm(dq.reshape(B, S, DN_HEADS, DN_HEAD_DIM)) * (DN_HEAD_DIM ** -0.5)
    dk = l2norm(dk.reshape(B, S, DN_HEADS, DN_HEAD_DIM))
    dv = dv.reshape(B, S, DN_HEADS, DN_HEAD_DIM)
    beta = jax.nn.sigmoid(dn_b.astype(jnp.float32))
    g = -jnp.exp(a_log.astype(jnp.float32)) * jax.nn.softplus(
        dn_a.astype(jnp.float32) + dt_bias.astype(jnp.float32))
    o = gated_delta_rule(dq, dk, dv, g, beta)
    z = dn_z.reshape(B, S, DN_HEADS, DN_HEAD_DIM).astype(jnp.float32)
    o = (o * lax.rsqrt(jnp.mean(o * o, axis=-1, keepdims=True) + RMS_EPS)
         * dn_norm_w.astype(jnp.float32) * jax.nn.silu(z))
    dn_out = o.reshape(B, S, DN_WIDTH).astype(h.dtype)

    return jnp.concatenate([attn_out, dn_out], axis=-1) @ w_out

def grouped_moe(h, router_w, router_bias, w_gate, w_up, w_down):
    B, S, D = h.shape
    t = h.reshape(-1, D)
    scores = jax.nn.sigmoid((t @ router_w).astype(jnp.float32))
    sel = scores + router_bias.astype(jnp.float32)
    grp_top = lax.top_k(sel.reshape(-1, N_GROUPS, EXPERTS_PER_GROUP), 2)[0]
    gidx = jnp.argmax(jnp.sum(grp_top, axis=-1), axis=-1)
    in_group = (jnp.arange(N_EXPERTS) // EXPERTS_PER_GROUP)[None, :] == gidx[:, None]
    _, eidx = lax.top_k(jnp.where(in_group, sel, -jnp.inf), TOP_K)
    wsel = jnp.take_along_axis(scores, eidx, axis=-1)
    wsel = wsel / jnp.sum(wsel, axis=-1, keepdims=True)
    gates = jnp.sum(jax.nn.one_hot(eidx, N_EXPERTS, dtype=jnp.float32) * wsel[..., None], axis=1)
    a = jnp.einsum('td,edf->etf', t, w_gate)
    u = jnp.einsum('td,edf->etf', t, w_up)
    hidden = jax.nn.silu(a) * u * gates.T.astype(t.dtype)[..., None]
    out = jnp.einsum('etf,efd->td', hidden, w_down)
    return out.reshape(B, S, D)

def setup_inputs(seed: int = 0) -> dict:
    key = jax.random.key(seed)
    ks = jax.random.split(key, 20)
    f32 = jnp.float32

    def nrm(k, shape, scale):
        return jax.random.normal(k, shape, f32) * scale

    x = nrm(ks[0], (BATCH, SEQ, D_MODEL), 1.0)
    positions = jnp.broadcast_to(jnp.arange(SEQ, dtype=jnp.int32), (BATCH, SEQ))
    w_in = nrm(ks[1], (DEPTH, D_MODEL, PROJ_DIM), D_MODEL ** -0.5)
    attn_sinks = nrm(ks[2], (DEPTH, N_Q_HEADS), 0.5)
    conv_w = nrm(ks[3], (DEPTH, CONV_WIDTH, DN_QKV_DIM), CONV_WIDTH ** -0.5)
    a_log = jnp.log(jax.random.uniform(ks[4], (DEPTH, DN_HEADS), f32, 1.0, 16.0))
    dt = jnp.exp(jax.random.uniform(ks[5], (DEPTH, DN_HEADS), f32, math.log(1e-3), math.log(1e-1)))
    dt_bias = dt + jnp.log(-jnp.expm1(-dt))
    dn_norm_w = 1.0 + nrm(ks[6], (DEPTH, DN_HEAD_DIM), 0.02)
    w_out = nrm(ks[7], (DEPTH, MIX_WIDTH, D_MODEL), MIX_WIDTH ** -0.5 * BETA_INIT)
    ln1_g = 1.0 + nrm(ks[8], (DEPTH, D_MODEL), 0.02)
    ln1_b = nrm(ks[9], (DEPTH, D_MODEL), 0.02)
    router_w = nrm(ks[10], (D_MODEL, N_EXPERTS), D_MODEL ** -0.5)
    router_bias = nrm(ks[11], (N_EXPERTS,), 0.01)
    w_gate = nrm(ks[12], (DEPTH, N_EXPERTS, D_MODEL, D_EXPERT), D_MODEL ** -0.5)
    w_up = nrm(ks[13], (DEPTH, N_EXPERTS, D_MODEL, D_EXPERT), D_MODEL ** -0.5)
    w_down = nrm(ks[14], (DEPTH, N_EXPERTS, D_EXPERT, D_MODEL), D_EXPERT ** -0.5 * BETA_INIT)
    ln2_g = 1.0 + nrm(ks[15], (DEPTH, D_MODEL), 0.02)
    ln2_b = nrm(ks[16], (DEPTH, D_MODEL), 0.02)
    return {"x": x, "positions": positions, "w_in": w_in, "attn_sinks": attn_sinks,
            "conv_w": conv_w, "a_log": a_log, "dt_bias": dt_bias, "dn_norm_w": dn_norm_w,
            "w_out": w_out, "ln1_g": ln1_g, "ln1_b": ln1_b, "router_w": router_w,
            "router_bias": router_bias, "w_gate": w_gate, "w_up": w_up, "w_down": w_down,
            "ln2_g": ln2_g, "ln2_b": ln2_b}

def reference(x, positions, w_in, attn_sinks, conv_w, a_log, dt_bias, dn_norm_w, w_out,
              ln1_g, ln1_b, router_w, router_bias, w_gate, w_up, w_down, ln2_g, ln2_b):
    cos, sin = rope_tables(positions)
    for l in range(DEPTH):
        mix = hybrid_mixer(x, w_in[l], attn_sinks[l], conv_w[l], a_log[l], dt_bias[l],
                           dn_norm_w[l], w_out[l], cos, sin)
        x = layer_norm(ALPHA * x + mix, ln1_g[l], ln1_b[l])
        ffn = grouped_moe(x, router_w, router_bias, w_gate[l], w_up[l], w_down[l])
        x = layer_norm(ALPHA * x + ffn, ln2_g[l], ln2_b[l])
    return x


_drawn_inputs = setup_inputs


def setup_inputs(seed=0):
    import zlib

    import numpy as np

    out = dict(_drawn_inputs(seed))
    spreads = {}
    factors = {'attn_sinks': 4.108, 'dn_norm_w': 3.969}
    for name, (base, spread) in spreads.items():
        noise = np.random.default_rng([zlib.crc32(name.encode()), seed]).standard_normal(out[name].shape)
        drawn = base * np.exp(spread * noise) if base else spread * noise
        out[name] = jnp.asarray(drawn.astype(out[name].dtype))
    for name, factor in factors.items():
        out[name] = (out[name] * factor).astype(out[name].dtype)
    return out
```

```python
from contextlib import ExitStack

import numpy as np

import concourse.bass as bass
from concourse import mybir

F32 = mybir.dt.float32
F32R = mybir.dt.float32r
I32 = mybir.dt.int32
ACT = mybir.ActivationFunctionType
ALU = mybir.AluOpType
AX = mybir.AxisListType

P = 128
WINDOW = 128
HEAD_DIM = 64
ROPE_THETA = 10000.0
LN_EPS = 1e-5
RMS_EPS = 1e-6
N_GROUPS = 4
SLOTS = 64
RING = 6
SIN_LIMIT = 3.1415925


class Signal:

    def __init__(self, sem, per):
        self.sem, self.per = sem, per

    def at(self, turn, n):
        return turn * self.per + n


class Steps:

    def __init__(self, eng, counted, turn):
        self.eng, self.counted, self.turn, self.n = eng, counted, turn, 0

    def do(self, ins):
        self.n += 1
        return ins.then_inc(self.counted.sem, 1)

    def sync(self):
        self.eng.wait_ge(self.counted.sem, self.counted.at(self.turn, self.n))

    def link(self, ins):
        self.do(ins)
        self.sync()

    def close(self):
        if self.counted.per != self.n:
            raise ValueError(f"{self.counted.sem.name} takes {self.n} steps a turn, not {self.counted.per}")


def bc(ap, axis, n):
    ap = ap.unsqueeze(axis)
    shape = list(ap.shape)
    shape[axis] = n
    return ap.to_broadcast(shape)


def trunk(nc, x_in, positions, w_in, attn_sinks, conv_w, a_log, dt_bias, dn_norm_w, w_out, ln1_g, ln1_b,
          router_w, router_bias, w_gate, w_up, w_down, ln2_g, ln2_b, out):
    depth, D, proj_dim = w_in.shape
    T = x_in.shape[1]
    NT = T // P
    KC = D // P
    n_q = attn_sinks.shape[1]
    q_dim = n_q * HEAD_DIM
    n_dn = a_log.shape[1]
    dk = dn_norm_w.shape[1]
    dn_dim = n_dn * dk
    kv_dim = (proj_dim - q_dim - 4 * dn_dim - 2 * n_dn) // 2
    n_kv = kv_dim // HEAD_DIM
    n_exp = router_w.shape[1]
    F = w_gate.shape[3]
    FC = F // P
    EPG = n_exp // N_GROUPS
    EXTRA = 2 * T // SLOTS
    TURNS = n_exp + EXTRA
    ALPHA = float((2 * depth) ** 0.25)
    HALF = n_dn // 2
    PANEL = 512
    PIECE = 4 * PANEL
    assert (T, NT, KC, HALF * P, FC) == (2 * P, 2, 16, PANEL, 4) and n_kv == 2 and dk == P

    off_kv = q_dim
    off_dn = q_dim + 2 * kv_dim
    off_z = off_dn + 3 * dn_dim
    off_ab = off_z + dn_dim
    IN_PANELS = [("q", 0), ("q", PANEL), ("kv", off_kv)]
    IN_PANELS += [("dn", off_dn + which * dn_dim + half * PANEL) for half in range(2) for which in range(3)]
    IN_PANELS += [("z", off_z), ("z", off_z + PANEL)]
    N_IN = len(IN_PANELS)
    N_OUT = D // PANEL
    MIX_PIECES = 4 * (N_IN + N_OUT)
    EXP_PIECES = 12
    assert MIX_PIECES % RING == 0 and EXP_PIECES == 2 * RING
    MIX_USES = MIX_PIECES // RING
    LEVELS = P.bit_length() - 1
    N_FLAGS = 3 * n_exp

    ctx = ExitStack()
    with ctx:
        def sb(name, shape, dt=F32):
            return ctx.enter_context(nc.sbuf_tensor(name, shape, dt))

        def signal(name, per):
            return Signal(ctx.enter_context(nc.semaphore(name)), per)

        ring = sb("ring", [P, RING, PIECE])
        x_nat = sb("x_nat", [P, NT, D])
        x_t = sb("x_t", [P, KC * T])
        xT = x_t[:, :].rearrange("p (c t) -> p c t", c=KC)
        mix_acc = sb("mix_acc", [P, KC * T])
        mixT = mix_acc[:, :].rearrange("p (c t) -> p c t", c=KC)
        acc = mix_acc[:, :].rearrange("p (t d) -> p t d", t=NT)

        region_a = sb("region_a", [P, 7168])
        region_a_at = nc.sbuf_base - 4 * 7168
        probs = region_a[:, 0:6144].rearrange("p (h k) -> p h k", h=n_q)

        def dn_mat(i):
            return region_a[:, i * 1024:(i + 1) * 1024].rearrange("p (t h c) -> p t h c", t=NT, h=HALF)

        decay, l_t, a_t, inv, inv_t, masked = (dn_mat(i) for i in range(6))
        gate_part = region_a[:, 0:512]
        up_part = region_a[:, 512:1024]
        act_t = region_a[:, 1024:1280]
        hid_t = region_a[:, 1280:1536].rearrange("p (f s) -> p f s", f=FC)
        pick = region_a[:, 1536:1792].rearrange("p (t s) -> p t s", t=NT)
        y_hi = nc.alloc_sbuf_tensor_at("y_hi", [P, D], F32R, offset=region_a_at + 4 * 1792)
        y_lo = nc.alloc_sbuf_tensor_at("y_lo", [P, D], F32R, offset=region_a_at + 4 * (1792 + D))
        scat_rows = nc.alloc_sbuf_tensor_at("scat_rows", [P, NT * P], F32R,
                                            offset=region_a_at + 4 * (1792 + 2 * D))
        scat = scat_rows[:, :].rearrange("p (t c) -> p t c", t=NT)
        assert 1792 + 2 * D + NT * P <= 7168
        region_b = sb("region_b", [P, 6144])
        qkv_t = region_b[:, :].rearrange("p (f w h t) -> p f w h t", f=2, w=3, h=HALF)
        region_cd = sb("region_cd", [P, 2 * NT * q_dim])
        region_c = region_cd[:, 0:NT * q_dim]
        q_rot = region_c[:, :].rearrange("p (t n) -> p t n", t=NT)
        z_act = q_rot
        region_d = region_cd[:, NT * q_dim:]
        q_t = region_d[:, :].rearrange("p (c t) -> p c t", t=T)
        o_nat = region_d[:, :].rearrange("p (t n) -> p t n", t=NT)
        ln_par = region_cd[:, 0:2 * D].rearrange("p (g d) -> p g d", g=2)

        slot_gate = sb("slot_gate", [P, 1])
        gate_col = sb("gate_col", [P, NT])
        k_rot = sb("k_rot", [P, NT, n_kv, 2, HEAD_DIM])
        v_nat = sb("v_nat", [P, NT, n_kv * HEAD_DIM])
        k_t = sb("k_t", [P, n_kv, T])
        v_rot = sb("v_rot", [P, 2 * PANEL])
        rot_a = v_rot[:, 0:PANEL]
        rot_b = v_rot[:, PANEL:2 * PANEL]
        conv_sq = sb("conv_sq", [P, 4 * PANEL])
        conv_y = conv_sq[:, 0:2 * PANEL].rearrange("p (a c) -> p a c", a=2)
        square = conv_sq[:, 2 * PANEL:].rearrange("p (a c) -> p a c", a=2)
        prob_t = sb("prob_t", [P, 4, 3 * P])
        xg_t = prob_t[:, :, :].rearrange("p a c -> p (a c)")[:, 0:KC * SLOTS].rearrange("p (c s) -> p c s", c=KC)
        v_beta = v_rot[:, :].rearrange("p (t h c) -> p t h c", t=NT, h=HALF)
        k_in = conv_y[:, 0, :].rearrange("p (h c) -> p h c", h=HALF)
        k_out = conv_y[:, 1, :].rearrange("p (h c) -> p h c", h=HALF)
        v_new = square[:, :, :].rearrange("p t (h c) -> p t h c", h=HALF)
        
        def w_t(h):
            return prob_t[:, h // 2, (h % 2) * P:(h % 2 + 1) * P]

        def state(h):
            return prob_t[:, 2 + h // 2, (h % 2) * P:(h % 2 + 1) * P]


        ident = sb("ident", [P, P])
        tri = sb("tri", [P, P])
        tri_strict = sb("tri_strict", [P, P])
        ones = sb("ones", [P, P])
        level_mask = sb("level_mask", [P, LEVELS, P])
        win_mask = sb("win_mask", [P, 3 * P])
        slot_id = sb("slot_id", [P, P])
        fold = sb("fold", [P, SLOTS])
        before = sb("before", [P, EPG, EPG])
        flag_exp = sb("flag_exp", [P, N_FLAGS])
        flag_off = sb("flag_off", [P, N_FLAGS])
        extra_id = sb("extra_id", [P, EXTRA])
        iota_i = sb("iota_i", [P, P], I32)
        inv_freq = sb("inv_freq", [P, HEAD_DIM // 2])
        cos_t = sb("cos_t", [P, NT, HEAD_DIM // 2])
        sin_t = sb("sin_t", [P, NT, HEAD_DIM // 2])
        ang = sb("ang", [P, 4, NT, HEAD_DIM // 2])
        pos_i = sb("pos_i", [P, NT], I32)
        pos_f = sb("pos_f", [P, NT])
        eps_dn = sb("eps_dn", [P, 3])

        w_rout = sb("w_rout", [P, KC, n_exp])
        b_rout = sb("b_rout", [P, n_exp])
        w_ab = sb("w_ab", [P, KC, 2 * n_dn])
        sinks = sb("sinks", [P, n_q])
        a_log_b = sb("a_log_b", [P, n_dn])
        dt_b = sb("dt_b", [P, n_dn])
        dn_w = sb("dn_w", [P, P])
        taps_nat = sb("taps_nat", [4 * 3 * n_dn, P])
        taps = sb("taps", [P, 4 * 3 * n_dn])

        mx = sb("mx", [P, NT, n_q])
        sink_e = sb("sink_e", [P, NT, n_q])
        row_sum = sb("row_sum", [P, NT, n_q])
        gates = sb("gates", [P, 10, NT, n_dn])
        g_nat = sb("g_nat", [P, NT, n_dn])
        beta = sb("beta", [P, NT, n_dn])
        gc = sb("gc", [P, 3, n_dn])
        gfac = sb("gfac", [P, 4, n_dn])
        rms = sb("rms", [P, 4, HALF])
        stats = sb("stats", [P, NT, D // PANEL, 6])
        mean_var = sb("mean_var", [P, NT, 2])
        ln_s = sb("ln_s", [P, 3, NT])
        r = sb("r", [P, 10, NT, n_exp])
        cmp_a = sb("cmp_a", [P, NT * N_GROUPS, EPG, EPG])
        cmp_b = sb("cmp_b", [P, NT * N_GROUPS, EPG, EPG])
        gr = sb("gr", [P, 3, NT, N_GROUPS])
        cum = sb("cum", [P, 2, N_FLAGS])
        flags = sb("flags", [P, N_FLAGS])
        route_tmp = prob_t[:, :, :].rearrange("p a c -> p (a c)")[:, 0:2 * EXTRA * N_FLAGS + EXTRA * n_exp]
        hot = route_tmp[:, 0:EXTRA * N_FLAGS].rearrange("p (j i) -> p j i", j=EXTRA)
        hot_w = route_tmp[:, EXTRA * N_FLAGS:2 * EXTRA * N_FLAGS].rearrange("p (j i) -> p j i", j=EXTRA)
        hot_e = route_tmp[:, 2 * EXTRA * N_FLAGS:].rearrange("p (j e) -> p j e", j=EXTRA)
        ext = sb("ext", [P, 3, EXTRA])
        slot_of = sb("slot_of", [P, NT, TURNS])
        gate_of = sb("gate_of", [P, NT, TURNS])
        turns_f = sb("turns_f", [P, depth + 1])
        turns = sb("turns", [P, depth + 1], I32)
        turn_n = sb("turn_n", [P, 1], I32)
        extra_n = sb("extra_n", [P, depth], I32)
        extra_e = sb("extra_e", [P, EXTRA], I32)

        bank = [ctx.enter_context(nc.psum_tensor(f"bank{i}", [P, PANEL], F32)) for i in range(8)]

        consts = signal("consts", 0)
        pool_steps = signal("pool_steps", 0)
        once_loaded = signal("once_loaded", 0)
        rope_act = signal("rope_act", 0)
        rope_dve = signal("rope_dve", 0)
        dve_setup = signal("dve_setup", 0)
        ring_free = signal("ring_free", 0)
        landed = [signal(f"landed{i}", 0) for i in range(2 * RING)]
        layer_open = signal("layer_open", 1)
        small_loaded = signal("small_loaded", 96)
        taps_done = signal("taps_done", 1)
        ln1_loaded = signal("ln1_loaded", 32)
        ln2_loaded = signal("ln2_loaded", 32)
        xt_done = signal("xt_done", 16)
        xt_act = signal("xt_act", 8)
        xt_dve = signal("xt_dve", 8)
        proj_done = signal("proj_done", 2 * (N_IN + N_OUT))
        proj_read = signal("proj_read", N_IN + N_OUT - 2)
        z_read = signal("z_read", 2)
        ab_done = signal("ab_done", 1)
        ab_act = signal("ab_act", 3)
        ab_dve = signal("ab_dve", 2)
        g_ready = signal("g_ready", 1)
        roped = signal("roped", 3)
        tq_done = signal("tq_done", 5)
        tq_read = signal("tq_read", 5)
        score_done = signal("score_done", n_q)
        score_read = signal("score_read", n_q)
        max_ready = signal("max_ready", 1)
        exp_done = signal("exp_done", 1)
        probs_ready = signal("probs_ready", 1)
        pt_done = signal("pt_done", n_q)
        pt_read = signal("pt_read", n_q)
        pv_done = signal("pv_done", n_q)
        pv_read = signal("pv_read", n_q // 2)
        conv_ready = signal("conv_ready", 12)
        silu_done = signal("silu_done", 12)
        square_ready = signal("square_ready", 8)
        ss_done = signal("ss_done", 8)
        norm_sqrt = signal("norm_sqrt", 8)
        normed = signal("normed", 8)
        gc_done = signal("gc_done", 1)
        gc_dve = signal("gc_dve", 1)
        gc_act = signal("gc_act", 1)
        factors_ready = signal("factors_ready", 1)
        spread_ready = signal("spread_ready", 4)
        spread_done = signal("spread_done", 4)
        decay_arg = signal("decay_arg", 4)
        decay_exp = signal("decay_exp", 4)
        pair_done = signal("pair_done", 4)
        pair_read = signal("pair_read", 4)
        kv_done = signal("kv_done", 4)
        kv_read = signal("kv_read", 4)
        inv_open = signal("inv_open", 2)
        lt_done = signal("lt_done", 4 * LEVELS)
        masked_ready = signal("masked_ready", 4 * LEVELS)
        tlt_done = signal("tlt_done", 4 * LEVELS)
        inv_ready = signal("inv_ready", 4 * LEVELS)
        u0_done = signal("u0_done", 2)
        v0_ready = signal("v0_ready", 2)
        s_done = signal("s_done", 2)
        s_ready = signal("s_ready", 2)
        v1_done = signal("v1_done", 2)
        v1_ready = signal("v1_ready", 2)
        o1_done = signal("o1_done", 2)
        o_ready = signal("o_ready", 2)
        rms_arg = signal("rms_arg", 4)
        rms_sqrt = signal("rms_sqrt", 4)
        dn_out = signal("dn_out", 4)
        to_done = signal("to_done", 4)
        to_read = signal("to_read", 4)
        res_ready = signal("res_ready", 2)
        ln_sqrt = signal("ln_sqrt", 4)
        ln_fac = signal("ln_fac", 4)
        ln_norm = signal("ln_norm", 4)
        ln_done = signal("ln_done", 4)
        logit_done = signal("logit_done", 1)
        logit_exp = signal("logit_exp", 1)
        member_ready = signal("member_ready", 1)
        rank_done = signal("rank_done", 1)
        route_ready = signal("route_ready", 1)
        route_seen = signal("route_seen", 1)
        moe_open = signal("moe_open", 1)
        act_steps = signal("act_steps", 5)
        dve_steps = signal("dve_steps", 348)
        gather_done = signal("gather_done", 2)
        gather_read = signal("gather_read", 2)
        pick_ready = signal("pick_ready", 1)
        gateup_done = signal("gateup_done", 2)
        gate_read = signal("gate_read", 1)
        up_read = signal("up_read", 1)
        scat_put = signal("scat_put", 8)
        scat_added = signal("scat_added", 8)
        scat_ready = signal("scat_ready", 1)
        fold_done = signal("fold_done", 1)
        silu_ready = signal("silu_ready", 1)
        hid_ready = signal("hid_ready", 1)
        down_done = signal("down_done", 4)
        hi_ready = signal("hi_ready", 4)
        y_ready = signal("y_ready", 4)
        stored = signal("stored", 0)

        w_in_v = w_in.rearrange("l (k p) n -> l p k n", p=P)
        w_out_v = w_out.rearrange("l (k p) n -> l p k n", p=P)
        w_gate_v = w_gate.rearrange("l e (k p) f -> (l e) p k f", p=P)
        w_up_v = w_up.rearrange("l e (k p) f -> (l e) p k f", p=P)
        w_down_v = w_down.rearrange("l e (f p) d -> (l e) p f d", p=P)

        def piece(n):
            return ring[:, n % RING, :].rearrange("p (k n) -> p k n", k=4)

        exp_slot = [ring[:, n, :] for n in range(RING)]
        exp_slot += [region_b[:, n * PIECE:(n + 1) * PIECE] for n in range(3)]
        exp_slot += [conv_sq[:, :], x_t[:, 0:PIECE], x_t[:, PIECE:2 * PIECE]]

        block = ctx.enter_context(nc.Block())

        @block.gpsimd
        def _(pool):
            s = Steps(pool, pool_steps, 0)

            def select(ap, op, fill, base, pattern):
                s.link(pool.affine_select(out=ap, in_=ap, compare_op=op, fill=fill, base=base,
                                          pattern=pattern, channel_multiplier=1))

            s.do(pool.memset(ones[:, :], 1.0))
            s.do(pool.memset(ident[:, :], 0.0))
            s.do(pool.memset(tri[:, :], 0.0))
            s.do(pool.memset(tri_strict[:, :], 0.0))
            s.do(pool.memset(level_mask[:, :, :], 0.0))
            s.do(pool.memset(win_mask[:, :], -1e30))
            s.do(pool.memset(fold[:, :], 0.0))
            s.do(pool.memset(before[:, :, :], 0.0))
            s.do(pool.memset(flag_off[:, :], 0.0))
            s.do(pool.memset(turns[:, :], 0))
            s.do(pool.memset(turns_f[:, :], 0.0))
            s.do(pool.memset(eps_dn[:, 0:1], float(dk * RMS_EPS)))
            s.do(pool.memset(eps_dn[:, 1:2], RMS_EPS))
            s.do(pool.memset(eps_dn[:, 2:3], LN_EPS))
            for i in range(HEAD_DIM // 2):
                f = np.float32(1.0) / np.power(np.float32(ROPE_THETA), np.float32(2 * i / HEAD_DIM))
                s.do(pool.memset(inv_freq[:, i:i + 1], float(f)))
            s.sync()
            select(ident[:, :], ALU.not_equal, 1.0, 0, [[-1, P]])
            select(tri[:, :], ALU.is_gt, 1.0, 0, [[-1, P]])
            select(tri_strict[:, :], ALU.is_ge, 1.0, 0, [[-1, P]])
            select(fold[:, :], ALU.not_equal, 1.0, 0, [[-1, SLOTS]])
            select(fold[:, :], ALU.not_equal, 1.0, -SLOTS, [[-1, SLOTS]])
            for j in (0, 2):
                own = win_mask[:, j * P:(j + 1) * P]
                s.link(pool.affine_select(out=own, in_=own, compare_op=ALU.is_gt, fill=0.0, base=0,
                                          pattern=[[1, P]], channel_multiplier=-1))
            select(win_mask[:, P:2 * P], ALU.is_ge, 0.0, 0, [[-1, P]])
            for lev in range(LEVELS):
                b = 1 << lev
                m = level_mask[:, lev, :].rearrange("p (n j i) -> p n j i", j=2, i=b)[:, :, 0, :]
                nb = P // (2 * b)
                s.link(pool.memset(m, -1.0))
                s.link(pool.affine_select(out=m, in_=m, compare_op=ALU.is_ge, fill=0.0, base=-b,
                                          pattern=[[-2 * b, nb], [0, b]], channel_multiplier=1))
                s.link(pool.affine_select(out=m, in_=m, compare_op=ALU.is_ge, fill=0.0, base=2 * b - 1,
                                          pattern=[[2 * b, nb], [0, b]], channel_multiplier=-1))
            s.link(pool.affine_select(out=before[:, :, :], in_=before[:, :, :], compare_op=ALU.is_ge, fill=1.0,
                                      base=0, pattern=[[-1, EPG], [1, EPG]], channel_multiplier=0))
            for tau in range(3):
                s.do(pool.memset(flag_off[:, tau * n_exp:(tau + 1) * n_exp], float(SLOTS * (tau + 1))))
            s.link(pool.iota(iota_i[:, 0:N_FLAGS], pattern=[[0, 3], [1, n_exp]], base=0, channel_multiplier=0))
            s.link(pool.tensor_copy(flag_exp[:, :], iota_i[:, 0:N_FLAGS]))
            s.link(pool.iota(iota_i[:, 0:EXTRA], pattern=[[1, EXTRA]], base=1, channel_multiplier=0))
            s.link(pool.tensor_copy(extra_id[:, :], iota_i[:, 0:EXTRA]))
            s.link(pool.iota(iota_i[:, :], pattern=[[0, 2], [1, SLOTS]], base=0, channel_multiplier=0))
            pool.tensor_copy(slot_id[:, :], iota_i[:, :]).then_inc(consts.sem, 1)

        @block.sync
        def _(sp):
            for t in range(NT):
                sp.dma_start(x_nat[:, t, :], x_in[0, t * P:(t + 1) * P, :]).then_inc(once_loaded.sem, 16)
            with nc.allow_non_contiguous_dma(reason="256 positions, one for each token's partition"):
                sp.dma_start(pos_i[:, :], positions.rearrange("b (t p) -> p (b t)", p=P)).then_inc(once_loaded.sem, 16)
            sp.dma_start(w_rout[:, :, :], router_w.rearrange("(k p) e -> p k e", p=P)).then_inc(once_loaded.sem, 16)
            sp.dma_start(b_rout[:, :], router_bias.partition_broadcast(P)).then_inc(once_loaded.sem, 16)
            sp.wait_ge(consts.sem, 1)

            def load(n, first, src):
                sp.wait_ge(ring_free.sem, first + (n + 1 if n < RING else n + 1 + RING))
                dst = piece(n)
                if src.shape[-1] != PANEL:
                    dst = dst[:, :, 0:src.shape[-1]]
                sp.dma_start(dst, src).then_inc(landed[n % RING].sem, 16)

            def expert(first, le, l=None):
                for j in range(EXP_PIECES):
                    if l is None or j >= RING:
                        sp.wait_ge(ring_free.sem, first + (j + 1))
                    else:
                        sp.wait_ge(ring_free.sem, first + (j + 1 + RING))
                    if l is not None and j == RING:
                        sp.wait_ge(o_ready.sem, o_ready.at(l, 2))
                    if l is not None and j == EXP_PIECES - 2:
                        sp.wait_ge(logit_done.sem, logit_done.at(l, 1))
                    dst = exp_slot[j]
                    if j < 8:
                        w = (w_gate_v, w_up_v)[j // 4]
                        dst = dst.rearrange("p (k n) -> p k n", k=4)
                        src = w[bass.ds(le, 1), :, 4 * (j % 4):4 * (j % 4) + 4, :].rearrange("a p k f -> (a p) k f")
                    else:
                        src = w_down_v[bass.ds(le, 1), :, j - 8, :].rearrange("a p d -> (a p) d")
                    sp.dma_start(dst, src).then_inc(landed[j].sem, 16)

            with sp.Fori(0, depth) as l:
                turns0 = sp.value_load(turns[0:1, bass.ds(l, 1)], min_val=0, max_val=depth * TURNS)
                first = sp.snap(l * MIX_PIECES + turns0 * EXP_PIECES)

                def row(a):
                    return a[bass.ds(l, 1)].rearrange("a n -> (a n)").partition_broadcast(P)

                n = 0
                for i, (kind, c0) in enumerate(IN_PANELS):
                    width = 2 * kv_dim if kind == "kv" else PANEL
                    for j in range(4):
                        load(n, first, w_in_v[bass.ds(l, 1), :, 4 * j:4 * j + 4, c0:c0 + width]
                             .rearrange("a p k n -> (a p) k n"))
                        n += 1
                    if i == 0:
                        sp.wait_ge(layer_open.sem, l + 1)
                        sp.dma_start(w_ab[:, :, :], w_in_v[bass.ds(l, 1), :, :, off_ab:off_ab + 2 * n_dn]
                                     .rearrange("a p k n -> (a p) k n")).then_inc(small_loaded.sem, 16)
                        sp.dma_start(taps_nat[:, :], conv_w[bass.ds(l, 1)].rearrange("a w (c p) -> (a w c) p", p=P))\
                            .then_inc(small_loaded.sem, 16)
                        for dst, src in ((sinks, attn_sinks), (a_log_b, a_log), (dt_b, dt_bias), (dn_w, dn_norm_w)):
                            sp.dma_start(dst[:, :], row(src)).then_inc(small_loaded.sem, 16)
                for i in range(N_OUT):
                    for j in range(4):
                        load(n, first, w_out_v[bass.ds(l, 1), :, 4 * j:4 * j + 4, i * PANEL:(i + 1) * PANEL]
                             .rearrange("a p k n -> (a p) k n"))
                        n += 1
                    if i == 1:
                        sp.wait_ge(to_done.sem, to_done.at(l, 4))
                        sp.dma_start(ln_par[:, 0, :], row(ln1_g)).then_inc(ln1_loaded.sem, 16)
                        sp.dma_start(ln_par[:, 1, :], row(ln1_b)).then_inc(ln1_loaded.sem, 16)
                first_e = sp.snap(l * MIX_PIECES + turns0 * EXP_PIECES + MIX_PIECES)
                expert(first_e, l * n_exp, l)
                sp.wait_ge(ln_done.sem, ln_done.at(l, 2))
                sp.dma_start(ln_par[:, 0, :], row(ln2_g)).then_inc(ln2_loaded.sem, 16)
                sp.dma_start(ln_par[:, 1, :], row(ln2_b)).then_inc(ln2_loaded.sem, 16)
                with sp.Fori(1, n_exp) as e:
                    expert(first_e + e * EXP_PIECES, l * n_exp + e)
                sp.wait_ge(route_ready.sem, l + 1)
                sp.sem_inc(route_seen.sem, 1)
                more = sp.value_load(extra_n[0:1, bass.ds(l, 1)], min_val=0, max_val=EXTRA)
                with sp.If(more > 0):
                    with sp.Fori(0, more) as j:
                        e = sp.value_load(extra_e[0:1, bass.ds(j, 1)], min_val=0, max_val=n_exp - 1)
                        expert(first_e + (n_exp + j) * EXP_PIECES, l * n_exp + e)

            sp.wait_ge(layer_open.sem, depth + 1)
            for t in range(NT):
                sp.dma_start(out[0, t * P:(t + 1) * P, :], x_nat[:, t, :]).then_inc(stored.sem, 16)
            sp.wait_ge(stored.sem, 16 * NT)

        @block.tensor
        def _(pe):
            pe.wait_ge(consts.sem, 1)

            def transposes(g, src, dst):
                for j in range(4):
                    last = pe.transpose(dst[:, j * P:(j + 1) * P], src(j), ident[:, :])
                return last

            def turn_x(l, rnd):
                for g in range(8):
                    t, c = g // 4, 4 * (g % 4)
                    transposes(g, lambda j: x_nat[:, t, (c + j) * P:(c + j + 1) * P], bank[g])\
                        .then_inc(xt_done.sem, 1)

            with pe.Fori(0, depth) as l:
                pe.wait_ge(layer_open.sem, l + 1)
                turns0 = pe.value_load(turns[0:1, bass.ds(l, 1)], min_val=0, max_val=depth * TURNS)
                uses = pe.snap(l * MIX_USES + turns0)

                def arrived(n, before_):
                    pe.wait_ge(landed[n % RING].sem, (before_ + (n // RING + 1)) * 16)

                turn_x(l, 0)
                pe.wait_ge(xt_act.sem, xt_act.at(l, 4))
                pe.wait_ge(xt_dve.sem, xt_dve.at(l, 4))

                def panel(i):
                    kind = IN_PANELS[i][0] if i < N_IN else "out"
                    if 2 <= i <= 10:
                        pe.wait_ge(proj_read.sem, proj_read.at(l, i - 1))
                    if i in (11, 12):
                        pe.wait_ge(z_read.sem, z_read.at(l, i - 10))
                    if i > 12:
                        pe.wait_ge(proj_read.sem, proj_read.at(l, i - 3))
                    owed = 2 if i == 0 else 1
                    b = [bank[2 * (i % 2)], bank[2 * (i % 2) + 1]]
                    width = 2 * kv_dim if kind == "kv" else PANEL
                    lhs = mixT if kind == "out" else xT
                    for j in range(4):
                        arrived(4 * i + j, uses)
                        w = piece(4 * i + j)
                        for kk in range(4):
                            k = 4 * j + kk
                            if kind == "dn":
                                for c in range(4):
                                    m = pe.matmul(b[c // 2][:, (c % 2) * T:(c % 2 + 1) * T],
                                                  w[:, kk, c * P:(c + 1) * P], xT[:, k, :],
                                                  start=(k == 0 and c % 2 == 0), stop=(k == KC - 1),
                                                  skip_group_check=True)
                                    if k == c == 0:
                                        m.then_inc(ring_free.sem, owed)
                                    if k == KC - 1 and c == 1:
                                        m.then_inc(proj_done.sem, 1)
                            else:
                                for t in range(NT):
                                    m = pe.matmul(b[t][:, 0:width], lhs[:, k, t * P:(t + 1) * P],
                                                  w[:, kk, 0:width], start=(k == 0), stop=(k == KC - 1))
                                    if k == t == 0:
                                        m.then_inc(ring_free.sem, owed)
                                    if k == KC - 1 and t == 0:
                                        m.then_inc(proj_done.sem, 1)
                            if kk == 3 and j < (2 if i == N_IN + N_OUT - 1 else 3):
                                m.then_inc(ring_free.sem, 1)
                    m.then_inc(proj_done.sem, 1)

                panel(0)
                panel(1)
                panel(2)
                pe.wait_ge(small_loaded.sem, small_loaded.at(l, 96))
                for t in range(NT):
                    for k in range(KC):
                        m = pe.matmul(bank[4][:, t * 2 * n_dn:(t + 1) * 2 * n_dn], xT[:, k, t * P:(t + 1) * P],
                                      w_ab[:, k, :], start=(k == 0), stop=(k == KC - 1))
                m = pe.transpose(bank[4][:, 64:64 + taps_nat.shape[0]], taps_nat[:, :],
                                 ident[0:taps_nat.shape[0], 0:taps_nat.shape[0]])
                m.then_inc(ab_done.sem, 1)

                for g in range(4):
                    t, c = g // 2, 4 * (g % 2)
                    pe.wait_ge(roped.sem, roped.at(l, 2))
                    if g == 3:
                        pe.wait_ge(tq_read.sem, tq_read.at(l, 1))
                    transposes(g, lambda j: q_rot[:, t, (c + j) * P:(c + j + 1) * P], bank[5 + g % 3])\
                        .then_inc(tq_done.sem, 1)
                pe.wait_ge(roped.sem, roped.at(l, 3))
                pe.wait_ge(tq_read.sem, tq_read.at(l, 2))
                transposes(4, lambda j: k_rot[:, j % 2, j // 2, :, :].rearrange("p a d -> p (a d)"), bank[6])\
                    .then_inc(tq_done.sem, 1)

                panel(3)
                pe.wait_ge(tq_read.sem, tq_read.at(l, 5))
                pe.wait_ge(ab_dve.sem, ab_dve.at(l, 2))
                for h in range(n_q):
                    lo = (h % 2) * HEAD_DIM
                    kv = h // (n_q // n_kv)
                    rows = slice(lo, lo + HEAD_DIM)
                    if h >= 4:
                        pe.wait_ge(score_read.sem, score_read.at(l, h - 3))
                    b = bank[4 + h % 4]
                    pe.matmul(b[:, 0:P], q_t[rows, h // 2, 0:P], k_t[rows, kv, 0:P], start=True, stop=True)
                    pe.matmul(b[:, P:3 * P], q_t[rows, h // 2, P:T], k_t[rows, kv, :], start=True, stop=True)\
                        .then_inc(score_done.sem, 1)
                panel(4)
                panel(5)

                def square_sums(half):
                    for u in range(4):
                        n = 4 * half + u
                        pe.wait_ge(square_ready.sem, square_ready.at(l, n + 1))
                        if u >= 2:
                            pe.wait_ge(norm_sqrt.sem, norm_sqrt.at(l, n - 1))
                        pe.matmul(bank[4 + u % 2][:, :], ones[:, :], square[:, n % 2, :], start=True, stop=True)\
                            .then_inc(ss_done.sem, 1)

                pe.wait_ge(score_read.sem, score_read.at(l, n_q))
                square_sums(0)
                panel(6)
                pe.wait_ge(probs_ready.sem, probs_ready.at(l, 1))
                pe.wait_ge(norm_sqrt.sem, norm_sqrt.at(l, 4))
                for h in range(n_q + 2):
                    if h < n_q:
                        if h >= 2:
                            pe.wait_ge(pt_read.sem, pt_read.at(l, h - 1))
                        for j in range(3):
                            m = pe.transpose(bank[4 + h % 2][:, j * P:(j + 1) * P],
                                             probs[:, h, j * P:(j + 1) * P], ident[:, :])
                        m.then_inc(pt_done.sem, 1)
                    if h >= 2:
                        hh = h - 2
                        lo = (hh % 2) * HEAD_DIM
                        kv = hh // (n_q // n_kv)
                        vs = slice(kv * HEAD_DIM, (kv + 1) * HEAD_DIM)
                        pe.wait_ge(pt_read.sem, pt_read.at(l, hh + 1))
                        if hh >= 4 and hh % 2 == 0:
                            pe.wait_ge(pv_read.sem, pv_read.at(l, hh // 2 - 1))
                        o = bank[6 + hh // 2 % 2][lo:lo + HEAD_DIM, 0:T]
                        pt = prob_t[:, hh % 4, :]
                        pe.matmul(o[:, 0:P], v_nat[:, 0, vs], pt[:, 0:P], start=True, stop=True)
                        pe.matmul(o[:, P:T], v_nat[:, 0, vs], pt[:, P:2 * P], start=True, stop=False)
                        pe.matmul(o[:, P:T], v_nat[:, 1, vs], pt[:, 2 * P:3 * P], start=False, stop=True)\
                            .then_inc(pv_done.sem, 1)
                panel(7)
                pe.wait_ge(g_ready.sem, g_ready.at(l, 1))
                pe.wait_ge(pv_read.sem, pv_read.at(l, n_q // 2))
                for t in range(NT):
                    pe.matmul(bank[4][:, t * n_dn:(t + 1) * n_dn], tri[:, :], g_nat[:, t, :], start=True, stop=True)
                pe.matmul(bank[4][:, 2 * n_dn:3 * n_dn], ones[:, :], g_nat[:, 0, :], start=True, stop=True)\
                    .then_inc(gc_done.sem, 1)
                panel(8)
                pe.wait_ge(gc_dve.sem, gc_dve.at(l, 1))
                square_sums(1)
                panel(9)
                panel(10)

                for half in range(2):
                    q_h, k_h, v_h = (qkv_t[:, half, w] for w in range(3))
                    pe.wait_ge(normed.sem, normed.at(l, 4 * half + 4))
                    pe.wait_ge(silu_done.sem, silu_done.at(l, 6 * half + 6))
                    for t in range(NT):
                        n = 2 * half + t
                        tok = slice(t * P, (t + 1) * P)
                        pe.wait_ge(spread_ready.sem, spread_ready.at(l, n + 1))
                        if t == 1 or half == 1:
                            pe.wait_ge(kv_read.sem, kv_read.at(l, n))
                        if t == 0 and half == 1:
                            pe.wait_ge(o_ready.sem, o_ready.at(l, 1))
                        pe.matmul(bank[4][:, :], ones[:, :], decay[:, t].rearrange("p h c -> p (h c)"),
                                  start=True, stop=True)
                        pe.matmul(bank[5][:, :], ones[:, :], l_t[:, t].rearrange("p h c -> p (h c)"),
                                  start=True, stop=True).then_inc(spread_done.sem, 1)
                        for h in range(HALF):
                            pe.matmul(bank[6][:, h * P:(h + 1) * P], k_h[:, h, tok], k_h[:, h, tok],
                                      start=True, stop=True)
                        for h in range(HALF):
                            m = pe.matmul(bank[7][:, h * P:(h + 1) * P], k_h[:, h, tok], q_h[:, h, tok],
                                          start=True, stop=True)
                        m.then_inc(pair_done.sem, 1)
                        pe.wait_ge(pair_read.sem, pair_read.at(l, n + 1))
                        transposes(0, lambda j: k_h[:, j, tok], bank[6])
                        transposes(0, lambda j: v_h[:, j, tok], bank[7]).then_inc(kv_done.sem, 1)
                    pe.wait_ge(kv_read.sem, kv_read.at(l, 2 * half + 2))
                    pe.wait_ge(inv_open.sem, inv_open.at(l, half + 1))
                    for lev in range(LEVELS):
                        for t in range(NT):
                            n = (half * LEVELS + lev) * NT + t
                            if lev:
                                pe.wait_ge(inv_ready.sem, inv_ready.at(l, n - 1))
                            for h in range(HALF):
                                m = pe.matmul(bank[4 + 2 * t][:, h * P:(h + 1) * P], l_t[:, t, h], inv[:, t, h],
                                              start=True, stop=True)
                            m.then_inc(lt_done.sem, 1)
                        for t in range(NT):
                            n = (half * LEVELS + lev) * NT + t
                            pe.wait_ge(masked_ready.sem, masked_ready.at(l, n + 1))
                            for h in range(HALF):
                                pe.matmul(bank[5 + 2 * t][:, h * P:(h + 1) * P], inv_t[:, t, h], masked[:, t, h],
                                          start=True, stop=True)
                            for h in range(HALF):
                                m = pe.matmul(bank[4 + 2 * t][:, h * P:(h + 1) * P], masked[:, t, h],
                                              inv_t[:, t, h], start=True, stop=True)
                            m.then_inc(tlt_done.sem, 1)
                    pe.wait_ge(inv_ready.sem, inv_ready.at(l, (half + 1) * LEVELS * NT))
                    for h in range(HALF):
                        pe.matmul(bank[4][:, h * P:(h + 1) * P], inv_t[:, 0, h], v_beta[:, 0, h], start=True, stop=True)
                    for h in range(HALF):
                        m = pe.matmul(bank[7][:, h * P:(h + 1) * P], k_in[:, h], inv_t[:, 1, h], start=True, stop=True)
                    m.then_inc(u0_done.sem, 1)
                    pe.wait_ge(v0_ready.sem, v0_ready.at(l, half + 1))
                    for h in range(HALF):
                        pe.matmul(bank[6][:, h * P:(h + 1) * P], k_out[:, h], v_new[:, 0, h], start=True, stop=True)
                    for h in range(HALF):
                        m = pe.matmul(bank[5][:, h * P:(h + 1) * P], a_t[:, 0, h], v_new[:, 0, h], start=True, stop=True)
                    m.then_inc(s_done.sem, 1)
                    pe.wait_ge(s_ready.sem, s_ready.at(l, half + 1))
                    for h in range(HALF):
                        pe.matmul(bank[4][:, h * P:(h + 1) * P], inv_t[:, 1, h], v_beta[:, 1, h], start=True, stop=False)
                        m = pe.matmul(bank[4][:, h * P:(h + 1) * P], w_t(h), state(h), start=False, stop=True)
                    m.then_inc(v1_done.sem, 1)
                    for h in range(HALF):
                        pe.matmul(bank[6][:, h * P:(h + 1) * P], q_h[:, h, P:T], state(h), start=True, stop=True)
                    pe.wait_ge(v1_ready.sem, v1_ready.at(l, half + 1))
                    for h in range(HALF):
                        m = pe.matmul(bank[7][:, h * P:(h + 1) * P], a_t[:, 1, h], v_new[:, 1, h], start=True, stop=True)
                    m.then_inc(o1_done.sem, 1)

                for half in range(2):
                    for t in range(NT):
                        n = 2 * half + t
                        pe.wait_ge(dn_out.sem, dn_out.at(l, n + 1))
                        if half == 0 and t == 0:
                            pe.wait_ge(o_ready.sem, o_ready.at(l, 2))
                        transposes(0, lambda j: o_nat[:, t, (half * HALF + j) * P:(half * HALF + j + 1) * P],
                                   bank[4 + n]).then_inc(to_done.sem, 1)
                pe.wait_ge(to_read.sem, to_read.at(l, 4))
                for i in range(N_IN, N_IN + N_OUT):
                    panel(i)

                pe.wait_ge(ln_done.sem, ln_done.at(l, 2))
                turn_x(l, 1)
                pe.wait_ge(xt_act.sem, xt_act.at(l, 8))
                pe.wait_ge(xt_dve.sem, xt_dve.at(l, 8))
                for t in range(NT):
                    for k in range(KC):
                        m = pe.matmul(bank[4][:, t * n_exp:(t + 1) * n_exp], xT[:, k, t * P:(t + 1) * P],
                                      w_rout[:, k, :], start=(k == 0), stop=(k == KC - 1))
                m.then_inc(logit_done.sem, 1)
                pe.wait_ge(member_ready.sem, member_ready.at(l, 1))
                member = r[:, 4]
                pe.matmul(bank[5][:, 0:n_exp], tri_strict[:, :], member[:, 0, :], start=True, stop=True)
                pe.matmul(bank[5][:, n_exp:2 * n_exp], tri_strict[:, :], member[:, 1, :], start=True, stop=False)
                pe.matmul(bank[5][:, n_exp:2 * n_exp], ones[:, :], member[:, 0, :], start=False, stop=True)
                pe.matmul(bank[5][:, 2 * n_exp:3 * n_exp], ones[:, :], member[:, 0, :], start=True, stop=False)
                pe.matmul(bank[5][:, 2 * n_exp:3 * n_exp], ones[:, :], member[:, 1, :], start=False, stop=True)\
                    .then_inc(rank_done.sem, 1)

                pe.wait_ge(moe_open.sem, l + 1)
                turns1 = pe.value_load(turns[0:1, bass.ds(l + 1, 1)], min_val=1, max_val=depth * TURNS)

                def gather(added=None):
                    for c in range(KC):
                        if c == 8 and added is not None:
                            pe.wait_ge(scat_added.sem, added)
                        o = bank[c // 8][:, (c % 8) * SLOTS:(c % 8 + 1) * SLOTS]
                        for t in range(NT):
                            m = pe.matmul(o, x_nat[:, t, c * P:(c + 1) * P], pick[:, t, 0:SLOTS],
                                          start=(t == 0), stop=(t == NT - 1))
                        if c % 8 == 7:
                            m.then_inc(gather_done.sem, 1)

                SCAT_BANKS = [1, 4, 5, 6, 7, 3, 1, 4]

                def scatter(i, last=False):
                    for n in range(8):
                        t, c = n // 4, n % 4
                        if n == 5 and not last:
                            pe.wait_ge(up_read.sem, i + 1)
                        if n >= 6:
                            pe.wait_ge(scat_added.sem, scat_added.at(i + l, n - 5))
                        pe.matmul(bank[SCAT_BANKS[n]][:, :], scat[:, t, :], y_hi[:, c * PANEL:(c + 1) * PANEL],
                                  start=True, stop=False)
                        pe.matmul(bank[SCAT_BANKS[n]][:, :], scat[:, t, :], y_lo[:, c * PANEL:(c + 1) * PANEL],
                                  start=False, stop=True).then_inc(scat_put.sem, 1)

                pe.wait_ge(pick_ready.sem, turns0 + (l + 1))
                gather()
                with pe.Fori(turns0, turns1) as i:
                    uses_e = pe.snap((l + 1) * MIX_USES + i)

                    def here(j):
                        pe.wait_ge(landed[j].sem, ((uses_e if j < RING else i) + 1) * 16)

                    pe.wait_ge(gather_read.sem, (i + l) * 2 + 2)
                    for t in range(NT):
                        pe.transpose(bank[0][:, t * P:(t + 1) * P], pick[:, t, :], ident[:, :])
                    for t in range(NT):
                        pe.matmul(bank[0][:, NT * P:NT * P + 1], pick[:, t, :], gate_col[:, t:t + 1],
                                  start=(t == 0), stop=(t == NT - 1))
                    for w in range(2):
                        for j in range(4):
                            n = 4 * w + j
                            here(n)
                            for kk in range(4):
                                k = 4 * j + kk
                                side = k % 2
                                m = pe.matmul(bank[2 + w][side * SLOTS:(side + 1) * SLOTS, :], xg_t[:, k, :],
                                              exp_slot[n][:, kk * PANEL:(kk + 1) * PANEL], start=(k < 2), stop=(k >= KC - 2))
                                if k == 0:
                                    m.then_inc(ring_free.sem, 2 - w)
                            m.then_inc(*((ring_free.sem, 1) if j < 3 else (gateup_done.sem, 1)))
                    pe.wait_ge(scat_ready.sem, i + (l + 1))
                    pe.wait_ge(y_ready.sem, (i + (l + 1)) * 4)
                    scatter(i)
                    pe.wait_ge(gate_read.sem, i + 1)
                    for w, part in enumerate((gate_part, up_part)):
                        for f in range(FC):
                            m = pe.matmul(bank[2][:, (w * FC + f) * SLOTS:(w * FC + f + 1) * SLOTS],
                                          part[:, f * P:(f + 1) * P], fold[:, :], start=True, stop=True)
                            if w == f == 0:
                                m.then_inc(ring_free.sem, 1)
                    m.then_inc(fold_done.sem, 1)
                    pe.wait_ge(pick_ready.sem, i + (l + 2))
                    pe.wait_ge(scat_ready.sem, i + (l + 2))
                    gather(scat_added.at(i + l, 7))
                    pe.wait_ge(scat_added.sem, scat_added.at(i + l, 8))
                    pe.wait_ge(hid_ready.sem, i + 1)
                    for pair in range(2):
                        for c in range(4):
                            for side in range(2):
                                f = 2 * pair + side
                                if c == 0:
                                    here(8 + f)
                                m = pe.matmul(bank[4 + c][side * SLOTS:(side + 1) * SLOTS, :], hid_t[:, f, :],
                                              exp_slot[8 + f][:, c * PANEL:(c + 1) * PANEL],
                                              start=(pair == 0), stop=(pair == 1))
                                if pair == 1 and c == side == 0:
                                    m.then_inc(ring_free.sem, 2)
                            if pair == 1:
                                m.then_inc(down_done.sem, 1)
                pe.wait_ge(scat_ready.sem, turns1 + (l + 1))
                pe.wait_ge(y_ready.sem, (turns1 + (l + 1)) * 4)
                pe.wait_ge(gather_read.sem, (turns1 + l) * 2 + 2)
                scatter(turns1, last=True)

        @block.scalar
        def _(act):
            act.wait_ge(consts.sem, 1)
            act.wait_ge(rope_dve.sem, 1)
            act.activation(sin_t[:, :, :], ang[:, 1], ACT.Sin).then_inc(rope_act.sem, 1)
            act.activation(cos_t[:, :, :], ang[:, 2], ACT.Sin).then_inc(rope_act.sem, 1)

            with act.Fori(0, depth) as l:
                act.wait_ge(layer_open.sem, l + 1)
                s = Steps(act, act_steps, l)

                def read_x(rnd):
                    for g in range(0, 8, 2):
                        t, c = g // 4, 4 * (g % 4)
                        act.wait_ge(xt_done.sem, xt_done.at(l, 8 * rnd + g + 1))
                        act.activation(xT[:, c:c + 4, t * P:(t + 1) * P],
                                       bank[g][:, :].rearrange("p (c t) -> p c t", c=4), ACT.Copy)\
                            .then_inc(xt_act.sem, 1)

                read_x(0)
                act.wait_ge(ab_dve.sem, ab_dve.at(l, 1))
                act.activation(gates[:, 1], gates[:, 0], ACT.Exp, scale=-1.0).then_inc(ab_act.sem, 1)
                s.do(act.activation(gates[:, 7, 0], a_log_b[:, :], ACT.Exp))
                act.activation(gates[:, 8], gates[:, 9], ACT.Exp, scale=-1.0).then_inc(ab_act.sem, 1)
                act.wait_ge(ab_dve.sem, ab_dve.at(l, 2))
                act.activation(gates[:, 3], gates[:, 2], ACT.Ln).then_inc(ab_act.sem, 1)
                for g in range(4):
                    t, c = g // 2, 4 * (g % 2)
                    act.wait_ge(tq_done.sem, tq_done.at(l, g + 1))
                    act.activation(q_t[:, c:c + 4, t * P:(t + 1) * P],
                                   bank[5 + g % 3][:, :].rearrange("p (c t) -> p c t", c=4), ACT.Copy)\
                        .then_inc(tq_read.sem, 1)
                act.wait_ge(tq_done.sem, tq_done.at(l, 5))
                act.activation(k_t[:, :, :].rearrange("p v t -> p (v t)"), bank[6][:, :], ACT.Copy)\
                    .then_inc(tq_read.sem, 1)

                def silu(n):
                    p, b = n // 2, n % 2
                    half, w = p // 3, p % 3
                    act.wait_ge(conv_ready.sem, conv_ready.at(l, n + 1))
                    act.activation(qkv_t[:, half, w, 2 * b:2 * b + 2, :].rearrange("p h t -> p (h t)"),
                                   conv_y[:, n % 2, :], ACT.Silu).then_inc(silu_done.sem, 1)

                def norms(half):
                    act.wait_ge(silu_done.sem, silu_done.at(l, 6 * half + 6))
                    for u in range(6):
                        n = 4 * half + u
                        if u < 4:
                            w, b = u // 2, u % 2
                            if n >= 2:
                                act.wait_ge(ss_done.sem, ss_done.at(l, n - 1))
                            act.activation(square[:, n % 2, :],
                                           qkv_t[:, half, w, 2 * b:2 * b + 2, :].rearrange("p h t -> p (h t)"),
                                           ACT.Square).then_inc(square_ready.sem, 1)
                        if u >= 2:
                            n = 4 * half + u - 2
                            w = (u - 2) // 2
                            act.wait_ge(ss_done.sem, ss_done.at(l, n + 1))
                            if n >= 2:
                                act.wait_ge(normed.sem, normed.at(l, n - 1))
                            act.activation(rot_ab[n % 2], bank[4 + n % 2][:, :], ACT.Sqrt,
                                           bias=eps_dn[:, w:w + 1], scale=float(dk) if w == 0 else 1.0)\
                                .then_inc(norm_sqrt.sem, 1)

                rot_ab = [rot_a[:, :], rot_b[:, :]]
                silu(0)
                silu(1)
                silu(2)
                silu(3)
                silu(4)
                silu(5)
                act.wait_ge(max_ready.sem, max_ready.at(l, 1))
                for h in range(n_q):
                    act.activation(probs[:, h, 0:P], probs[:, h, 0:P], ACT.Exp, bias=mx[:, 0, h:h + 1],
                                   accum_out=row_sum[:, 0, h:h + 1])
                    act.activation(probs[:, h, P:3 * P], probs[:, h, P:3 * P], ACT.Exp, bias=mx[:, 1, h:h + 1],
                                   accum_out=row_sum[:, 1, h:h + 1])
                act.activation(sink_e[:, :, :], sink_e[:, :, :], ACT.Exp).then_inc(exp_done.sem, 1)
                norms(0)
                silu(6)
                silu(7)
                for h in range(n_q):
                    act.wait_ge(pt_done.sem, pt_done.at(l, h + 1))
                    if h >= 4:
                        act.wait_ge(pv_done.sem, pv_done.at(l, h - 3))
                    act.activation(prob_t[:, h % 4, :], bank[4 + h % 2][:, 0:3 * P], ACT.Copy)\
                        .then_inc(pt_read.sem, 1)
                silu(8)
                silu(9)
                act.wait_ge(gc_dve.sem, gc_dve.at(l, 1))
                act.activation(gfac[:, 0:2, :], gfac[:, 0:2, :], ACT.Exp).then_inc(gc_act.sem, 1)
                silu(10)
                silu(11)
                norms(1)
                for i in range(2):
                    for t in range(NT):
                        act.wait_ge(proj_done.sem, proj_done.at(l, 2 * (9 + i) + t + 1))
                        z = act.activation(z_act[:, t, i * PANEL:(i + 1) * PANEL], bank[2 * ((9 + i) % 2) + t][:, :],
                                           ACT.Silu)
                    z.then_inc(z_read.sem, 1)

                for half in range(2):
                    for t in range(NT):
                        n = 2 * half + t
                        act.wait_ge(decay_arg.sem, decay_arg.at(l, n + 1))
                        d = decay[:, t].rearrange("p h c -> p (h c)")
                        act.activation(d, d, ACT.Exp).then_inc(decay_exp.sem, 1)
                    act.wait_ge(u0_done.sem, u0_done.at(l, half + 1))
                    s.do(act.activation(prob_t[:, 0:2, 0:2 * P], bank[7][:, :].rearrange("p (a c) -> p a c", a=2), ACT.Copy))
                    act.activation(v_new[:, 0].rearrange("p h c -> p (h c)"), bank[4][:, :], ACT.Copy)\
                        .then_inc(v0_ready.sem, 1)
                    act.wait_ge(s_done.sem, s_done.at(l, half + 1))
                    s.do(act.activation(o_nat[:, 0, half * PANEL:(half + 1) * PANEL], bank[5][:, :], ACT.Copy))
                    act.activation(prob_t[:, 2:4, 0:2 * P], bank[6][:, :].rearrange("p (a c) -> p a c", a=2), ACT.Copy)\
                        .then_inc(s_ready.sem, 1)
                    act.wait_ge(v1_done.sem, v1_done.at(l, half + 1))
                    act.activation(v_new[:, 1].rearrange("p h c -> p (h c)"), bank[4][:, :], ACT.Copy)\
                        .then_inc(v1_ready.sem, 1)
                    for t in range(NT):
                        n = 2 * half + t
                        act.wait_ge(rms_arg.sem, rms_arg.at(l, n + 1))
                        act.activation(rms[:, 1], rms[:, 0], ACT.Sqrt, bias=eps_dn[:, 1:2], scale=1.0 / dk)\
                            .then_inc(rms_sqrt.sem, 1)
                for n in range(4):
                    half, t = n // 2, n % 2
                    act.wait_ge(to_done.sem, to_done.at(l, n + 1))
                    c = q_dim // P + half * HALF
                    act.activation(mixT[:, c:c + HALF, t * P:(t + 1) * P],
                                   bank[4 + n][:, :].rearrange("p (c t) -> p c t", c=4), ACT.Copy)\
                        .then_inc(to_read.sem, 1)

                def layer_norm(rnd, src):
                    for t in range(NT):
                        n = 2 * rnd + t
                        act.wait_ge(res_ready.sem, res_ready.at(l, rnd + 1))
                        act.activation(ln_s[:, 0, t:t + 1], mean_var[:, t, 1:2], ACT.Sqrt, bias=eps_dn[:, 2:3])\
                            .then_inc(ln_sqrt.sem, 1)
                    for t in range(NT):
                        n = 2 * rnd + t
                        act.wait_ge(ln_fac.sem, ln_fac.at(l, n + 1))
                        act.activation(src[:, t, :], src[:, t, :], ACT.Identity, bias=ln_s[:, 2, t:t + 1],
                                       scale=ln_s[:, 1, t:t + 1]).then_inc(ln_norm.sem, 1)

                layer_norm(0, x_nat)
                act.wait_ge(ln_done.sem, ln_done.at(l, 2))
                read_x(1)
                act.wait_ge(logit_done.sem, logit_done.at(l, 1))
                act.activation(r[:, 0].rearrange("p t e -> p (t e)"), bank[4][:, 0:NT * n_exp], ACT.Exp, scale=-1.0)\
                    .then_inc(logit_exp.sem, 1)

                act.wait_ge(moe_open.sem, l + 1)
                turns0 = act.value_load(turns[0:1, bass.ds(l, 1)], min_val=0, max_val=depth * TURNS)
                turns1 = act.value_load(turns[0:1, bass.ds(l + 1, 1)], min_val=1, max_val=depth * TURNS)

                def gather_out(n):
                    for b in range(2):
                        act.wait_ge(gather_done.sem, n * 2 + (b + 1))
                        act.activation(xg_t[:, 8 * b:8 * b + 8, :].rearrange("p c s -> p (c s)"), bank[b][:, :],
                                       ACT.Copy).then_inc(gather_read.sem, 1)

                gather_out(turns0 + l)
                with act.Fori(turns0, turns1) as i:
                    act.wait_ge(gateup_done.sem, i * 2 + 1)
                    act.activation(gate_part, bank[2][:, :], ACT.Copy).then_inc(gate_read.sem, 1)
                    act.wait_ge(scat_put.sem, scat_put.at(i + l, 8))
                    act.activation(slot_gate[:, :], bank[0][:, NT * P:NT * P + 1], ACT.Copy)
                    act.activation(scat_rows[:, :], bank[0][:, 0:NT * P], ACT.Copy).then_inc(scat_ready.sem, 1)
                    act.wait_ge(fold_done.sem, i + 1)
                    act.activation(act_t, bank[2][:, 0:FC * SLOTS], ACT.Silu).then_inc(silu_ready.sem, 1)
                    gather_out(i + (l + 1))
                    for c in range(4):
                        act.wait_ge(down_done.sem, i * 4 + (c + 1))
                        if c == 0:
                            act.wait_ge(scat_ready.sem, i + (l + 2))
                        act.activation(y_hi[:, c * PANEL:(c + 1) * PANEL], bank[4 + c][:, :], ACT.Copy,
                                       scale=slot_gate[:, 0:1]).then_inc(hi_ready.sem, 1)
                layer_norm(1, acc)
                s.close()

        @block.vector
        def _(dve):
            tt, ts, stt = dve.tensor_tensor, dve.tensor_scalar, dve.scalar_tensor_tensor
            s = Steps(dve, dve_setup, 0)
            dve.wait_ge(consts.sem, 1)
            dve.wait_ge(once_loaded.sem, 16 * 5)
            s.link(dve.tensor_copy(pos_f[:, :], pos_i[:, :]))
            for t in range(NT):
                s.link(ts(ang[:, 0, t, :], inv_freq[:, :], pos_f[:, t:t + 1], None, ALU.mult))
            big = 1.5 * 2.0 ** 23
            parts = (6.28125, 1.93500518798828125e-3, 3.0199159819e-07)
            for j, shift in ((1, 0.0), (2, 0.25)):
                s.link(ts(ang[:, 3], ang[:, 0], 1.0 / (2.0 * np.pi), shift, ALU.mult, ALU.add))
                s.link(ts(ang[:, 3], ang[:, 3], big, -big, ALU.add, ALU.add))
                src = ang[:, 0]
                for part in parts:
                    s.link(stt(out=ang[:, j], in0=ang[:, 3], scalar=-part, in1=src, op0=ALU.mult, op1=ALU.add))
                    src = ang[:, j]
                if j == 2:
                    s.link(ts(ang[:, j], ang[:, j], float(np.pi / 2), None, ALU.add))
                s.link(ts(ang[:, j], ang[:, j], SIN_LIMIT, -SIN_LIMIT, ALU.min, ALU.max))
            dve.sem_inc(rope_dve.sem, 1)
            dve.wait_ge(rope_act.sem, 2)
            dve.sem_inc(ring_free.sem, 2 * RING - 2)
            dve.sem_inc(layer_open.sem, 1)

            with dve.Fori(0, depth) as l:
                dve.wait_ge(layer_open.sem, l + 1)
                s = Steps(dve, dve_steps, l)

                def read_x(rnd):
                    for g in range(1, 8, 2):
                        t, c = g // 4, 4 * (g % 4)
                        dve.wait_ge(xt_done.sem, xt_done.at(l, 8 * rnd + g + 1))
                        dve.tensor_copy(xT[:, c:c + 4, t * P:(t + 1) * P],
                                        bank[g][:, :].rearrange("p (c t) -> p c t", c=4)).then_inc(xt_dve.sem, 1)

                read_x(0)

                def rope(ps, t, heads, out_ap):
                    v = ps.rearrange("p (h r d) -> p h r d", h=heads, r=2)
                    n = heads * HEAD_DIM
                    a = rot_a[:, 0:n].rearrange("p (h d) -> p h d", h=2 * heads)
                    b = rot_b[:, 0:n].rearrange("p (h d) -> p h d", h=2 * heads)
                    src = ps.rearrange("p (h d) -> p h d", h=2 * heads)
                    s.do(tt(a, src, bc(cos_t[:, t, :], 1, 2 * heads), ALU.mult))
                    s.do(tt(b, src, bc(sin_t[:, t, :], 1, 2 * heads), ALU.mult))
                    s.sync()
                    a2 = rot_a[:, 0:n].rearrange("p (h r d) -> p h r d", h=heads, r=2)
                    b2 = rot_b[:, 0:n].rearrange("p (h r d) -> p h r d", h=heads, r=2)
                    return [(tt, out_ap(0), a2[:, :, 0, :], b2[:, :, 1, :], ALU.subtract),
                            (tt, out_ap(1), a2[:, :, 1, :], b2[:, :, 0, :], ALU.add)]

                for i in range(2):
                    for t in range(NT):
                        dve.wait_ge(proj_done.sem, proj_done.at(l, 2 * i + t + 1))
                        o = q_rot[:, t, i * PANEL:(i + 1) * PANEL].rearrange("p (h r d) -> p h r d", h=8, r=2)
                        ops = rope(bank[2 * i + t][:, :], t, 8, lambda half: o[:, :, half, :])
                        for f, *args in ops:
                            s.do(f(*args))
                        s.sync()
                    dve.sem_inc(proj_read.sem, 1)
                    dve.sem_inc(roped.sem, 1)
                for t in range(NT):
                    dve.wait_ge(proj_done.sem, proj_done.at(l, 4 + t + 1))
                    for dup in range(2):
                        ops = rope(bank[t][:, 0:kv_dim], t, n_kv,
                                   lambda half: k_rot[:, t, :, dup, half * 32:(half + 1) * 32])
                        for f, *args in ops:
                            s.do(f(*args))
                        s.sync()
                    s.do(dve.tensor_copy(v_nat[:, t, :], bank[t][:, kv_dim:2 * kv_dim]))
                s.sync()
                dve.sem_inc(proj_read.sem, 1)
                dve.sem_inc(roped.sem, 1)

                dve.wait_ge(ab_done.sem, ab_done.at(l, 1))
                dve.wait_ge(small_loaded.sem, small_loaded.at(l, 96))
                ab = bank[4][:, 0:4 * n_dn].rearrange("p (t w h) -> p t w h", t=NT, w=2)
                s.do(tt(gates[:, 4], ab[:, :, 0, :], bc(dt_b[:, :], 1, NT), ALU.add))
                s.do(dve.tensor_copy(gates[:, 9], ab[:, :, 1, :]))
                s.do(dve.tensor_copy(taps[:, :], bank[4][:, 64:64 + taps_nat.shape[0]]))
                s.sync()
                stt(out=gates[:, 0], in0=gates[:, 4], scalar=-1.0, in1=gates[:, 4], op0=ALU.mult, op1=ALU.max)\
                    .then_inc(ab_dve.sem, 1)
                dve.wait_ge(ab_act.sem, ab_act.at(l, 1))
                s.do(ts(gates[:, 5], gates[:, 4], 0.0, None, ALU.max))
                ts(gates[:, 2], gates[:, 1], 1.0, None, ALU.add).then_inc(ab_dve.sem, 1)
                dve.wait_ge(ab_act.sem, ab_act.at(l, 3))
                s.do(ts(gates[:, 8], gates[:, 8], 1.0, None, ALU.add))
                s.do(ts(gates[:, 2], gates[:, 2], -1.0, None, ALU.add))
                s.do(tt(gates[:, 3], gates[:, 3], gates[:, 1], ALU.mult))
                s.sync()
                s.link(ts(gates[:, 6], gates[:, 2], 0.0, None, ALU.is_equal))
                s.do(dve.reciprocal(beta[:, :, :], gates[:, 8]))
                s.do(tt(gates[:, 2], gates[:, 2], gates[:, 6], ALU.add))
                s.do(tt(gates[:, 6], gates[:, 6], gates[:, 1], ALU.mult))
                s.sync()
                s.do(tt(gates[:, 3], gates[:, 3], gates[:, 6], ALU.add))
                s.do(dve.reciprocal(gates[:, 2], gates[:, 2]))
                s.sync()
                s.link(tt(gates[:, 3], gates[:, 3], gates[:, 2], ALU.mult))
                s.link(tt(gates[:, 3], gates[:, 3], gates[:, 5], ALU.add))
                s.link(tt(gates[:, 3], gates[:, 3], bc(gates[:, 7, 0, :], 1, NT), ALU.mult))
                ts(g_nat[:, :, :], gates[:, 3], -1.0, None, ALU.mult).then_inc(g_ready.sem, 1)

                def conv(p):
                    half, w = p // 3, p % 3
                    i = 3 + p
                    for b in range(2):
                        n = 2 * p + b
                        dve.wait_ge(proj_done.sem, proj_done.at(l, 2 * i + b + 1))
                        if n >= 2:
                            dve.wait_ge(silu_done.sem, silu_done.at(l, n - 1))
                        chunk = w * n_dn + half * HALF + 2 * b
                        ps = bank[2 * (i % 2) + b]
                        for tap in range(4):
                            back = 3 - tap
                            for c in range(2):
                                w_c = taps[:, tap * 3 * n_dn + chunk + c:tap * 3 * n_dn + chunk + c + 1]
                                o = conv_y[:, n % 2, c * T:(c + 1) * T]
                                src = ps[:, c * T:(c + 1) * T]
                                if tap == 0:
                                    w_c = taps[:, 3 * 3 * n_dn + chunk + c:3 * 3 * n_dn + chunk + c + 1]
                                    s.do(ts(o, src, w_c, None, ALU.mult))
                                else:
                                    back = tap
                                    w_c = taps[:, (3 - tap) * 3 * n_dn + chunk + c:(3 - tap) * 3 * n_dn + chunk + c + 1]
                                    s.do(stt(out=o[:, back:T], in0=src[:, 0:T - back], scalar=w_c,
                                             in1=o[:, back:T], op0=ALU.mult, op1=ALU.add))
                            s.sync()
                        dve.sem_inc(conv_ready.sem, 1)
                    dve.sem_inc(proj_read.sem, 1)

                def normalise(half):
                    for u in range(4):
                        n = 4 * half + u
                        w, b = u // 2, u % 2
                        dve.wait_ge(norm_sqrt.sem, norm_sqrt.at(l, n + 1))
                        ra = (rot_a, rot_b)[n % 2]
                        s.link(dve.reciprocal(ra[:, :], ra[:, :]))
                        v = qkv_t[:, half, w, 2 * b:2 * b + 2, :].rearrange("p h t -> p (h t)")
                        tt(v, v, ra[:, :], ALU.mult).then_inc(normed.sem, 1)

                conv(0)
                for h in range(n_q):
                    dve.wait_ge(score_done.sem, score_done.at(l, h + 1))
                    stt(out=probs[:, h, :], in0=bank[4 + h % 4][:, 0:3 * P], scalar=HEAD_DIM ** -0.5,
                        in1=win_mask[:, :], op0=ALU.mult, op1=ALU.add).then_inc(score_read.sem, 1)
                dve.wait_ge(score_read.sem, score_read.at(l, n_q))
                s.do(dve.tensor_reduce(mx[:, 0, :], probs[:, :, 0:P], AX.X, ALU.max))
                s.do(dve.tensor_reduce(mx[:, 1, :], probs[:, :, P:3 * P], AX.X, ALU.max))
                s.sync()
                s.link(tt(mx[:, :, :], mx[:, :, :], bc(sinks[:, :], 1, NT), ALU.max))
                s.do(tt(sink_e[:, :, :], bc(sinks[:, :], 1, NT), mx[:, :, :], ALU.subtract))
                ts(mx[:, :, :], mx[:, :, :], -1.0, None, ALU.mult).then_inc(max_ready.sem, 1)
                conv(1)
                conv(2)
                dve.wait_ge(exp_done.sem, exp_done.at(l, 1))
                s.link(tt(row_sum[:, :, :], row_sum[:, :, :], sink_e[:, :, :], ALU.add))
                s.link(dve.reciprocal(row_sum[:, :, :], row_sum[:, :, :]))
                s.do(tt(probs[:, :, 0:P], probs[:, :, 0:P], bc(row_sum[:, 0, :], 2, P), ALU.mult))
                tt(probs[:, :, P:3 * P], probs[:, :, P:3 * P], bc(row_sum[:, 1, :], 2, 2 * P), ALU.mult)\
                    .then_inc(probs_ready.sem, 1)
                normalise(0)
                conv(3)
                for j in range(n_q // 2):
                    dve.wait_ge(pv_done.sem, pv_done.at(l, 2 * j + 2))
                    dve.tensor_copy(mixT[:, j, :], bank[6 + j % 2][:, 0:T]).then_inc(pv_read.sem, 1)
                conv(4)
                dve.wait_ge(gc_done.sem, gc_done.at(l, 1))
                s.link(dve.tensor_copy(gc[:, :, :].rearrange("p t h -> p (t h)"), bank[4][:, 0:3 * n_dn]))
                s.do(dve.tensor_copy(gfac[:, 1, :], gc[:, 1, :]))
                tt(gfac[:, 0, :], gc[:, 2, :], gc[:, 0, :], ALU.subtract).then_inc(gc_dve.sem, 1)
                conv(5)
                dve.wait_ge(gc_act.sem, gc_act.at(l, 1))
                s.link(tt(gfac[:, 2, :], gfac[:, 1, :], beta[:, 1, :], ALU.mult))
                s.link(ts(gfac[:, 2, :], gfac[:, 2, :], -1.0, None, ALU.mult))
                normalise(1)

                def heads(ap, half):
                    return ap[:, half * HALF:(half + 1) * HALF]

                def spread(half, t):
                    s.do(tt(decay[:, t], bc(tri[:, :], 1, HALF), bc(heads(g_nat[:, t, :], half), 2, P), ALU.mult))
                    tt(l_t[:, t], bc(ident[:, :], 1, HALF), bc(heads(beta[:, t, :], half), 2, P), ALU.mult)\
                        .then_inc(spread_ready.sem, 1)

                for half in range(2):
                    if half == 0:
                        dve.wait_ge(pt_done.sem, pt_done.at(l, n_q))
                    else:
                        dve.wait_ge(o1_done.sem, o1_done.at(l, 1))
                    spread(half, 0)
                    spread(half, 1)
                    for t in range(NT):
                        n = 2 * half + t
                        dve.wait_ge(spread_done.sem, spread_done.at(l, n + 1))
                        v4 = bank[4][:, :].rearrange("p (h c) -> p h c", h=HALF)
                        s.link(tt(decay[:, t], v4, bc(heads(gc[:, t, :], half), 2, P), ALU.subtract))
                        ts(decay[:, t], decay[:, t], 0.0, None, ALU.min).then_inc(decay_arg.sem, 1)
                        dve.wait_ge(pair_done.sem, pair_done.at(l, n + 1))
                        dve.wait_ge(decay_exp.sem, decay_exp.at(l, n + 1))
                        kk = bank[6][:, :].rearrange("p (h c) -> p h c", h=HALF)
                        qk = bank[7][:, :].rearrange("p (h c) -> p h c", h=HALF)
                        bb = bank[5][:, :].rearrange("p (h c) -> p h c", h=HALF)
                        s.link(tt(l_t[:, t], kk, decay[:, t], ALU.mult))
                        s.do(tt(l_t[:, t], bb, l_t[:, t], ALU.mult))
                        s.link(tt(decay[:, t], decay[:, t], bc(tri[:, :], 1, HALF), ALU.mult))
                        tt(a_t[:, t], qk, decay[:, t], ALU.mult).then_inc(pair_read.sem, 1)
                        dve.wait_ge(kv_done.sem, kv_done.at(l, n + 1))
                        if t == 0:
                            s.do(tt(k_out[:, :, :], kk, bc(heads(gfac[:, 0, :], half), 2, P), ALU.mult))
                        else:
                            s.do(tt(k_in[:, :, :], kk, bc(heads(gfac[:, 2, :], half), 2, P), ALU.mult))
                        tt(v_beta[:, t], qk, bc(heads(beta[:, t, :], half), 2, P), ALU.mult).then_inc(kv_read.sem, 1)
                    for t in range(NT):
                        s.do(dve.tensor_copy(inv[:, t], bc(ident[:, :], 1, HALF)))
                    s.do(dve.tensor_copy(inv_t[:, 0], bc(ident[:, :], 1, HALF)))
                    dve.tensor_copy(inv_t[:, 1], bc(ident[:, :], 1, HALF)).then_inc(inv_open.sem, 1)
                    for lev in range(LEVELS):
                        for t in range(NT):
                            n = (half * LEVELS + lev) * NT + t
                            dve.wait_ge(lt_done.sem, lt_done.at(l, n + 1))
                            tt(masked[:, t], bank[4 + 2 * t][:, :].rearrange("p (h c) -> p h c", h=HALF),
                               bc(level_mask[:, lev, :], 1, HALF), ALU.mult).then_inc(masked_ready.sem, 1)
                        for t in range(NT):
                            n = (half * LEVELS + lev) * NT + t
                            dve.wait_ge(tlt_done.sem, tlt_done.at(l, n + 1))
                            s.do(tt(inv[:, t], bank[5 + 2 * t][:, :].rearrange("p (h c) -> p h c", h=HALF),
                                    inv[:, t], ALU.add))
                            tt(inv_t[:, t], bank[4 + 2 * t][:, :].rearrange("p (h c) -> p h c", h=HALF),
                               inv_t[:, t], ALU.add).then_inc(inv_ready.sem, 1)
                    dve.wait_ge(o1_done.sem, o1_done.at(l, half + 1))
                    o = o_nat[:, :, half * PANEL:(half + 1) * PANEL].rearrange("p t (h c) -> p t h c", h=HALF)
                    s.link(tt(o[:, 1], bank[6][:, :].rearrange("p (h c) -> p h c", h=HALF),
                              bc(heads(gfac[:, 1, :], half), 2, P), ALU.mult))
                    tt(o[:, 1], bank[7][:, :].rearrange("p (h c) -> p h c", h=HALF), o[:, 1], ALU.add)\
                        .then_inc(o_ready.sem, 1)
                    dve.wait_ge(o_ready.sem, o_ready.at(l, half + 1))
                    dve.wait_ge(s_ready.sem, s_ready.at(l, half + 1))
                    dve.wait_ge(z_read.sem, z_read.at(l, 2))
                    for t in range(NT):
                        n = 2 * half + t
                        sq = decay[:, t]
                        s.link(tt(sq, o[:, t], o[:, t], ALU.mult))
                        dve.tensor_reduce(rms[:, 0], sq, AX.X, ALU.add).then_inc(rms_arg.sem, 1)
                        dve.wait_ge(rms_sqrt.sem, rms_sqrt.at(l, n + 1))
                        s.link(dve.reciprocal(rms[:, 2], rms[:, 1]))
                        s.link(tt(o[:, t], o[:, t], bc(rms[:, 2], 2, P), ALU.mult))
                        s.link(tt(o[:, t], o[:, t], bc(dn_w[:, :], 1, HALF), ALU.mult))
                        zz = z_act[:, t, half * PANEL:(half + 1) * PANEL].rearrange("p (h c) -> p h c", h=HALF)
                        tt(o[:, t], o[:, t], zz, ALU.mult).then_inc(dn_out.sem, 1)

                for i in range(N_OUT):
                    for t in range(NT):
                        dve.wait_ge(proj_done.sem, proj_done.at(l, 2 * (N_IN + i) + t + 1))
                        xs = x_nat[:, t, i * PANEL:(i + 1) * PANEL]
                        s.do(stt(out=xs, in0=xs, scalar=ALPHA, in1=bank[2 * ((N_IN + i) % 2) + t][:, :],
                                 op0=ALU.mult, op1=ALU.add))
                    s.sync()
                    dve.sem_inc(proj_read.sem, 1)

                def layer_norm(rnd, src, loaded):
                    for t in range(NT):
                        for c in range(D // PANEL):
                            s.do(dve.bn_stats(stats[:, t, c, :], src[:, t, c * PANEL:(c + 1) * PANEL]))
                    s.sync()
                    s.do(dve.memset(ln_s[:, :, :], 0.0))
                    s.do(dve.bn_aggr(mean_var[:, 0, :], stats[:, 0, :, :]))
                    dve.bn_aggr(mean_var[:, 1, :], stats[:, 1, :, :]).then_inc(res_ready.sem, 1)
                    for t in range(NT):
                        n = 2 * rnd + t
                        dve.wait_ge(ln_sqrt.sem, ln_sqrt.at(l, n + 1))
                        s.link(dve.reciprocal(ln_s[:, 1, t:t + 1], ln_s[:, 0, t:t + 1]))
                        stt(out=ln_s[:, 2, t:t + 1], in0=mean_var[:, t, 0:1], scalar=-1.0,
                            in1=ln_s[:, 1, t:t + 1], op0=ALU.mult, op1=ALU.mult).then_inc(ln_fac.sem, 1)
                    dve.wait_ge(loaded.sem, loaded.at(l, 32))
                    for t in range(NT):
                        n = 2 * rnd + t
                        dve.wait_ge(ln_norm.sem, ln_norm.at(l, n + 1))
                        s.link(tt(x_nat[:, t, :], src[:, t, :], ln_par[:, 0, :], ALU.mult))
                        tt(x_nat[:, t, :], x_nat[:, t, :], ln_par[:, 1, :], ALU.add).then_inc(ln_done.sem, 1)

                layer_norm(0, x_nat, ln1_loaded)
                dve.wait_ge(ln_done.sem, ln_done.at(l, 2))
                read_x(1)
                for t in range(NT):
                    s.do(ts(acc[:, t, :], x_nat[:, t, :], ALPHA, None, ALU.mult))

                score, sel, rank, top, member, wsel = (r[:, i] for i in range(6))
                gate = r[:, 6]
                dve.wait_ge(logit_exp.sem, logit_exp.at(l, 1))
                s.link(ts(r[:, 0], r[:, 0], 1.0, None, ALU.add))
                s.link(dve.reciprocal(r[:, 0], r[:, 0]))
                s.link(tt(sel, score, bc(b_rout[:, :], 1, NT), ALU.add))
                tg = NT * N_GROUPS

                def ranks(values, n, m, out_ap):
                    mine, other = bc(values, 3, m), bc(values, 2, m)
                    ca, cb = cmp_a[:, 0:n], cmp_b[:, 0:n]
                    s.do(tt(ca, other, mine, ALU.is_gt))
                    s.link(tt(cb, other, mine, ALU.is_equal))
                    s.link(tt(cb, cb, bc(before[:, :, :], 1, n), ALU.mult))
                    s.link(tt(ca, ca, cb, ALU.add))
                    s.link(dve.tensor_reduce(out_ap, ca, AX.X, ALU.add))

                def grouped(ap):
                    return ap.rearrange("p t (g e) -> p (t g) e", e=EPG)

                ranks(grouped(sel), tg, EPG, grouped(rank))
                s.link(ts(top, rank, 1.5, None, ALU.is_lt))
                s.link(tt(wsel, top, sel, ALU.mult))
                s.link(dve.tensor_reduce(gr[:, 0].rearrange("p t g -> p (t g)"), grouped(wsel), AX.X, ALU.add))
                ranks(gr[:, 0], NT, N_GROUPS, gr[:, 1])
                s.link(ts(gr[:, 2], gr[:, 1], 0.5, None, ALU.is_lt))
                tt(grouped(member), grouped(top), bc(gr[:, 2].rearrange("p t g -> p (t g)"), 2, EPG), ALU.mult)\
                    .then_inc(member_ready.sem, 1)
                dve.wait_ge(member_ready.sem, member_ready.at(l, 1))
                s.link(tt(wsel, member, score, ALU.mult))
                s.link(dve.tensor_reduce(gr[:, 0, :, 0], wsel, AX.X, ALU.add))
                s.link(dve.reciprocal(gr[:, 0, :, 1], gr[:, 0, :, 0]))
                s.link(tt(gate, wsel, bc(gr[:, 0, :, 1], 2, n_exp), ALU.mult))
                dve.wait_ge(rank_done.sem, rank_done.at(l, 1))
                slot1 = r[:, 7]
                pos = bank[5][:, 0:2 * n_exp].rearrange("p (t e) -> p t e", t=NT)
                s.link(ts(slot1, pos, 1.0, None, ALU.add))
                s.link(tt(slot1, slot1, member, ALU.mult))
                for tau in range(3):
                    s.do(ts(flags[:, tau * n_exp:(tau + 1) * n_exp], bank[5][:, 2 * n_exp:3 * n_exp],
                            SLOTS * (tau + 1) + 0.5, None, ALU.is_gt))
                s.sync()
                s.link(dve.tensor_copy(cum[:, 0, :], flags[:, :]))
                side, step = 0, 1
                while step < N_FLAGS:
                    s.do(dve.tensor_copy(cum[:, 1 - side, 0:step], cum[:, side, 0:step]))
                    s.link(tt(cum[:, 1 - side, step:], cum[:, side, step:], cum[:, side, 0:N_FLAGS - step], ALU.add))
                    side, step = 1 - side, 2 * step
                s.link(tt(hot[:, :, :], bc(cum[:, side, :], 1, EXTRA), bc(extra_id[:, :], 2, N_FLAGS), ALU.is_equal))
                s.link(tt(hot[:, :, :], hot[:, :, :], bc(flags[:, :], 1, EXTRA), ALU.mult))
                s.link(tt(hot_w[:, :, :], hot[:, :, :], bc(flag_exp[:, :], 1, EXTRA), ALU.mult))
                s.link(dve.tensor_reduce(ext[:, 0, :], hot_w[:, :, :], AX.X, ALU.add))
                s.link(tt(hot_w[:, :, :], hot[:, :, :], bc(flag_off[:, :], 1, EXTRA), ALU.mult))
                s.link(dve.tensor_reduce(ext[:, 1, :], hot_w[:, :, :], AX.X, ALU.add))
                s.do(dve.tensor_copy(extra_e[:, :], ext[:, 0, :]))
                s.do(dve.tensor_copy(extra_n[:, bass.ds(l, 1)], cum[:, side, N_FLAGS - 1:N_FLAGS]))
                s.link(dve.tensor_copy(ext[:, 2, 0:1], cum[:, side, N_FLAGS - 1:N_FLAGS]))
                s.link(tt(hot_e[:, :, :], hot[:, :, 0:n_exp], hot[:, :, n_exp:2 * n_exp], ALU.add))
                s.link(tt(hot_e[:, :, :], hot_e[:, :, :], hot[:, :, 2 * n_exp:3 * n_exp], ALU.add))
                s.do(ts(slot_of[:, :, 0:n_exp], slot1, -1.0, None, ALU.add))
                s.do(dve.tensor_copy(gate_of[:, :, 0:n_exp], gate))
                for t in range(NT):
                    h1 = hot_w[:, :, 0:n_exp]
                    s.link(tt(h1, hot_e[:, :, :], bc(slot1[:, t, :], 1, EXTRA), ALU.mult))
                    s.link(dve.tensor_reduce(slot_of[:, t, n_exp:], h1, AX.X, ALU.add))
                    s.link(tt(h1, hot_e[:, :, :], bc(gate[:, t, :], 1, EXTRA), ALU.mult))
                    s.link(dve.tensor_reduce(gate_of[:, t, n_exp:], h1, AX.X, ALU.add))
                    s.link(tt(slot_of[:, t, n_exp:], slot_of[:, t, n_exp:], ext[:, 1, :], ALU.subtract))
                    s.link(ts(slot_of[:, t, n_exp:], slot_of[:, t, n_exp:], -1.0, None, ALU.add))
                s.link(ts(turn_n[:, :], ext[:, 2, 0:1], float(n_exp), None, ALU.add))
                s.link(ts(ext[:, 2, 0:1], ext[:, 2, 0:1], turns_f[:, 0:1], float(n_exp), ALU.add, ALU.add))
                s.do(dve.tensor_copy(turns_f[:, 0:1], ext[:, 2, 0:1]))
                s.link(dve.memset(gate_part, 0.0))
                dve.tensor_copy(scat_rows[:, :], gate_part[:, 0:NT * P]).then_inc(scat_ready.sem, 1)
                dve.tensor_copy(y_hi[:, :].rearrange("p (a c) -> p a c", a=4), bc(gate_part, 1, 4))
                dve.tensor_copy(y_lo[:, :].rearrange("p (a c) -> p a c", a=4), bc(gate_part, 1, 4))\
                    .then_inc(y_ready.sem, 4)
                s.link(dve.tensor_copy(turns[:, bass.ds(l + 1, 1)], ext[:, 2, 0:1]))
                dve.sem_inc(route_ready.sem, 1)
                dve.sem_inc(moe_open.sem, 1)

                turns0 = dve.value_load(turns[0:1, bass.ds(l, 1)], min_val=0, max_val=depth * TURNS)
                turns1 = dve.value_load(turns[0:1, bass.ds(l + 1, 1)], min_val=1, max_val=depth * TURNS)

                n_turns = dve.value_load(turn_n[0:1, 0:1], min_val=n_exp, max_val=TURNS - 1)

                def pick_tokens(col):
                    dve.tensor_copy(gate_col[:, :], gate_of[:, :, bass.ds(col, 1)].rearrange("p t a -> p (t a)"))
                    for t in range(NT):
                        m = ts(pick[:, t, :], slot_id[:, :], slot_of[:, t, bass.ds(col, 1)], None, ALU.is_equal)
                    return m

                def add_scattered(i):
                    for n in range(8):
                        t, c = n // 4, n % 4
                        dve.wait_ge(scat_put.sem, scat_put.at(i + l, n + 1))
                        a = acc[:, t, c * PANEL:(c + 1) * PANEL]
                        tt(a, bank[[1, 4, 5, 6, 7, 3, 1, 4][n]][:, :], a, ALU.add).then_inc(scat_added.sem, 1)

                pick_tokens(0).then_inc(pick_ready.sem, 1)
                with dve.Fori(0, n_turns) as turn:
                    i = dve.snap(turns0 + turn)
                    dve.wait_ge(gateup_done.sem, i * 2 + 2)
                    dve.tensor_copy(up_part, bank[3][:, :]).then_inc(up_read.sem, 1)
                    pick_tokens(turn + 1).then_inc(pick_ready.sem, 1)
                    add_scattered(i)
                    dve.wait_ge(fold_done.sem, i + 1)
                    dve.wait_ge(silu_ready.sem, i + 1)
                    tt(hid_t[:, :, :].rearrange("p f s -> p (f s)"), bank[2][:, FC * SLOTS:2 * FC * SLOTS], act_t,
                       ALU.mult).then_inc(hid_ready.sem, 1)
                    for c in range(4):
                        dve.wait_ge(hi_ready.sem, i * 4 + (c + 1))
                        cols = slice(c * PANEL, (c + 1) * PANEL)
                        stt(out=y_lo[:, cols], in0=bank[4 + c][:, :], scalar=slot_gate[:, 0:1], in1=y_hi[:, cols],
                            op0=ALU.mult, op1=ALU.subtract).then_inc(y_ready.sem, 1)
                add_scattered(turns1)
                dve.wait_ge(scat_added.sem, scat_added.at(turns1 + l, 8))
                layer_norm(1, acc, ln2_loaded)
                dve.wait_ge(ln_done.sem, ln_done.at(l, 4))
                dve.sem_inc(layer_open.sem, 1)
                s.close()


_INS = ["x", "positions", "w_in", "attn_sinks", "conv_w", "a_log", "dt_bias", "dn_norm_w", "w_out", "ln1_g",
        "ln1_b", "router_w", "router_bias", "w_gate", "w_up", "w_down", "ln2_g", "ln2_b"]


def kernel(**inputs):
    import numpy as _np
    import concourse.bacc as _bacc
    from concourse import mybir as _mybir
    from concourse.bass_utils import run_bass_kernel_spmd as _run

    nc = _bacc.Bacc("TRN2", target_bir_lowering=False, num_devices=1)
    arrays, args = {}, []
    for name in _INS:
        a = _np.ascontiguousarray(inputs[name])
        arrays[f"in_{name}_dram"] = a
        args.append(nc.dram_tensor(f"in_{name}_dram", a.shape, _mybir.dt.from_np(a.dtype), kind="ExternalInput").ap())
    shape = tuple(inputs["x"].shape)
    args.append(nc.dram_tensor("out_0_dram", shape, _mybir.dt.float32, kind="ExternalOutput").ap())
    trunk(nc, *args)
    r = _run(nc, [arrays], core_ids=[0])
    return r.results[0]["out_0_dram"]
```

```python
from contextlib import ExitStack

import numpy as np

import concourse.bass as bass
from concourse import mybir

F32 = mybir.dt.float32
F32R = mybir.dt.float32r
I32 = mybir.dt.int32
ACT = mybir.ActivationFunctionType
ALU = mybir.AluOpType
AX = mybir.AxisListType

P = 128
WINDOW = 128
HEAD_DIM = 64
ROPE_THETA = 10000.0
LN_EPS = 1e-5
RMS_EPS = 1e-6
N_GROUPS = 4
SLOTS = 64
RING = 6
SIN_LIMIT = 3.1415925


class Signal:

    def __init__(self, sem, per):
        self.sem, self.per = sem, per

    def at(self, turn, n):
        return turn * self.per + n


class Steps:

    def __init__(self, eng, counted, turn):
        self.eng, self.counted, self.turn, self.n = eng, counted, turn, 0

    def do(self, ins):
        self.n += 1
        return ins.then_inc(self.counted.sem, 1)

    def sync(self):
        self.eng.wait_ge(self.counted.sem, self.counted.at(self.turn, self.n))

    def link(self, ins):
        self.do(ins)
        self.sync()

    def close(self):
        if self.counted.per != self.n:
            raise ValueError(f"{self.counted.sem.name} takes {self.n} steps a turn, not {self.counted.per}")


def bc(ap, axis, n):
    ap = ap.unsqueeze(axis)
    shape = list(ap.shape)
    shape[axis] = n
    return ap.to_broadcast(shape)


def trunk(nc, x_in, positions, w_in, attn_sinks, conv_w, a_log, dt_bias, dn_norm_w, w_out, ln1_g, ln1_b,
          router_w, router_bias, w_gate, w_up, w_down, ln2_g, ln2_b, out):
    depth, D, proj_dim = w_in.shape
    T = x_in.shape[1]
    NT = T // P
    KC = D // P
    n_q = attn_sinks.shape[1]
    q_dim = n_q * HEAD_DIM
    n_dn = a_log.shape[1]
    dk = dn_norm_w.shape[1]
    dn_dim = n_dn * dk
    kv_dim = (proj_dim - q_dim - 4 * dn_dim - 2 * n_dn) // 2
    n_kv = kv_dim // HEAD_DIM
    n_exp = router_w.shape[1]
    F = w_gate.shape[3]
    FC = F // P
    EPG = n_exp // N_GROUPS
    EXTRA = 2 * T // SLOTS
    TURNS = n_exp + EXTRA
    ALPHA = float((2 * depth) ** 0.25)
    HALF = n_dn // 2
    PANEL = 512
    PIECE = 4 * PANEL
    assert (T, NT, KC, HALF * P, FC) == (2 * P, 2, 16, PANEL, 4) and n_kv == 2 and dk == P

    off_kv = q_dim
    off_dn = q_dim + 2 * kv_dim
    off_z = off_dn + 3 * dn_dim
    off_ab = off_z + dn_dim
    IN_PANELS = [("q", 0), ("q", PANEL), ("kv", off_kv)]
    IN_PANELS += [("dn", off_dn + which * dn_dim + half * PANEL) for half in range(2) for which in range(3)]
    IN_PANELS += [("z", off_z), ("z", off_z + PANEL)]
    N_IN = len(IN_PANELS)
    N_OUT = D // PANEL
    MIX_PIECES = 4 * (N_IN + N_OUT)
    ORDER = [(i, j) for i in range(N_IN) for j in range(4)]
    ORDER += [(i, j) for i in (N_IN, N_IN + 1) for j in range(3)] + [(N_IN, 3), (N_IN + 1, 3)]
    ORDER += [(i, j) for i in (N_IN + 2, N_IN + 3) for j in range(4)]
    assert len(ORDER) == MIX_PIECES
    XT_BANKS = [[0, 2, 5, 6, 1, 3, 4, 7], [2, 3, 6, 7, 0, 1, 2, 3]]
    EXP_PIECES = 12
    assert MIX_PIECES % RING == 0 and EXP_PIECES == 2 * RING
    MIX_USES = MIX_PIECES // RING
    LEVELS = P.bit_length() - 1
    N_FLAGS = 3 * n_exp

    ctx = ExitStack()
    with ctx:
        def sb(name, shape, dt=F32):
            return ctx.enter_context(nc.sbuf_tensor(name, shape, dt))

        def signal(name, per):
            return Signal(ctx.enter_context(nc.semaphore(name)), per)

        ring = sb("ring", [P, RING, PIECE])
        x_nat = sb("x_nat", [P, NT, D])
        x_t = sb("x_t", [P, KC * T])
        xT = x_t[:, :].rearrange("p (c t) -> p c t", c=KC)
        mix_acc = sb("mix_acc", [P, KC * T])
        mixT = mix_acc[:, :].rearrange("p (c t) -> p c t", c=KC)
        acc = mix_acc[:, :].rearrange("p (t d) -> p t d", t=NT)

        region_a = sb("region_a", [P, 7168])
        region_a_at = nc.sbuf_base - 4 * 7168
        probs = region_a[:, 0:6144].rearrange("p (h k) -> p h k", h=n_q)

        def dn_mat(i):
            return region_a[:, i * 1024:(i + 1) * 1024].rearrange("p (t h c) -> p t h c", t=NT, h=HALF)

        decay, l_t, a_t, inv, inv_t, masked = (dn_mat(i) for i in range(6))
        gate_part = region_a[:, 0:512]
        up_part = region_a[:, 512:1024]
        act_t = region_a[:, 1024:1280]
        hid_t = region_a[:, 1280:1536].rearrange("p (f s) -> p f s", f=FC)
        pick = region_a[:, 1536:1792].rearrange("p (t s) -> p t s", t=NT)
        y_hi = nc.alloc_sbuf_tensor_at("y_hi", [P, D], F32R, offset=region_a_at + 4 * 1792)
        y_lo = nc.alloc_sbuf_tensor_at("y_lo", [P, D], F32R, offset=region_a_at + 4 * (1792 + D))
        scat_rows = nc.alloc_sbuf_tensor_at("scat_rows", [P, NT * P], F32R,
                                            offset=region_a_at + 4 * (1792 + 2 * D))
        scat = scat_rows[:, :].rearrange("p (t c) -> p t c", t=NT)
        assert 1792 + 2 * D + NT * P <= 7168
        region_b = sb("region_b", [P, 6144])
        qkv_t = region_b[:, :].rearrange("p (f w h t) -> p f w h t", f=2, w=3, h=HALF)
        region_cd = sb("region_cd", [P, 2 * NT * q_dim])
        region_c = region_cd[:, 0:NT * q_dim]
        q_rot = region_c[:, :].rearrange("p (t n) -> p t n", t=NT)
        z_act = q_rot
        region_d = region_cd[:, NT * q_dim:]
        q_t = region_d[:, :].rearrange("p (c t) -> p c t", t=T)
        o_nat = region_d[:, :].rearrange("p (t n) -> p t n", t=NT)
        ln_par = region_cd[:, 0:2 * D].rearrange("p (g d) -> p g d", g=2)

        slot_gate = sb("slot_gate", [P, 1])
        gate_col = sb("gate_col", [P, NT])
        k_rot = sb("k_rot", [P, NT, n_kv, 2, HEAD_DIM])
        v_nat = sb("v_nat", [P, NT, n_kv * HEAD_DIM])
        k_t = sb("k_t", [P, n_kv, T])
        v_rot = sb("v_rot", [P, 2 * PANEL])
        rot_a = v_rot[:, 0:PANEL]
        rot_b = v_rot[:, PANEL:2 * PANEL]
        conv_sq = sb("conv_sq", [P, 4 * PANEL])
        conv_y = conv_sq[:, 0:2 * PANEL].rearrange("p (a c) -> p a c", a=2)
        square = conv_sq[:, 2 * PANEL:].rearrange("p (a c) -> p a c", a=2)
        prob_t = sb("prob_t", [P, 4, 3 * P])
        xg_t = prob_t[:, :, :].rearrange("p a c -> p (a c)")[:, 0:KC * SLOTS].rearrange("p (c s) -> p c s", c=KC)
        v_beta = v_rot[:, :].rearrange("p (t h c) -> p t h c", t=NT, h=HALF)
        k_in = conv_y[:, 0, :].rearrange("p (h c) -> p h c", h=HALF)
        k_out = conv_y[:, 1, :].rearrange("p (h c) -> p h c", h=HALF)
        v_new = square[:, :, :].rearrange("p t (h c) -> p t h c", h=HALF)
        
        def w_t(h):
            return prob_t[:, h // 2, (h % 2) * P:(h % 2 + 1) * P]

        def state(h):
            return prob_t[:, 2 + h // 2, (h % 2) * P:(h % 2 + 1) * P]


        ident = sb("ident", [P, P])
        tri = sb("tri", [P, P])
        tri_strict = sb("tri_strict", [P, P])
        ones = sb("ones", [P, P])
        level_mask = sb("level_mask", [P, LEVELS, P])
        win_mask = sb("win_mask", [P, 3 * P])
        slot_id = sb("slot_id", [P, P])
        fold = sb("fold", [P, SLOTS])
        before = sb("before", [P, EPG, EPG])
        flag_exp = sb("flag_exp", [P, N_FLAGS])
        flag_off = sb("flag_off", [P, N_FLAGS])
        extra_id = sb("extra_id", [P, EXTRA])
        iota_i = sb("iota_i", [P, P], I32)
        inv_freq = sb("inv_freq", [P, HEAD_DIM // 2])
        cos_t = sb("cos_t", [P, NT, HEAD_DIM // 2])
        sin_t = sb("sin_t", [P, NT, HEAD_DIM // 2])
        ang = sb("ang", [P, 4, NT, HEAD_DIM // 2])
        pos_i = sb("pos_i", [P, NT], I32)
        pos_f = sb("pos_f", [P, NT])
        zero = sb("zero", [P, 1])
        eps_dn = sb("eps_dn", [P, 3])

        w_rout = sb("w_rout", [P, KC, n_exp])
        b_rout = sb("b_rout", [P, n_exp])
        w_ab = sb("w_ab", [P, KC, 2 * n_dn])
        sinks = sb("sinks", [P, n_q])
        a_log_b = sb("a_log_b", [P, n_dn])
        dt_b = sb("dt_b", [P, n_dn])
        dn_w = sb("dn_w", [P, P])
        taps_nat = sb("taps_nat", [4 * 3 * n_dn, P])
        taps = sb("taps", [P, 4 * 3 * n_dn])

        mx = sb("mx", [P, NT, n_q])
        sink_e = sb("sink_e", [P, NT, n_q])
        row_sum = sb("row_sum", [P, NT, n_q])
        gates = sb("gates", [P, 10, NT, n_dn])
        g_nat = sb("g_nat", [P, NT, n_dn])
        beta = sb("beta", [P, NT, n_dn])
        gc = sb("gc", [P, 3, n_dn])
        gfac = sb("gfac", [P, 4, n_dn])
        rms = sb("rms", [P, 4, HALF])
        stats = sb("stats", [P, NT, D // PANEL, 6])
        mean_var = sb("mean_var", [P, NT, 2])
        ln_s = sb("ln_s", [P, 3, NT])
        r = sb("r", [P, 10, NT, n_exp])
        cmp_a = sb("cmp_a", [P, NT * N_GROUPS, EPG, EPG])
        cmp_b = sb("cmp_b", [P, NT * N_GROUPS, EPG, EPG])
        gr = sb("gr", [P, 3, NT, N_GROUPS])
        cum = sb("cum", [P, 2, N_FLAGS])
        flags = sb("flags", [P, N_FLAGS])
        route_tmp = region_a[:, 0:2 * EXTRA * N_FLAGS + EXTRA * n_exp]
        hot = route_tmp[:, 0:EXTRA * N_FLAGS].rearrange("p (j i) -> p j i", j=EXTRA)
        hot_w = route_tmp[:, EXTRA * N_FLAGS:2 * EXTRA * N_FLAGS].rearrange("p (j i) -> p j i", j=EXTRA)
        hot_e = route_tmp[:, 2 * EXTRA * N_FLAGS:].rearrange("p (j e) -> p j e", j=EXTRA)
        ext = sb("ext", [P, 3, EXTRA])
        slot_of = sb("slot_of", [P, NT, TURNS])
        gate_of = sb("gate_of", [P, NT, TURNS])
        turns_f = sb("turns_f", [P, depth + 1])
        turns = sb("turns", [P, depth + 1], I32)
        turn_n = sb("turn_n", [P, 1], I32)
        extra_n = sb("extra_n", [P, depth], I32)
        extra_e = sb("extra_e", [P, EXTRA], I32)

        bank = [ctx.enter_context(nc.psum_tensor(f"bank{i}", [P, PANEL], F32)) for i in range(8)]

        consts = signal("consts", 0)
        pool_steps = signal("pool_steps", 0)
        once_loaded = signal("once_loaded", 0)
        pos_loaded = signal("pos_loaded", 0)
        rope_act = signal("rope_act", 0)
        rope_dve = signal("rope_dve", 0)
        dve_setup = signal("dve_setup", 0)
        ring_free = signal("ring_free", 0)
        landed = [signal(f"landed{i}", 0) for i in range(2 * RING)]
        layer_open = signal("layer_open", 4)
        small_loaded = signal("small_loaded", 96)
        taps_done = signal("taps_done", 1)
        ln1_loaded = signal("ln1_loaded", 32)
        ln2_loaded = signal("ln2_loaded", 32)
        xt_done = signal("xt_done", 16)
        xt_act = signal("xt_act", 10)
        xt_dve = signal("xt_dve", 6)
        proj_done = signal("proj_done", 2 * (N_IN + N_OUT))
        proj_read = signal("proj_read", N_IN + N_OUT - 2)
        z_read = signal("z_read", 2)
        ab_done = signal("ab_done", 1)
        ab_act = signal("ab_act", 3)
        ab_dve = signal("ab_dve", 2)
        g_ready = signal("g_ready", 1)
        roped = signal("roped", 3)
        tq_done = signal("tq_done", 5)
        tq_read = signal("tq_read", 5)
        score_done = signal("score_done", n_q)
        score_read = signal("score_read", n_q)
        max_ready = signal("max_ready", 1)
        exp_done = signal("exp_done", 1)
        probs_ready = signal("probs_ready", 1)
        pt_done = signal("pt_done", n_q)
        pt_read = signal("pt_read", n_q)
        pv_done = signal("pv_done", n_q)
        pv_read = signal("pv_read", n_q // 2)
        conv_ready = signal("conv_ready", 12)
        silu_done = signal("silu_done", 12)
        square_ready = signal("square_ready", 8)
        ss_done = signal("ss_done", 8)
        norm_sqrt = signal("norm_sqrt", 8)
        normed = signal("normed", 8)
        gc_done = signal("gc_done", 1)
        gc_dve = signal("gc_dve", 1)
        gc_act = signal("gc_act", 1)
        factors_ready = signal("factors_ready", 1)
        spread_ready = signal("spread_ready", 4)
        spread_done = signal("spread_done", 4)
        decay_arg = signal("decay_arg", 4)
        decay_exp = signal("decay_exp", 4)
        pair_done = signal("pair_done", 4)
        pair_read = signal("pair_read", 4)
        kv_done = signal("kv_done", 4)
        kv_read = signal("kv_read", 4)
        inv_open = signal("inv_open", 2)
        lt_done = signal("lt_done", 4 * LEVELS)
        masked_ready = signal("masked_ready", 4 * LEVELS)
        tlt_done = signal("tlt_done", 4 * LEVELS)
        inv_ready = signal("inv_ready", 4 * LEVELS)
        u0_done = signal("u0_done", 2)
        v0_ready = signal("v0_ready", 2)
        s_done = signal("s_done", 2)
        s_ready = signal("s_ready", 2)
        v1_done = signal("v1_done", 2)
        v1_ready = signal("v1_ready", 2)
        o1_done = signal("o1_done", 2)
        o_ready = signal("o_ready", 2)
        rms_arg = signal("rms_arg", 4)
        rms_sqrt = signal("rms_sqrt", 4)
        dn_out = signal("dn_out", 4)
        to_done = signal("to_done", 4)
        to_read = signal("to_read", 4)
        var_ready = signal("var_ready", 4)
        ln_sqrt = signal("ln_sqrt", 4)
        acc_ready = signal("acc_ready", 1)
        ln_done = signal("ln_done", 4)
        logit_done = signal("logit_done", 1)
        logit_exp = signal("logit_exp", 1)
        member_ready = signal("member_ready", 1)
        rank_done = signal("rank_done", 1)
        route_ready = signal("route_ready", 1)
        route_seen = signal("route_seen", 1)
        open_seen = signal("open_seen", 2)
        moe_open = signal("moe_open", 1)
        act_steps = signal("act_steps", 5)
        dve_steps = signal("dve_steps", 345)
        gather_done = signal("gather_done", 2)
        gather_read = signal("gather_read", 2)
        pick_ready = signal("pick_ready", 1)
        gateup_done = signal("gateup_done", 2)
        gate_read = signal("gate_read", 1)
        up_read = signal("up_read", 1)
        scat_put = signal("scat_put", 8)
        scat_added = signal("scat_added", 8)
        scat_ready = signal("scat_ready", 1)
        fold_done = signal("fold_done", 1)
        silu_ready = signal("silu_ready", 1)
        hid_ready = signal("hid_ready", 1)
        down_done = signal("down_done", 4)
        hi_ready = signal("hi_ready", 4)
        y_ready = signal("y_ready", 4)
        stored = signal("stored", 0)

        w_in_v = w_in.rearrange("l (k p) n -> l p k n", p=P)
        w_out_v = w_out.rearrange("l (k p) n -> l p k n", p=P)
        w_gate_v = w_gate.rearrange("l e (k p) f -> (l e) p k f", p=P)
        w_up_v = w_up.rearrange("l e (k p) f -> (l e) p k f", p=P)
        w_down_v = w_down.rearrange("l e (f p) d -> (l e) p f d", p=P)

        def piece(n):
            return ring[:, n % RING, :].rearrange("p (k n) -> p k n", k=4)

        exp_slot = [ring[:, n, :] for n in range(RING)]
        exp_slot += [region_b[:, n * PIECE:(n + 1) * PIECE] for n in range(3)]
        exp_slot += [conv_sq[:, :], x_t[:, 0:PIECE], x_t[:, PIECE:2 * PIECE]]

        block = ctx.enter_context(nc.Block())

        @block.gpsimd
        def _(pool):
            s = Steps(pool, pool_steps, 0)

            def select(ap, op, fill, base, pattern):
                s.link(pool.affine_select(out=ap, in_=ap, compare_op=op, fill=fill, base=base,
                                          pattern=pattern, channel_multiplier=1))

            s.do(pool.memset(ident[:, :], 0.0))
            s.do(pool.memset(turns[:, :], 0))
            for i in range(HEAD_DIM // 2):
                f = np.float32(1.0) / np.power(np.float32(ROPE_THETA), np.float32(2 * i / HEAD_DIM))
                s.do(pool.memset(inv_freq[:, i:i + 1], float(f)))
            s.sync()
            select(ident[:, :], ALU.not_equal, 1.0, 0, [[-1, P]])
            pool.sem_inc(consts.sem, 1)
            s.do(pool.memset(ones[:, :], 1.0))
            s.do(pool.memset(tri[:, :], 0.0))
            s.do(pool.memset(tri_strict[:, :], 0.0))
            s.do(pool.memset(level_mask[:, :, :], 0.0))
            s.do(pool.memset(win_mask[:, :], -1e30))
            s.do(pool.memset(fold[:, :], 0.0))
            s.do(pool.memset(before[:, :, :], 0.0))
            s.do(pool.memset(flag_off[:, :], 0.0))
            s.do(pool.memset(turns_f[:, :], 0.0))
            s.do(pool.memset(zero[:, :], 0.0))
            s.do(pool.memset(eps_dn[:, 0:1], float(dk * RMS_EPS)))
            s.do(pool.memset(eps_dn[:, 1:2], RMS_EPS))
            s.do(pool.memset(eps_dn[:, 2:3], LN_EPS))
            s.sync()
            select(tri[:, :], ALU.is_gt, 1.0, 0, [[-1, P]])
            select(tri_strict[:, :], ALU.is_ge, 1.0, 0, [[-1, P]])
            select(fold[:, :], ALU.not_equal, 1.0, 0, [[-1, SLOTS]])
            select(fold[:, :], ALU.not_equal, 1.0, -SLOTS, [[-1, SLOTS]])
            for j in (0, 2):
                own = win_mask[:, j * P:(j + 1) * P]
                s.link(pool.affine_select(out=own, in_=own, compare_op=ALU.is_gt, fill=0.0, base=0,
                                          pattern=[[1, P]], channel_multiplier=-1))
            select(win_mask[:, P:2 * P], ALU.is_ge, 0.0, 0, [[-1, P]])
            for lev in range(LEVELS):
                b = 1 << lev
                m = level_mask[:, lev, :].rearrange("p (n j i) -> p n j i", j=2, i=b)[:, :, 0, :]
                nb = P // (2 * b)
                s.link(pool.memset(m, -1.0))
                s.link(pool.affine_select(out=m, in_=m, compare_op=ALU.is_ge, fill=0.0, base=-b,
                                          pattern=[[-2 * b, nb], [0, b]], channel_multiplier=1))
                s.link(pool.affine_select(out=m, in_=m, compare_op=ALU.is_ge, fill=0.0, base=2 * b - 1,
                                          pattern=[[2 * b, nb], [0, b]], channel_multiplier=-1))
            s.link(pool.affine_select(out=before[:, :, :], in_=before[:, :, :], compare_op=ALU.is_ge, fill=1.0,
                                      base=0, pattern=[[-1, EPG], [1, EPG]], channel_multiplier=0))
            for tau in range(3):
                s.do(pool.memset(flag_off[:, tau * n_exp:(tau + 1) * n_exp], float(SLOTS * (tau + 1))))
            s.link(pool.iota(iota_i[:, 0:N_FLAGS], pattern=[[0, 3], [1, n_exp]], base=0, channel_multiplier=0))
            s.link(pool.tensor_copy(flag_exp[:, :], iota_i[:, 0:N_FLAGS]))
            s.link(pool.iota(iota_i[:, 0:EXTRA], pattern=[[1, EXTRA]], base=1, channel_multiplier=0))
            s.link(pool.tensor_copy(extra_id[:, :], iota_i[:, 0:EXTRA]))
            s.link(pool.iota(iota_i[:, :], pattern=[[0, 2], [1, SLOTS]], base=0, channel_multiplier=0))
            pool.tensor_copy(slot_id[:, :], iota_i[:, :]).then_inc(consts.sem, 1)

        @block.sync
        def _(sp):
            with nc.allow_non_contiguous_dma(reason="256 positions, one for each token's partition"):
                sp.dma_start(pos_i[:, :], positions.rearrange("b (t p) -> p (b t)", p=P)).then_inc(pos_loaded.sem, 16)
            for t in range(NT):
                sp.dma_start(x_nat[:, t, :], x_in[0, t * P:(t + 1) * P, :]).then_inc(once_loaded.sem, 16)
            sp.dma_start(w_rout[:, :, :], router_w.rearrange("(k p) e -> p k e", p=P)).then_inc(once_loaded.sem, 16)
            sp.dma_start(b_rout[:, :], router_bias.partition_broadcast(P)).then_inc(once_loaded.sem, 16)
            sp.wait_ge(consts.sem, 1)

            def load(n, first, src):
                sp.wait_ge(ring_free.sem, first + (n + 1 if n < RING else n + 1 + RING))
                dst = piece(n)
                if src.shape[-1] != PANEL:
                    dst = dst[:, :, 0:src.shape[-1]]
                sp.dma_start(dst, src).then_inc(landed[n % RING].sem, 16)

            def expert(first, le, l=None):
                for j in range(EXP_PIECES):
                    if l is None or j >= RING:
                        sp.wait_ge(ring_free.sem, first + (j + 1))
                    else:
                        sp.wait_ge(ring_free.sem, first + (j + 1 + RING))
                    if l is not None and j == RING:
                        sp.wait_ge(o_ready.sem, o_ready.at(l, 2))
                    if l is not None and j == EXP_PIECES - 2:
                        sp.sem_inc(open_seen.sem, 1)
                        sp.wait_ge(logit_done.sem, logit_done.at(l, 1))
                    dst = exp_slot[j]
                    if j < 8:
                        w = (w_gate_v, w_up_v)[j // 4]
                        dst = dst.rearrange("p (k n) -> p k n", k=4)
                        src = w[bass.ds(le, 1), :, 4 * (j % 4):4 * (j % 4) + 4, :].rearrange("a p k f -> (a p) k f")
                    else:
                        src = w_down_v[bass.ds(le, 1), :, j - 8, :].rearrange("a p d -> (a p) d")
                    sp.dma_start(dst, src).then_inc(landed[j].sem, 16)

            with sp.Fori(0, depth) as l:
                turns0 = sp.value_load(turns[0:1, bass.ds(l, 1)], min_val=0, max_val=depth * TURNS)
                first = sp.snap(l * MIX_PIECES + turns0 * EXP_PIECES)

                def row(a):
                    return a[bass.ds(l, 1)].rearrange("a n -> (a n)").partition_broadcast(P)

                for n, (i, j) in enumerate(ORDER):
                    if i < N_IN:
                        kind, c0 = IN_PANELS[i]
                        width = 2 * kv_dim if kind == "kv" else PANEL
                        load(n, first, w_in_v[bass.ds(l, 1), :, 4 * j:4 * j + 4, c0:c0 + width]
                             .rearrange("a p k n -> (a p) k n"))
                    else:
                        c0 = (i - N_IN) * PANEL
                        load(n, first, w_out_v[bass.ds(l, 1), :, 4 * j:4 * j + 4, c0:c0 + PANEL]
                             .rearrange("a p k n -> (a p) k n"))
                    if (i, j) == (0, 3):
                        sp.wait_ge(layer_open.sem, layer_open.at(l, 4))
                        sp.sem_inc(open_seen.sem, 1)
                        sp.dma_start(w_ab[:, :, :], w_in_v[bass.ds(l, 1), :, :, off_ab:off_ab + 2 * n_dn]
                                     .rearrange("a p k n -> (a p) k n")).then_inc(small_loaded.sem, 16)
                        sp.dma_start(taps_nat[:, :], conv_w[bass.ds(l, 1)].rearrange("a w (c p) -> (a w c) p", p=P))\
                            .then_inc(small_loaded.sem, 16)
                        for dst, src in ((sinks, attn_sinks), (a_log_b, a_log), (dt_b, dt_bias), (dn_w, dn_norm_w)):
                            sp.dma_start(dst[:, :], row(src)).then_inc(small_loaded.sem, 16)
                    if (i, j) == (N_IN + 2, 0):
                        sp.wait_ge(to_done.sem, to_done.at(l, 4))
                        sp.dma_start(ln_par[:, 0, :], row(ln1_g)).then_inc(ln1_loaded.sem, 16)
                        sp.dma_start(ln_par[:, 1, :], row(ln1_b)).then_inc(ln1_loaded.sem, 16)
                first_e = sp.snap(l * MIX_PIECES + turns0 * EXP_PIECES + MIX_PIECES)
                expert(first_e, l * n_exp, l)
                sp.wait_ge(ln_done.sem, ln_done.at(l, 4))
                sp.dma_start(ln_par[:, 0, :], row(ln2_g)).then_inc(ln2_loaded.sem, 16)
                sp.dma_start(ln_par[:, 1, :], row(ln2_b)).then_inc(ln2_loaded.sem, 16)
                with sp.Fori(1, n_exp) as e:
                    expert(first_e + e * EXP_PIECES, l * n_exp + e)
                sp.wait_ge(route_ready.sem, l + 1)
                sp.sem_inc(route_seen.sem, 1)
                more = sp.value_load(extra_n[0:1, bass.ds(l, 1)], min_val=0, max_val=EXTRA)
                with sp.If(more > 0):
                    with sp.Fori(0, more) as j:
                        e = sp.value_load(extra_e[0:1, bass.ds(j, 1)], min_val=0, max_val=n_exp - 1)
                        expert(first_e + (n_exp + j) * EXP_PIECES, l * n_exp + e)

            for t in range(NT):
                sp.wait_ge(layer_open.sem, layer_open.at(depth, 2 * t + 2))
                sp.dma_start(out[0, t * P:(t + 1) * P, :], x_nat[:, t, :]).then_inc(stored.sem, 16)
            sp.wait_ge(stored.sem, 16 * NT)

        @block.tensor
        def _(pe):
            pe.wait_ge(consts.sem, 1)

            def transposes(g, src, dst):
                for j in range(4):
                    last = pe.transpose(dst[:, j * P:(j + 1) * P], src(j), ident[:, :])
                return last

            def turn_x(g, rnd, dst):
                t, c = g // 4, 4 * (g % 4)
                transposes(g, lambda j: x_nat[:, t, (c + j) * P:(c + j + 1) * P], dst).then_inc(xt_done.sem, 1)

            with pe.Fori(0, depth) as l:
                pe.wait_ge(layer_open.sem, layer_open.at(l, 1))
                turns0 = pe.value_load(turns[0:1, bass.ds(l, 1)], min_val=0, max_val=depth * TURNS)
                uses = pe.snap(l * MIX_USES + turns0)

                def arrived(n, before_):
                    pe.wait_ge(landed[n % RING].sem, (before_ + (n // RING + 1)) * 16)

                for g in range(8):
                    pe.wait_ge(layer_open.sem, layer_open.at(l, g // 2 + 1))
                    turn_x(g, 0, bank[XT_BANKS[0][g]])
                pe.wait_ge(xt_act.sem, xt_act.at(l, 4))
                pe.wait_ge(xt_dve.sem, xt_dve.at(l, 4))

                owed = [2]

                def k_step(i, k):
                    kind = IN_PANELS[i][0] if i < N_IN else "out"
                    j, kk = k // 4, k % 4
                    n = ORDER.index((i, j))
                    if k == 0:
                        if 2 <= i <= 10:
                            pe.wait_ge(proj_read.sem, proj_read.at(l, i - 1))
                        if i in (11, 12):
                            pe.wait_ge(z_read.sem, z_read.at(l, i - 10))
                        if i > 12:
                            pe.wait_ge(proj_read.sem, proj_read.at(l, i - 3))
                    if i in (11, 12) and k in (8, 12):
                        pe.wait_ge(to_read.sem, to_read.at(l, k // 2 - 2))
                    if kk == 0:
                        arrived(n, uses)
                    b = [bank[2 * (i % 2)], bank[2 * (i % 2) + 1]]
                    width = 2 * kv_dim if kind == "kv" else PANEL
                    w = piece(n)

                    def settle(m):
                        if kk == 0 and owed[0]:
                            m.then_inc(ring_free.sem, owed[0])
                            owed[0] = 0

                    if kind == "dn":
                        for c in range(4):
                            m = pe.matmul(b[c // 2][:, (c % 2) * T:(c % 2 + 1) * T],
                                          w[:, kk, c * P:(c + 1) * P], xT[:, k, :],
                                          start=(k == 0 and c % 2 == 0), stop=(k == KC - 1),
                                          skip_group_check=True)
                            if c == 0:
                                settle(m)
                            if k == KC - 1 and c == 1:
                                m.then_inc(proj_done.sem, 1)
                    else:
                        lhs = mixT if kind == "out" else xT
                        for t in range(NT):
                            m = pe.matmul(b[t][:, 0:width], lhs[:, k, t * P:(t + 1) * P],
                                          w[:, kk, 0:width], start=(k == 0), stop=(k == KC - 1))
                            if t == 0:
                                settle(m)
                            if k == KC - 1 and t == 0:
                                m.then_inc(proj_done.sem, 1)
                    if k == KC - 1:
                        m.then_inc(proj_done.sem, 1)
                        owed[0] += 1
                    elif kk == 3:
                        m.then_inc(ring_free.sem, 1)

                def last_panel():
                    i = N_IN + N_OUT - 1
                    pe.wait_ge(proj_read.sem, proj_read.at(l, i - 3))
                    for t in range(NT):
                        for k in range(KC):
                            j, kk = k // 4, k % 4
                            n = ORDER.index((i, j))
                            if t == kk == 0:
                                arrived(n, uses)
                            m = pe.matmul(bank[2 * (i % 2) + t][:, :], mixT[:, k, t * P:(t + 1) * P],
                                          piece(n)[:, kk, :], start=(k == 0), stop=(k == KC - 1))
                            if t == k == 0:
                                m.then_inc(ring_free.sem, owed[0])
                            if t == 1 and kk == 3 and j < 2:
                                m.then_inc(ring_free.sem, 1)
                        m.then_inc(proj_done.sem, 1)

                def panel(i, first=0, end=KC):
                    for k in range(first, end):
                        k_step(i, k)

                panel(0)
                pe.wait_ge(consts.sem, 2)
                panel(1)
                panel(2)
                pe.wait_ge(small_loaded.sem, small_loaded.at(l, 96))
                for t in range(NT):
                    for k in range(KC):
                        m = pe.matmul(bank[4][:, t * 2 * n_dn:(t + 1) * 2 * n_dn], xT[:, k, t * P:(t + 1) * P],
                                      w_ab[:, k, :], start=(k == 0), stop=(k == KC - 1))
                m = pe.transpose(bank[4][:, 64:64 + taps_nat.shape[0]], taps_nat[:, :],
                                 ident[0:taps_nat.shape[0], 0:taps_nat.shape[0]])
                m.then_inc(ab_done.sem, 1)

                for g in range(4):
                    t, c = g // 2, 4 * (g % 2)
                    pe.wait_ge(roped.sem, roped.at(l, 2))
                    if g == 3:
                        pe.wait_ge(tq_read.sem, tq_read.at(l, 1))
                    transposes(g, lambda j: q_rot[:, t, (c + j) * P:(c + j + 1) * P], bank[5 + g % 3])\
                        .then_inc(tq_done.sem, 1)
                pe.wait_ge(roped.sem, roped.at(l, 3))
                pe.wait_ge(tq_read.sem, tq_read.at(l, 2))
                transposes(4, lambda j: k_rot[:, j % 2, j // 2, :, :].rearrange("p a d -> p (a d)"), bank[6])\
                    .then_inc(tq_done.sem, 1)

                panel(3)
                pe.wait_ge(tq_read.sem, tq_read.at(l, 5))
                pe.wait_ge(ab_dve.sem, ab_dve.at(l, 2))
                for h in range(n_q):
                    lo = (h % 2) * HEAD_DIM
                    kv = h // (n_q // n_kv)
                    rows = slice(lo, lo + HEAD_DIM)
                    if h >= 4:
                        pe.wait_ge(score_read.sem, score_read.at(l, h - 3))
                    b = bank[4 + h % 4]
                    pe.matmul(b[:, 0:P], q_t[rows, h // 2, 0:P], k_t[rows, kv, 0:P], start=True, stop=True)
                    pe.matmul(b[:, P:3 * P], q_t[rows, h // 2, P:T], k_t[rows, kv, :], start=True, stop=True)\
                        .then_inc(score_done.sem, 1)
                    k_step(4, h)
                panel(5)

                def square_sums(half, i, k):
                    for u in range(4):
                        n = 4 * half + u
                        if u:
                            k_step(i, k + u - 1)
                        pe.wait_ge(square_ready.sem, square_ready.at(l, n + 1))
                        if u >= 2:
                            pe.wait_ge(norm_sqrt.sem, norm_sqrt.at(l, n - 1))
                        pe.matmul(bank[4 + u % 2][:, :], ones[:, :], square[:, n % 2, :], start=True, stop=True)\
                            .then_inc(ss_done.sem, 1)

                pe.wait_ge(score_read.sem, score_read.at(l, n_q))
                panel(6, 0, 4)
                pe.wait_ge(probs_ready.sem, probs_ready.at(l, 1))
                for h in range(n_q + 2):
                    if h < n_q:
                        if h >= 2:
                            pe.wait_ge(pt_read.sem, pt_read.at(l, h - 1))
                        for j in range(3):
                            m = pe.transpose(bank[4 + h % 2][:, j * P:(j + 1) * P],
                                             probs[:, h, j * P:(j + 1) * P], ident[:, :])
                        m.then_inc(pt_done.sem, 1)
                    if h >= 2:
                        hh = h - 2
                        lo = (hh % 2) * HEAD_DIM
                        kv = hh // (n_q // n_kv)
                        vs = slice(kv * HEAD_DIM, (kv + 1) * HEAD_DIM)
                        pe.wait_ge(pt_read.sem, pt_read.at(l, hh + 1))
                        if hh >= 4 and hh % 2 == 0:
                            pe.wait_ge(pv_read.sem, pv_read.at(l, hh // 2 - 1))
                        o = bank[6 + hh // 2 % 2][lo:lo + HEAD_DIM, 0:T]
                        pt = prob_t[:, hh % 4, :]
                        pe.matmul(o[:, 0:P], v_nat[:, 0, vs], pt[:, 0:P], start=True, stop=True)
                        pe.matmul(o[:, P:T], v_nat[:, 0, vs], pt[:, P:2 * P], start=True, stop=False)
                        pe.matmul(o[:, P:T], v_nat[:, 1, vs], pt[:, 2 * P:3 * P], start=False, stop=True)\
                            .then_inc(pv_done.sem, 1)
                    if 4 + h < KC:
                        k_step(6, 4 + h)
                pe.wait_ge(pt_read.sem, pt_read.at(l, n_q))
                panel(7, 0, 2)
                square_sums(0, 7, 2)
                panel(7, 5)
                pe.wait_ge(g_ready.sem, g_ready.at(l, 1))
                pe.wait_ge(norm_sqrt.sem, norm_sqrt.at(l, 4))
                pe.wait_ge(pv_read.sem, pv_read.at(l, n_q // 2))
                for t in range(NT):
                    pe.matmul(bank[4][:, t * n_dn:(t + 1) * n_dn], tri[:, :], g_nat[:, t, :], start=True, stop=True)
                pe.matmul(bank[4][:, 2 * n_dn:3 * n_dn], ones[:, :], g_nat[:, 0, :], start=True, stop=True)\
                    .then_inc(gc_done.sem, 1)
                panel(8)
                pe.wait_ge(gc_dve.sem, gc_dve.at(l, 1))
                panel(9, 0, 6)
                square_sums(1, 9, 6)
                panel(9, 9)

                between = [[(10, k) for k in range(KC)] + [(11, k) for k in range(8)],
                           [(11, k) for k in range(8, 12)] + [(12, k) for k in range(12)]]
                left = []

                def meanwhile(n):
                    for _ in range(min(n, len(left))):
                        k_step(*left.pop(0))

                def turn_out(half):
                    for t in range(NT):
                        n = 2 * half + t
                        pe.wait_ge(dn_out.sem, dn_out.at(l, n + 1))
                        transposes(0, lambda j: o_nat[:, t, (half * HALF + j) * P:(half * HALF + j + 1) * P],
                                   bank[4 + t]).then_inc(to_done.sem, 1)

                for half in range(2):
                    q_h, k_h, v_h = (qkv_t[:, half, w] for w in range(3))
                    pe.wait_ge(normed.sem, normed.at(l, 4 * half + 4))
                    pe.wait_ge(silu_done.sem, silu_done.at(l, 6 * half + 6))
                    left += between[half]
                    for t in range(NT):
                        n = 2 * half + t
                        tok = slice(t * P, (t + 1) * P)
                        pe.wait_ge(spread_ready.sem, spread_ready.at(l, n + 1))
                        if t == 1 or half == 1:
                            pe.wait_ge(kv_read.sem, kv_read.at(l, n))
                        if t == 0 and half == 1:
                            pe.wait_ge(o_ready.sem, o_ready.at(l, 1))
                            pe.wait_ge(to_read.sem, to_read.at(l, 2))
                        pe.matmul(bank[4][:, :], ones[:, :], decay[:, t].rearrange("p h c -> p (h c)"),
                                  start=True, stop=True)
                        pe.matmul(bank[5][:, :], ones[:, :], l_t[:, t].rearrange("p h c -> p (h c)"),
                                  start=True, stop=True).then_inc(spread_done.sem, 1)
                        for h in range(HALF):
                            pe.matmul(bank[6][:, h * P:(h + 1) * P], k_h[:, h, tok], k_h[:, h, tok],
                                      start=True, stop=True)
                        for h in range(HALF):
                            m = pe.matmul(bank[7][:, h * P:(h + 1) * P], k_h[:, h, tok], q_h[:, h, tok],
                                          start=True, stop=True)
                        m.then_inc(pair_done.sem, 1)
                        meanwhile(2)
                        pe.wait_ge(pair_read.sem, pair_read.at(l, n + 1))
                        transposes(0, lambda j: k_h[:, j, tok], bank[6])
                        transposes(0, lambda j: v_h[:, j, tok], bank[7]).then_inc(kv_done.sem, 1)
                        meanwhile(1)
                    pe.wait_ge(kv_read.sem, kv_read.at(l, 2 * half + 2))
                    pe.wait_ge(inv_open.sem, inv_open.at(l, half + 1))
                    for lev in range(LEVELS):
                        for t in range(NT):
                            n = (half * LEVELS + lev) * NT + t
                            if lev:
                                pe.wait_ge(inv_ready.sem, inv_ready.at(l, n - 1))
                            for h in range(HALF):
                                m = pe.matmul(bank[4 + 2 * t][:, h * P:(h + 1) * P], l_t[:, t, h], inv[:, t, h],
                                              start=True, stop=True)
                            m.then_inc(lt_done.sem, 1)
                        meanwhile(1)
                        for t in range(NT):
                            n = (half * LEVELS + lev) * NT + t
                            pe.wait_ge(masked_ready.sem, masked_ready.at(l, n + 1))
                            for h in range(HALF):
                                pe.matmul(bank[5 + 2 * t][:, h * P:(h + 1) * P], inv_t[:, t, h], masked[:, t, h],
                                          start=True, stop=True)
                            for h in range(HALF):
                                m = pe.matmul(bank[4 + 2 * t][:, h * P:(h + 1) * P], masked[:, t, h],
                                              inv_t[:, t, h], start=True, stop=True)
                            m.then_inc(tlt_done.sem, 1)
                        meanwhile(1)
                    assert not left or left[0][0] > 10
                    pe.wait_ge(inv_ready.sem, inv_ready.at(l, (half + 1) * LEVELS * NT))
                    for h in range(HALF):
                        pe.matmul(bank[4][:, h * P:(h + 1) * P], inv_t[:, 0, h], v_beta[:, 0, h], start=True, stop=True)
                    for h in range(HALF):
                        m = pe.matmul(bank[7][:, h * P:(h + 1) * P], k_in[:, h], inv_t[:, 1, h], start=True, stop=True)
                    m.then_inc(u0_done.sem, 1)
                    meanwhile(1)
                    pe.wait_ge(v0_ready.sem, v0_ready.at(l, half + 1))
                    for h in range(HALF):
                        pe.matmul(bank[6][:, h * P:(h + 1) * P], k_out[:, h], v_new[:, 0, h], start=True, stop=True)
                    for h in range(HALF):
                        m = pe.matmul(bank[5][:, h * P:(h + 1) * P], a_t[:, 0, h], v_new[:, 0, h], start=True, stop=True)
                    m.then_inc(s_done.sem, 1)
                    meanwhile(1)
                    pe.wait_ge(s_ready.sem, s_ready.at(l, half + 1))
                    for h in range(HALF):
                        pe.matmul(bank[4][:, h * P:(h + 1) * P], inv_t[:, 1, h], v_beta[:, 1, h], start=True, stop=False)
                        m = pe.matmul(bank[4][:, h * P:(h + 1) * P], w_t(h), state(h), start=False, stop=True)
                    m.then_inc(v1_done.sem, 1)
                    for h in range(HALF):
                        pe.matmul(bank[6][:, h * P:(h + 1) * P], q_h[:, h, P:T], state(h), start=True, stop=True)
                    meanwhile(1)
                    pe.wait_ge(v1_ready.sem, v1_ready.at(l, half + 1))
                    for h in range(HALF):
                        m = pe.matmul(bank[7][:, h * P:(h + 1) * P], a_t[:, 1, h], v_new[:, 1, h], start=True, stop=True)
                    m.then_inc(o1_done.sem, 1)

                    meanwhile(KC)
                    if half == 1:
                        pe.wait_ge(o_ready.sem, o_ready.at(l, 2))
                    turn_out(half)
                panel(11, 12)
                panel(12, 12)
                panel(13)
                last_panel()

                for t in range(NT):
                    for g in range(4 * t, 4 * t + 4):
                        pe.wait_ge(ln_done.sem, ln_done.at(l, g // 2 + 1))
                        if g >= 6:
                            pe.wait_ge(xt_act.sem, xt_act.at(l, 4 + g - 5))
                        turn_x(g, 1, bank[XT_BANKS[1][g]])
                    pe.wait_ge(xt_act.sem, xt_act.at(l, 8 + 2 * t))
                    if t:
                        pe.wait_ge(xt_dve.sem, xt_dve.at(l, 6))
                    for k in range(KC):
                        m = pe.matmul(bank[4][:, t * n_exp:(t + 1) * n_exp], xT[:, k, t * P:(t + 1) * P],
                                      w_rout[:, k, :], start=(k == 0), stop=(k == KC - 1))
                m.then_inc(logit_done.sem, 1)
                pe.wait_ge(member_ready.sem, member_ready.at(l, 1))
                member = r[:, 4]
                pe.matmul(bank[5][:, 0:n_exp], tri_strict[:, :], member[:, 0, :], start=True, stop=True)
                pe.matmul(bank[5][:, n_exp:2 * n_exp], tri_strict[:, :], member[:, 1, :], start=True, stop=False)
                pe.matmul(bank[5][:, n_exp:2 * n_exp], ones[:, :], member[:, 0, :], start=False, stop=True)
                pe.matmul(bank[5][:, 2 * n_exp:3 * n_exp], ones[:, :], member[:, 0, :], start=True, stop=False)
                pe.matmul(bank[5][:, 2 * n_exp:3 * n_exp], ones[:, :], member[:, 1, :], start=False, stop=True)\
                    .then_inc(rank_done.sem, 1)

                def gather(added=None):
                    for c in range(KC):
                        if c == 8 and added is not None:
                            pe.wait_ge(scat_added.sem, added)
                        o = bank[c // 8][:, (c % 8) * SLOTS:(c % 8 + 1) * SLOTS]
                        for t in range(NT):
                            m = pe.matmul(o, x_nat[:, t, c * P:(c + 1) * P], pick[:, t, 0:SLOTS],
                                          start=(t == 0), stop=(t == NT - 1))
                        if c % 8 == 7:
                            m.then_inc(gather_done.sem, 1)

                SCAT_BANKS = [1, 4, 5, 6, 7, 3, 1, 4]

                def scatter(i, last=False):
                    for n in range(8):
                        t, c = n // 4, n % 4
                        if n == 5 and not last:
                            pe.wait_ge(up_read.sem, i + 1)
                        if n >= 6:
                            pe.wait_ge(scat_added.sem, scat_added.at(i + l, n - 5))
                        pe.matmul(bank[SCAT_BANKS[n]][:, :], scat[:, t, :], y_hi[:, c * PANEL:(c + 1) * PANEL],
                                  start=True, stop=False)
                        pe.matmul(bank[SCAT_BANKS[n]][:, :], scat[:, t, :], y_lo[:, c * PANEL:(c + 1) * PANEL],
                                  start=False, stop=True).then_inc(scat_put.sem, 1)

                pe.wait_ge(pick_ready.sem, turns0 + (l + 1))
                gather()
                pe.wait_ge(moe_open.sem, l + 1)
                turns1 = pe.value_load(turns[0:1, bass.ds(l + 1, 1)], min_val=1, max_val=depth * TURNS)
                with pe.Fori(turns0, turns1) as i:
                    uses_e = pe.snap((l + 1) * MIX_USES + i)

                    def here(j):
                        pe.wait_ge(landed[j].sem, ((uses_e if j < RING else i) + 1) * 16)

                    pe.wait_ge(gather_read.sem, (i + l) * 2 + 2)
                    for t in range(NT):
                        pe.transpose(bank[0][:, t * P:(t + 1) * P], pick[:, t, :], ident[:, :])
                    for t in range(NT):
                        pe.matmul(bank[0][:, NT * P:NT * P + 1], pick[:, t, :], gate_col[:, t:t + 1],
                                  start=(t == 0), stop=(t == NT - 1))
                    for w in range(2):
                        for j in range(4):
                            n = 4 * w + j
                            here(n)
                            for kk in range(4):
                                k = 4 * j + kk
                                side = k % 2
                                m = pe.matmul(bank[2 + w][side * SLOTS:(side + 1) * SLOTS, :], xg_t[:, k, :],
                                              exp_slot[n][:, kk * PANEL:(kk + 1) * PANEL], start=(k < 2), stop=(k >= KC - 2))
                                if k == 0:
                                    m.then_inc(ring_free.sem, 2 - w)
                            m.then_inc(*((ring_free.sem, 1) if j < 3 else (gateup_done.sem, 1)))
                    pe.wait_ge(scat_ready.sem, i + (l + 1))
                    pe.wait_ge(y_ready.sem, (i + (l + 1)) * 4)
                    scatter(i)
                    pe.wait_ge(gate_read.sem, i + 1)
                    for w, part in enumerate((gate_part, up_part)):
                        for f in range(FC):
                            m = pe.matmul(bank[2][:, (w * FC + f) * SLOTS:(w * FC + f + 1) * SLOTS],
                                          part[:, f * P:(f + 1) * P], fold[:, :], start=True, stop=True)
                            if w == f == 0:
                                m.then_inc(ring_free.sem, 1)
                    m.then_inc(fold_done.sem, 1)
                    pe.wait_ge(pick_ready.sem, i + (l + 2))
                    pe.wait_ge(scat_ready.sem, i + (l + 2))
                    gather(scat_added.at(i + l, 7))
                    pe.wait_ge(scat_added.sem, scat_added.at(i + l, 8))
                    pe.wait_ge(hid_ready.sem, i + 1)
                    for pair in range(2):
                        for c in range(4):
                            for side in range(2):
                                f = 2 * pair + side
                                if c == 0:
                                    here(8 + f)
                                m = pe.matmul(bank[4 + c][side * SLOTS:(side + 1) * SLOTS, :], hid_t[:, f, :],
                                              exp_slot[8 + f][:, c * PANEL:(c + 1) * PANEL],
                                              start=(pair == 0), stop=(pair == 1))
                                if pair == 1 and c == side == 0:
                                    m.then_inc(ring_free.sem, 2)
                            if pair == 1:
                                m.then_inc(down_done.sem, 1)
                pe.wait_ge(scat_ready.sem, turns1 + (l + 1))
                pe.wait_ge(y_ready.sem, (turns1 + (l + 1)) * 4)
                pe.wait_ge(gather_read.sem, (turns1 + l) * 2 + 2)
                scatter(turns1, last=True)

        @block.scalar
        def _(act):
            act.wait_ge(consts.sem, 1)
            act.wait_ge(rope_dve.sem, 1)
            act.activation(sin_t[:, :, :], ang[:, 1], ACT.Sin).then_inc(rope_act.sem, 1)
            act.activation(cos_t[:, :, :], ang[:, 2], ACT.Sin).then_inc(rope_act.sem, 1)

            with act.Fori(0, depth) as l:
                act.wait_ge(layer_open.sem, layer_open.at(l, 4))
                s = Steps(act, act_steps, l)

                def read_x(g, rnd, src):
                    t, c = g // 4, 4 * (g % 4)
                    act.wait_ge(xt_done.sem, xt_done.at(l, 8 * rnd + g + 1))
                    act.activation(xT[:, c:c + 4, t * P:(t + 1) * P],
                                   src[:, :].rearrange("p (c t) -> p c t", c=4), ACT.Copy).then_inc(xt_act.sem, 1)

                for g in range(0, 8, 2):
                    read_x(g, 0, bank[XT_BANKS[0][g]])
                act.wait_ge(consts.sem, 2)
                act.wait_ge(ab_dve.sem, ab_dve.at(l, 1))
                act.activation(gates[:, 1], gates[:, 0], ACT.Exp, scale=-1.0).then_inc(ab_act.sem, 1)
                s.do(act.activation(gates[:, 7, 0], a_log_b[:, :], ACT.Exp))
                act.activation(gates[:, 8], gates[:, 9], ACT.Exp, scale=-1.0).then_inc(ab_act.sem, 1)
                act.wait_ge(ab_dve.sem, ab_dve.at(l, 2))
                act.activation(gates[:, 3], gates[:, 2], ACT.Ln).then_inc(ab_act.sem, 1)
                for g in range(4):
                    t, c = g // 2, 4 * (g % 2)
                    act.wait_ge(tq_done.sem, tq_done.at(l, g + 1))
                    act.activation(q_t[:, c:c + 4, t * P:(t + 1) * P],
                                   bank[5 + g % 3][:, :].rearrange("p (c t) -> p c t", c=4), ACT.Copy)\
                        .then_inc(tq_read.sem, 1)
                act.wait_ge(tq_done.sem, tq_done.at(l, 5))
                act.activation(k_t[:, :, :].rearrange("p v t -> p (v t)"), bank[6][:, :], ACT.Copy)\
                    .then_inc(tq_read.sem, 1)

                def silu(n):
                    p, b = n // 2, n % 2
                    half, w = p // 3, p % 3
                    act.wait_ge(conv_ready.sem, conv_ready.at(l, n + 1))
                    act.activation(qkv_t[:, half, w, 2 * b:2 * b + 2, :].rearrange("p h t -> p (h t)"),
                                   conv_y[:, n % 2, :], ACT.Silu).then_inc(silu_done.sem, 1)

                def norms(half):
                    act.wait_ge(silu_done.sem, silu_done.at(l, 6 * half + 6))
                    for u in range(6):
                        n = 4 * half + u
                        if u < 4:
                            w, b = u // 2, u % 2
                            if n >= 2:
                                act.wait_ge(ss_done.sem, ss_done.at(l, n - 1))
                            act.activation(square[:, n % 2, :],
                                           qkv_t[:, half, w, 2 * b:2 * b + 2, :].rearrange("p h t -> p (h t)"),
                                           ACT.Square).then_inc(square_ready.sem, 1)
                        if u >= 2:
                            n = 4 * half + u - 2
                            w = (u - 2) // 2
                            act.wait_ge(ss_done.sem, ss_done.at(l, n + 1))
                            if n >= 2:
                                act.wait_ge(normed.sem, normed.at(l, n - 1))
                            act.activation(rot_ab[n % 2], bank[4 + n % 2][:, :], ACT.Sqrt,
                                           bias=eps_dn[:, w:w + 1], scale=float(dk) if w == 0 else 1.0)\
                                .then_inc(norm_sqrt.sem, 1)

                rot_ab = [rot_a[:, :], rot_b[:, :]]
                silu(0)
                silu(1)
                act.wait_ge(max_ready.sem, max_ready.at(l, 1))
                for h in range(n_q):
                    act.activation(probs[:, h, 0:P], probs[:, h, 0:P], ACT.Exp, bias=mx[:, 0, h:h + 1],
                                   accum_out=row_sum[:, 0, h:h + 1])
                    act.activation(probs[:, h, P:3 * P], probs[:, h, P:3 * P], ACT.Exp, bias=mx[:, 1, h:h + 1],
                                   accum_out=row_sum[:, 1, h:h + 1])
                act.activation(sink_e[:, :, :], sink_e[:, :, :], ACT.Exp).then_inc(exp_done.sem, 1)
                for n in range(2, 6):
                    silu(n)
                for h in range(n_q):
                    act.wait_ge(pt_done.sem, pt_done.at(l, h + 1))
                    if h >= 4:
                        act.wait_ge(pv_done.sem, pv_done.at(l, h - 3))
                    act.activation(prob_t[:, h % 4, :], bank[4 + h % 2][:, 0:3 * P], ACT.Copy)\
                        .then_inc(pt_read.sem, 1)
                norms(0)
                silu(6)
                silu(7)
                silu(8)
                silu(9)
                act.wait_ge(gc_dve.sem, gc_dve.at(l, 1))
                act.activation(gfac[:, 0:2, :], gfac[:, 0:2, :], ACT.Exp).then_inc(gc_act.sem, 1)
                silu(10)
                silu(11)
                norms(1)

                def silu_z(i):
                    for t in range(NT):
                        act.wait_ge(proj_done.sem, proj_done.at(l, 2 * (9 + i) + t + 1))
                        z = act.activation(z_act[:, t, i * PANEL:(i + 1) * PANEL], bank[2 * ((9 + i) % 2) + t][:, :],
                                           ACT.Silu)
                    z.then_inc(z_read.sem, 1)

                silu_z(0)
                for half in range(2):
                    for t in range(NT):
                        n = 2 * half + t
                        act.wait_ge(decay_arg.sem, decay_arg.at(l, n + 1))
                        d = decay[:, t].rearrange("p h c -> p (h c)")
                        act.activation(d, d, ACT.Exp).then_inc(decay_exp.sem, 1)
                    if half == 0:
                        silu_z(1)
                    act.wait_ge(u0_done.sem, u0_done.at(l, half + 1))
                    s.do(act.activation(prob_t[:, 0:2, 0:2 * P], bank[7][:, :].rearrange("p (a c) -> p a c", a=2), ACT.Copy))
                    act.activation(v_new[:, 0].rearrange("p h c -> p (h c)"), bank[4][:, :], ACT.Copy)\
                        .then_inc(v0_ready.sem, 1)
                    act.wait_ge(s_done.sem, s_done.at(l, half + 1))
                    s.do(act.activation(o_nat[:, 0, half * PANEL:(half + 1) * PANEL], bank[5][:, :], ACT.Copy))
                    act.activation(prob_t[:, 2:4, 0:2 * P], bank[6][:, :].rearrange("p (a c) -> p a c", a=2), ACT.Copy)\
                        .then_inc(s_ready.sem, 1)
                    act.wait_ge(v1_done.sem, v1_done.at(l, half + 1))
                    act.activation(v_new[:, 1].rearrange("p h c -> p (h c)"), bank[4][:, :], ACT.Copy)\
                        .then_inc(v1_ready.sem, 1)
                    for t in range(NT):
                        n = 2 * half + t
                        act.wait_ge(rms_arg.sem, rms_arg.at(l, n + 1))
                        act.activation(rms[:, 1], rms[:, 0], ACT.Sqrt, bias=eps_dn[:, 1:2], scale=1.0 / dk)\
                            .then_inc(rms_sqrt.sem, 1)
                    for t in range(NT):
                        act.wait_ge(to_done.sem, to_done.at(l, 2 * half + t + 1))
                        c = q_dim // P + half * HALF
                        act.activation(mixT[:, c:c + HALF, t * P:(t + 1) * P],
                                       bank[4 + t][:, :].rearrange("p (c t) -> p c t", c=4), ACT.Copy)\
                            .then_inc(to_read.sem, 1)

                def deviations(rnd):
                    for t in range(NT):
                        n = 2 * rnd + t
                        act.wait_ge(var_ready.sem, var_ready.at(l, n + 1))
                        act.activation(ln_s[:, 0, t:t + 1], mean_var[:, t, 1:2], ACT.Sqrt, bias=eps_dn[:, 2:3])\
                            .then_inc(ln_sqrt.sem, 1)

                deviations(0)
                for g in (0, 1, 2, 3, 4, 6):
                    read_x(g, 1, bank[XT_BANKS[1][g]])
                act.wait_ge(logit_done.sem, logit_done.at(l, 1))
                act.activation(r[:, 0].rearrange("p t e -> p (t e)"), bank[4][:, 0:NT * n_exp], ACT.Exp, scale=-1.0)\
                    .then_inc(logit_exp.sem, 1)
                act.activation(scat_rows[:, :], zero[:, 0:1].to_broadcast([P, NT * P]), ACT.Copy)\
                    .then_inc(scat_ready.sem, 1)
                act.activation(y_hi[:, :], zero[:, 0:1].to_broadcast([P, D]), ACT.Copy)
                act.activation(y_lo[:, :], zero[:, 0:1].to_broadcast([P, D]), ACT.Copy).then_inc(y_ready.sem, 4)
                for t in range(NT):
                    m = act.activation(acc[:, t, :], x_nat[:, t, :], ACT.Copy, scale=ALPHA)
                m.then_inc(acc_ready.sem, 1)

                turns0 = act.value_load(turns[0:1, bass.ds(l, 1)], min_val=0, max_val=depth * TURNS)

                def gather_out(n):
                    for b in range(2):
                        act.wait_ge(gather_done.sem, n * 2 + (b + 1))
                        act.activation(xg_t[:, 8 * b:8 * b + 8, :].rearrange("p c s -> p (c s)"), bank[b][:, :],
                                       ACT.Copy).then_inc(gather_read.sem, 1)

                gather_out(turns0 + l)
                act.wait_ge(moe_open.sem, l + 1)
                turns1 = act.value_load(turns[0:1, bass.ds(l + 1, 1)], min_val=1, max_val=depth * TURNS)
                with act.Fori(turns0, turns1) as i:
                    act.wait_ge(gateup_done.sem, i * 2 + 1)
                    act.activation(gate_part, bank[2][:, :], ACT.Copy).then_inc(gate_read.sem, 1)
                    act.wait_ge(scat_put.sem, scat_put.at(i + l, 8))
                    act.activation(slot_gate[:, :], bank[0][:, NT * P:NT * P + 1], ACT.Copy)
                    act.activation(scat_rows[:, :], bank[0][:, 0:NT * P], ACT.Copy).then_inc(scat_ready.sem, 1)
                    act.wait_ge(fold_done.sem, i + 1)
                    act.activation(act_t, bank[2][:, 0:FC * SLOTS], ACT.Silu).then_inc(silu_ready.sem, 1)
                    gather_out(i + (l + 1))
                    for c in range(4):
                        act.wait_ge(down_done.sem, i * 4 + (c + 1))
                        if c == 0:
                            act.wait_ge(scat_ready.sem, i + (l + 2))
                        act.activation(y_hi[:, c * PANEL:(c + 1) * PANEL], bank[4 + c][:, :], ACT.Copy,
                                       scale=slot_gate[:, 0:1]).then_inc(hi_ready.sem, 1)
                deviations(1)
                s.close()

        @block.vector
        def _(dve):
            tt, ts, stt = dve.tensor_tensor, dve.tensor_scalar, dve.scalar_tensor_tensor
            s = Steps(dve, dve_setup, 0)
            dve.wait_ge(consts.sem, 1)
            dve.wait_ge(pos_loaded.sem, 16)
            s.link(dve.tensor_copy(pos_f[:, :], pos_i[:, :]))
            for t in range(NT):
                s.link(ts(ang[:, 0, t, :], inv_freq[:, :], pos_f[:, t:t + 1], None, ALU.mult))
            big = 1.5 * 2.0 ** 23
            parts = (6.28125, 1.93500518798828125e-3, 3.0199159819e-07)
            for j, shift in ((1, 0.0), (2, 0.25)):
                s.link(ts(ang[:, 3], ang[:, 0], 1.0 / (2.0 * np.pi), shift, ALU.mult, ALU.add))
                s.link(ts(ang[:, 3], ang[:, 3], big, -big, ALU.add, ALU.add))
                src = ang[:, 0]
                for part in parts:
                    s.link(stt(out=ang[:, j], in0=ang[:, 3], scalar=-part, in1=src, op0=ALU.mult, op1=ALU.add))
                    src = ang[:, j]
                if j == 2:
                    s.link(ts(ang[:, j], ang[:, j], float(np.pi / 2), None, ALU.add))
                s.link(ts(ang[:, j], ang[:, j], SIN_LIMIT, -SIN_LIMIT, ALU.min, ALU.max))
            dve.sem_inc(rope_dve.sem, 1)
            dve.wait_ge(rope_act.sem, 2)
            dve.sem_inc(ring_free.sem, 2 * RING - 2)
            dve.wait_ge(once_loaded.sem, 16 * 4)
            dve.sem_inc(layer_open.sem, 4)

            with dve.Fori(0, depth) as l:
                s = Steps(dve, dve_steps, l)

                def read_x(g, rnd, src):
                    t, c = g // 4, 4 * (g % 4)
                    dve.wait_ge(xt_done.sem, xt_done.at(l, 8 * rnd + g + 1))
                    dve.tensor_copy(xT[:, c:c + 4, t * P:(t + 1) * P],
                                    src[:, :].rearrange("p (c t) -> p c t", c=4)).then_inc(xt_dve.sem, 1)

                for g in range(1, 8, 2):
                    read_x(g, 0, bank[XT_BANKS[0][g]])
                dve.wait_ge(consts.sem, 2)

                def rope(ps, t, heads, out_ap):
                    v = ps.rearrange("p (h r d) -> p h r d", h=heads, r=2)
                    n = heads * HEAD_DIM
                    a = rot_a[:, 0:n].rearrange("p (h d) -> p h d", h=2 * heads)
                    b = rot_b[:, 0:n].rearrange("p (h d) -> p h d", h=2 * heads)
                    src = ps.rearrange("p (h d) -> p h d", h=2 * heads)
                    s.do(tt(a, src, bc(cos_t[:, t, :], 1, 2 * heads), ALU.mult))
                    s.do(tt(b, src, bc(sin_t[:, t, :], 1, 2 * heads), ALU.mult))
                    s.sync()
                    a2 = rot_a[:, 0:n].rearrange("p (h r d) -> p h r d", h=heads, r=2)
                    b2 = rot_b[:, 0:n].rearrange("p (h r d) -> p h r d", h=heads, r=2)
                    return [(tt, out_ap(0), a2[:, :, 0, :], b2[:, :, 1, :], ALU.subtract),
                            (tt, out_ap(1), a2[:, :, 1, :], b2[:, :, 0, :], ALU.add)]

                for i in range(2):
                    for t in range(NT):
                        dve.wait_ge(proj_done.sem, proj_done.at(l, 2 * i + t + 1))
                        o = q_rot[:, t, i * PANEL:(i + 1) * PANEL].rearrange("p (h r d) -> p h r d", h=8, r=2)
                        ops = rope(bank[2 * i + t][:, :], t, 8, lambda half: o[:, :, half, :])
                        for f, *args in ops:
                            s.do(f(*args))
                        s.sync()
                    dve.sem_inc(proj_read.sem, 1)
                    dve.sem_inc(roped.sem, 1)
                for t in range(NT):
                    dve.wait_ge(proj_done.sem, proj_done.at(l, 4 + t + 1))
                    for dup in range(2):
                        ops = rope(bank[t][:, 0:kv_dim], t, n_kv,
                                   lambda half: k_rot[:, t, :, dup, half * 32:(half + 1) * 32])
                        for f, *args in ops:
                            s.do(f(*args))
                        s.sync()
                    s.do(dve.tensor_copy(v_nat[:, t, :], bank[t][:, kv_dim:2 * kv_dim]))
                s.sync()
                dve.sem_inc(proj_read.sem, 1)
                dve.sem_inc(roped.sem, 1)

                dve.wait_ge(ab_done.sem, ab_done.at(l, 1))
                dve.wait_ge(small_loaded.sem, small_loaded.at(l, 96))
                ab = bank[4][:, 0:4 * n_dn].rearrange("p (t w h) -> p t w h", t=NT, w=2)
                s.do(tt(gates[:, 4], ab[:, :, 0, :], bc(dt_b[:, :], 1, NT), ALU.add))
                s.do(dve.tensor_copy(gates[:, 9], ab[:, :, 1, :]))
                s.do(dve.tensor_copy(taps[:, :], bank[4][:, 64:64 + taps_nat.shape[0]]))
                s.sync()
                stt(out=gates[:, 0], in0=gates[:, 4], scalar=-1.0, in1=gates[:, 4], op0=ALU.mult, op1=ALU.max)\
                    .then_inc(ab_dve.sem, 1)
                dve.wait_ge(ab_act.sem, ab_act.at(l, 1))
                s.do(ts(gates[:, 5], gates[:, 4], 0.0, None, ALU.max))
                ts(gates[:, 2], gates[:, 1], 1.0, None, ALU.add).then_inc(ab_dve.sem, 1)
                dve.wait_ge(ab_act.sem, ab_act.at(l, 3))
                s.do(ts(gates[:, 8], gates[:, 8], 1.0, None, ALU.add))
                s.do(ts(gates[:, 2], gates[:, 2], -1.0, None, ALU.add))
                s.do(tt(gates[:, 3], gates[:, 3], gates[:, 1], ALU.mult))
                s.sync()
                s.link(ts(gates[:, 6], gates[:, 2], 0.0, None, ALU.is_equal))
                s.do(dve.reciprocal(beta[:, :, :], gates[:, 8]))
                s.do(tt(gates[:, 2], gates[:, 2], gates[:, 6], ALU.add))
                s.do(tt(gates[:, 6], gates[:, 6], gates[:, 1], ALU.mult))
                s.sync()
                s.do(tt(gates[:, 3], gates[:, 3], gates[:, 6], ALU.add))
                s.do(dve.reciprocal(gates[:, 2], gates[:, 2]))
                s.sync()
                s.link(tt(gates[:, 3], gates[:, 3], gates[:, 2], ALU.mult))
                s.link(tt(gates[:, 3], gates[:, 3], gates[:, 5], ALU.add))
                s.link(tt(gates[:, 3], gates[:, 3], bc(gates[:, 7, 0, :], 1, NT), ALU.mult))
                ts(g_nat[:, :, :], gates[:, 3], -1.0, None, ALU.mult).then_inc(g_ready.sem, 1)

                def conv(p):
                    half, w = p // 3, p % 3
                    i = 3 + p
                    for b in range(2):
                        n = 2 * p + b
                        dve.wait_ge(proj_done.sem, proj_done.at(l, 2 * i + b + 1))
                        if n >= 2:
                            dve.wait_ge(silu_done.sem, silu_done.at(l, n - 1))
                        chunk = w * n_dn + half * HALF + 2 * b
                        ps = bank[2 * (i % 2) + b]
                        for tap in range(4):
                            back = 3 - tap
                            for c in range(2):
                                w_c = taps[:, tap * 3 * n_dn + chunk + c:tap * 3 * n_dn + chunk + c + 1]
                                o = conv_y[:, n % 2, c * T:(c + 1) * T]
                                src = ps[:, c * T:(c + 1) * T]
                                if tap == 0:
                                    w_c = taps[:, 3 * 3 * n_dn + chunk + c:3 * 3 * n_dn + chunk + c + 1]
                                    s.do(ts(o, src, w_c, None, ALU.mult))
                                else:
                                    back = tap
                                    w_c = taps[:, (3 - tap) * 3 * n_dn + chunk + c:(3 - tap) * 3 * n_dn + chunk + c + 1]
                                    s.do(stt(out=o[:, back:T], in0=src[:, 0:T - back], scalar=w_c,
                                             in1=o[:, back:T], op0=ALU.mult, op1=ALU.add))
                            s.sync()
                        dve.sem_inc(conv_ready.sem, 1)
                    dve.sem_inc(proj_read.sem, 1)

                def normalise(half):
                    for u in range(4):
                        n = 4 * half + u
                        w, b = u // 2, u % 2
                        dve.wait_ge(norm_sqrt.sem, norm_sqrt.at(l, n + 1))
                        ra = (rot_a, rot_b)[n % 2]
                        s.link(dve.reciprocal(ra[:, :], ra[:, :]))
                        v = qkv_t[:, half, w, 2 * b:2 * b + 2, :].rearrange("p h t -> p (h t)")
                        tt(v, v, ra[:, :], ALU.mult).then_inc(normed.sem, 1)

                conv(0)
                for h in range(n_q):
                    dve.wait_ge(score_done.sem, score_done.at(l, h + 1))
                    stt(out=probs[:, h, :], in0=bank[4 + h % 4][:, 0:3 * P], scalar=HEAD_DIM ** -0.5,
                        in1=win_mask[:, :], op0=ALU.mult, op1=ALU.add).then_inc(score_read.sem, 1)
                dve.wait_ge(score_read.sem, score_read.at(l, n_q))
                s.do(dve.tensor_reduce(mx[:, 0, :], probs[:, :, 0:P], AX.X, ALU.max))
                s.do(dve.tensor_reduce(mx[:, 1, :], probs[:, :, P:3 * P], AX.X, ALU.max))
                s.sync()
                s.link(tt(mx[:, :, :], mx[:, :, :], bc(sinks[:, :], 1, NT), ALU.max))
                s.do(tt(sink_e[:, :, :], bc(sinks[:, :], 1, NT), mx[:, :, :], ALU.subtract))
                ts(mx[:, :, :], mx[:, :, :], -1.0, None, ALU.mult).then_inc(max_ready.sem, 1)
                dve.wait_ge(exp_done.sem, exp_done.at(l, 1))
                s.link(tt(row_sum[:, :, :], row_sum[:, :, :], sink_e[:, :, :], ALU.add))
                s.link(dve.reciprocal(row_sum[:, :, :], row_sum[:, :, :]))
                s.do(tt(probs[:, :, 0:P], probs[:, :, 0:P], bc(row_sum[:, 0, :], 2, P), ALU.mult))
                tt(probs[:, :, P:3 * P], probs[:, :, P:3 * P], bc(row_sum[:, 1, :], 2, 2 * P), ALU.mult)\
                    .then_inc(probs_ready.sem, 1)
                conv(1)
                conv(2)
                for j in range(n_q // 2):
                    dve.wait_ge(pv_done.sem, pv_done.at(l, 2 * j + 2))
                    dve.tensor_copy(mixT[:, j, :], bank[6 + j % 2][:, 0:T]).then_inc(pv_read.sem, 1)
                conv(3)
                normalise(0)
                conv(4)
                dve.wait_ge(gc_done.sem, gc_done.at(l, 1))
                s.link(dve.tensor_copy(gc[:, :, :].rearrange("p t h -> p (t h)"), bank[4][:, 0:3 * n_dn]))
                s.do(dve.tensor_copy(gfac[:, 1, :], gc[:, 1, :]))
                tt(gfac[:, 0, :], gc[:, 2, :], gc[:, 0, :], ALU.subtract).then_inc(gc_dve.sem, 1)
                conv(5)
                dve.wait_ge(gc_act.sem, gc_act.at(l, 1))
                s.link(tt(gfac[:, 2, :], gfac[:, 1, :], beta[:, 1, :], ALU.mult))
                s.link(ts(gfac[:, 2, :], gfac[:, 2, :], -1.0, None, ALU.mult))
                normalise(1)

                def heads(ap, half):
                    return ap[:, half * HALF:(half + 1) * HALF]

                def spread(half, t):
                    s.do(tt(decay[:, t], bc(tri[:, :], 1, HALF), bc(heads(g_nat[:, t, :], half), 2, P), ALU.mult))
                    tt(l_t[:, t], bc(ident[:, :], 1, HALF), bc(heads(beta[:, t, :], half), 2, P), ALU.mult)\
                        .then_inc(spread_ready.sem, 1)

                for half in range(2):
                    if half == 0:
                        dve.wait_ge(pt_done.sem, pt_done.at(l, n_q))
                    else:
                        dve.wait_ge(o1_done.sem, o1_done.at(l, 1))
                    spread(half, 0)
                    spread(half, 1)
                    for t in range(NT):
                        n = 2 * half + t
                        dve.wait_ge(spread_done.sem, spread_done.at(l, n + 1))
                        v4 = bank[4][:, :].rearrange("p (h c) -> p h c", h=HALF)
                        s.link(tt(decay[:, t], v4, bc(heads(gc[:, t, :], half), 2, P), ALU.subtract))
                        ts(decay[:, t], decay[:, t], 0.0, None, ALU.min).then_inc(decay_arg.sem, 1)
                        dve.wait_ge(pair_done.sem, pair_done.at(l, n + 1))
                        dve.wait_ge(decay_exp.sem, decay_exp.at(l, n + 1))
                        kk = bank[6][:, :].rearrange("p (h c) -> p h c", h=HALF)
                        qk = bank[7][:, :].rearrange("p (h c) -> p h c", h=HALF)
                        bb = bank[5][:, :].rearrange("p (h c) -> p h c", h=HALF)
                        s.link(tt(l_t[:, t], kk, decay[:, t], ALU.mult))
                        s.do(tt(l_t[:, t], bb, l_t[:, t], ALU.mult))
                        s.link(tt(decay[:, t], decay[:, t], bc(tri[:, :], 1, HALF), ALU.mult))
                        tt(a_t[:, t], qk, decay[:, t], ALU.mult).then_inc(pair_read.sem, 1)
                        dve.wait_ge(kv_done.sem, kv_done.at(l, n + 1))
                        if t == 0:
                            s.do(tt(k_out[:, :, :], kk, bc(heads(gfac[:, 0, :], half), 2, P), ALU.mult))
                        else:
                            s.do(tt(k_in[:, :, :], kk, bc(heads(gfac[:, 2, :], half), 2, P), ALU.mult))
                        tt(v_beta[:, t], qk, bc(heads(beta[:, t, :], half), 2, P), ALU.mult).then_inc(kv_read.sem, 1)
                    for t in range(NT):
                        s.do(dve.tensor_copy(inv[:, t], bc(ident[:, :], 1, HALF)))
                    s.do(dve.tensor_copy(inv_t[:, 0], bc(ident[:, :], 1, HALF)))
                    dve.tensor_copy(inv_t[:, 1], bc(ident[:, :], 1, HALF)).then_inc(inv_open.sem, 1)
                    for lev in range(LEVELS):
                        for t in range(NT):
                            n = (half * LEVELS + lev) * NT + t
                            dve.wait_ge(lt_done.sem, lt_done.at(l, n + 1))
                            tt(masked[:, t], bank[4 + 2 * t][:, :].rearrange("p (h c) -> p h c", h=HALF),
                               bc(level_mask[:, lev, :], 1, HALF), ALU.mult).then_inc(masked_ready.sem, 1)
                        for t in range(NT):
                            n = (half * LEVELS + lev) * NT + t
                            dve.wait_ge(tlt_done.sem, tlt_done.at(l, n + 1))
                            s.do(tt(inv[:, t], bank[5 + 2 * t][:, :].rearrange("p (h c) -> p h c", h=HALF),
                                    inv[:, t], ALU.add))
                            tt(inv_t[:, t], bank[4 + 2 * t][:, :].rearrange("p (h c) -> p h c", h=HALF),
                               inv_t[:, t], ALU.add).then_inc(inv_ready.sem, 1)
                    dve.wait_ge(o1_done.sem, o1_done.at(l, half + 1))
                    o = o_nat[:, :, half * PANEL:(half + 1) * PANEL].rearrange("p t (h c) -> p t h c", h=HALF)
                    s.link(tt(o[:, 1], bank[6][:, :].rearrange("p (h c) -> p h c", h=HALF),
                              bc(heads(gfac[:, 1, :], half), 2, P), ALU.mult))
                    tt(o[:, 1], bank[7][:, :].rearrange("p (h c) -> p h c", h=HALF), o[:, 1], ALU.add)\
                        .then_inc(o_ready.sem, 1)
                    dve.wait_ge(o_ready.sem, o_ready.at(l, half + 1))
                    dve.wait_ge(s_ready.sem, s_ready.at(l, half + 1))
                    dve.wait_ge(z_read.sem, z_read.at(l, 2))
                    for t in range(NT):
                        n = 2 * half + t
                        sq = decay[:, t]
                        s.link(tt(sq, o[:, t], o[:, t], ALU.mult))
                        dve.tensor_reduce(rms[:, 0], sq, AX.X, ALU.add).then_inc(rms_arg.sem, 1)
                        dve.wait_ge(rms_sqrt.sem, rms_sqrt.at(l, n + 1))
                        s.link(dve.reciprocal(rms[:, 2], rms[:, 1]))
                        s.link(tt(o[:, t], o[:, t], bc(rms[:, 2], 2, P), ALU.mult))
                        s.link(tt(o[:, t], o[:, t], bc(dn_w[:, :], 1, HALF), ALU.mult))
                        zz = z_act[:, t, half * PANEL:(half + 1) * PANEL].rearrange("p (h c) -> p h c", h=HALF)
                        tt(o[:, t], o[:, t], zz, ALU.mult).then_inc(dn_out.sem, 1)

                def statistics(t, c, src):
                    s.do(dve.bn_stats(stats[:, t, c, :], src[:, t, c * PANEL:(c + 1) * PANEL]))

                def add_panel(i, t):
                    dve.wait_ge(proj_done.sem, proj_done.at(l, 2 * (N_IN + i) + t + 1))
                    xs = x_nat[:, t, i * PANEL:(i + 1) * PANEL]
                    s.do(stt(out=xs, in0=xs, scalar=ALPHA, in1=bank[2 * ((N_IN + i) % 2) + t][:, :],
                             op0=ALU.mult, op1=ALU.add))

                def layer_norm(rnd, t, src, loaded, signal_to):
                    s.sync()
                    s.do(dve.memset(ln_s[:, :, t], 0.0))
                    dve.bn_aggr(mean_var[:, t, :], stats[:, t, :, :]).then_inc(var_ready.sem, 1)
                    dve.wait_ge(var_ready.sem, var_ready.at(l, 2 * rnd + t + 1))
                    dve.wait_ge(loaded.sem, loaded.at(l, 32))
                    s.do(stt(out=x_nat[:, t, :], in0=src[:, t, :], scalar=mean_var[:, t, 0:1], in1=ln_par[:, 0, :],
                             op0=ALU.subtract, op1=ALU.mult))
                    dve.wait_ge(ln_sqrt.sem, ln_sqrt.at(l, 2 * rnd + t + 1))
                    s.link(dve.reciprocal(ln_s[:, 1, t:t + 1], ln_s[:, 0, t:t + 1]))
                    for side in range(2):
                        cols = slice(side * D // 2, (side + 1) * D // 2)
                        stt(out=x_nat[:, t, cols], in0=x_nat[:, t, cols], scalar=ln_s[:, 1, t:t + 1],
                            in1=ln_par[:, 1, cols], op0=ALU.mult, op1=ALU.add).then_inc(signal_to.sem, 1)

                for i in range(N_OUT - 1):
                    for t in range(NT):
                        add_panel(i, t)
                    s.sync()
                    dve.sem_inc(proj_read.sem, 1)
                    for t in range(NT):
                        statistics(t, i, x_nat)
                for t in range(NT):
                    add_panel(N_OUT - 1, t)
                    s.sync()
                    statistics(t, N_OUT - 1, x_nat)
                    layer_norm(0, t, x_nat, ln1_loaded, ln_done)
                dve.sem_inc(proj_read.sem, 1)
                for g in (5, 7):
                    read_x(g, 1, bank[XT_BANKS[1][g]])

                score, sel, rank, top, member, wsel = (r[:, i] for i in range(6))
                gate = r[:, 6]
                dve.wait_ge(logit_exp.sem, logit_exp.at(l, 1))
                s.link(ts(r[:, 0], r[:, 0], 1.0, None, ALU.add))
                s.link(dve.reciprocal(r[:, 0], r[:, 0]))
                s.link(tt(sel, score, bc(b_rout[:, :], 1, NT), ALU.add))
                tg = NT * N_GROUPS

                def ranks(values, n, m, out_ap):
                    mine, other = bc(values, 3, m), bc(values, 2, m)
                    ca, cb = cmp_a[:, 0:n], cmp_b[:, 0:n]
                    s.do(tt(ca, other, mine, ALU.is_gt))
                    s.link(tt(cb, other, mine, ALU.is_equal))
                    s.link(tt(cb, cb, bc(before[:, :, :], 1, n), ALU.mult))
                    s.link(tt(ca, ca, cb, ALU.add))
                    s.link(dve.tensor_reduce(out_ap, ca, AX.X, ALU.add))

                def grouped(ap):
                    return ap.rearrange("p t (g e) -> p (t g) e", e=EPG)

                ranks(grouped(sel), tg, EPG, grouped(rank))
                s.link(ts(top, rank, 1.5, None, ALU.is_lt))
                s.link(tt(wsel, top, sel, ALU.mult))
                s.link(dve.tensor_reduce(gr[:, 0].rearrange("p t g -> p (t g)"), grouped(wsel), AX.X, ALU.add))
                ranks(gr[:, 0], NT, N_GROUPS, gr[:, 1])
                s.link(ts(gr[:, 2], gr[:, 1], 0.5, None, ALU.is_lt))
                tt(grouped(member), grouped(top), bc(gr[:, 2].rearrange("p t g -> p (t g)"), 2, EPG), ALU.mult)\
                    .then_inc(member_ready.sem, 1)
                dve.wait_ge(member_ready.sem, member_ready.at(l, 1))
                s.link(tt(wsel, member, score, ALU.mult))
                s.link(dve.tensor_reduce(gr[:, 0, :, 0], wsel, AX.X, ALU.add))
                s.link(dve.reciprocal(gr[:, 0, :, 1], gr[:, 0, :, 0]))
                s.link(tt(gate, wsel, bc(gr[:, 0, :, 1], 2, n_exp), ALU.mult))
                dve.wait_ge(rank_done.sem, rank_done.at(l, 1))
                slot1 = r[:, 7]
                pos = bank[5][:, 0:2 * n_exp].rearrange("p (t e) -> p t e", t=NT)
                s.link(ts(slot1, pos, 1.0, None, ALU.add))
                s.link(tt(slot1, slot1, member, ALU.mult))
                s.do(ts(slot_of[:, :, 0:n_exp], slot1, -1.0, None, ALU.add))
                s.do(dve.tensor_copy(gate_of[:, :, 0:n_exp], gate))
                s.sync()

                def pick_tokens(col):
                    dve.tensor_copy(gate_col[:, :], gate_of[:, :, bass.ds(col, 1)].rearrange("p t a -> p (t a)"))
                    for t in range(NT):
                        m = ts(pick[:, t, :], slot_id[:, :], slot_of[:, t, bass.ds(col, 1)], None, ALU.is_equal)
                    return m

                pick_tokens(0).then_inc(pick_ready.sem, 1)
                for tau in range(3):
                    s.do(ts(flags[:, tau * n_exp:(tau + 1) * n_exp], bank[5][:, 2 * n_exp:3 * n_exp],
                            SLOTS * (tau + 1) + 0.5, None, ALU.is_gt))
                s.sync()
                s.link(dve.tensor_copy(cum[:, 0, :], flags[:, :]))
                side, step = 0, 1
                while step < N_FLAGS:
                    s.do(dve.tensor_copy(cum[:, 1 - side, 0:step], cum[:, side, 0:step]))
                    s.link(tt(cum[:, 1 - side, step:], cum[:, side, step:], cum[:, side, 0:N_FLAGS - step], ALU.add))
                    side, step = 1 - side, 2 * step
                s.link(tt(hot[:, :, :], bc(cum[:, side, :], 1, EXTRA), bc(extra_id[:, :], 2, N_FLAGS), ALU.is_equal))
                s.link(tt(hot[:, :, :], hot[:, :, :], bc(flags[:, :], 1, EXTRA), ALU.mult))
                s.link(tt(hot_w[:, :, :], hot[:, :, :], bc(flag_exp[:, :], 1, EXTRA), ALU.mult))
                s.link(dve.tensor_reduce(ext[:, 0, :], hot_w[:, :, :], AX.X, ALU.add))
                s.link(tt(hot_w[:, :, :], hot[:, :, :], bc(flag_off[:, :], 1, EXTRA), ALU.mult))
                s.link(dve.tensor_reduce(ext[:, 1, :], hot_w[:, :, :], AX.X, ALU.add))
                s.do(dve.tensor_copy(extra_e[:, :], ext[:, 0, :]))
                s.do(dve.tensor_copy(extra_n[:, bass.ds(l, 1)], cum[:, side, N_FLAGS - 1:N_FLAGS]))
                s.link(dve.tensor_copy(ext[:, 2, 0:1], cum[:, side, N_FLAGS - 1:N_FLAGS]))
                s.link(tt(hot_e[:, :, :], hot[:, :, 0:n_exp], hot[:, :, n_exp:2 * n_exp], ALU.add))
                s.link(tt(hot_e[:, :, :], hot_e[:, :, :], hot[:, :, 2 * n_exp:3 * n_exp], ALU.add))
                for t in range(NT):
                    h1 = hot_w[:, :, 0:n_exp]
                    s.link(tt(h1, hot_e[:, :, :], bc(slot1[:, t, :], 1, EXTRA), ALU.mult))
                    s.link(dve.tensor_reduce(slot_of[:, t, n_exp:], h1, AX.X, ALU.add))
                    s.link(tt(h1, hot_e[:, :, :], bc(gate[:, t, :], 1, EXTRA), ALU.mult))
                    s.link(dve.tensor_reduce(gate_of[:, t, n_exp:], h1, AX.X, ALU.add))
                    s.link(tt(slot_of[:, t, n_exp:], slot_of[:, t, n_exp:], ext[:, 1, :], ALU.subtract))
                    s.link(ts(slot_of[:, t, n_exp:], slot_of[:, t, n_exp:], -1.0, None, ALU.add))
                s.link(ts(turn_n[:, :], ext[:, 2, 0:1], float(n_exp), None, ALU.add))
                s.link(ts(ext[:, 2, 0:1], ext[:, 2, 0:1], turns_f[:, 0:1], float(n_exp), ALU.add, ALU.add))
                s.do(dve.tensor_copy(turns_f[:, 0:1], ext[:, 2, 0:1]))
                s.link(dve.tensor_copy(turns[:, bass.ds(l + 1, 1)], ext[:, 2, 0:1]))
                dve.wait_ge(acc_ready.sem, acc_ready.at(l, 1))
                dve.sem_inc(route_ready.sem, 1)
                dve.sem_inc(moe_open.sem, 1)

                turns0 = dve.value_load(turns[0:1, bass.ds(l, 1)], min_val=0, max_val=depth * TURNS)
                turns1 = dve.value_load(turns[0:1, bass.ds(l + 1, 1)], min_val=1, max_val=depth * TURNS)

                n_turns = dve.value_load(turn_n[0:1, 0:1], min_val=n_exp, max_val=TURNS - 1)

                def add_scattered(i, tiles=range(NT)):
                    for n in range(4 * tiles[0], 4 * tiles[-1] + 4):
                        t, c = n // 4, n % 4
                        dve.wait_ge(scat_put.sem, scat_put.at(i + l, n + 1))
                        a = acc[:, t, c * PANEL:(c + 1) * PANEL]
                        tt(a, bank[[1, 4, 5, 6, 7, 3, 1, 4][n]][:, :], a, ALU.add).then_inc(scat_added.sem, 1)

                with dve.Fori(0, n_turns) as turn:
                    i = dve.snap(turns0 + turn)
                    dve.wait_ge(gateup_done.sem, i * 2 + 2)
                    dve.tensor_copy(up_part, bank[3][:, :]).then_inc(up_read.sem, 1)
                    pick_tokens(turn + 1).then_inc(pick_ready.sem, 1)
                    add_scattered(i)
                    dve.wait_ge(fold_done.sem, i + 1)
                    dve.wait_ge(silu_ready.sem, i + 1)
                    tt(hid_t[:, :, :].rearrange("p f s -> p (f s)"), bank[2][:, FC * SLOTS:2 * FC * SLOTS], act_t,
                       ALU.mult).then_inc(hid_ready.sem, 1)
                    for c in range(4):
                        dve.wait_ge(hi_ready.sem, i * 4 + (c + 1))
                        cols = slice(c * PANEL, (c + 1) * PANEL)
                        stt(out=y_lo[:, cols], in0=bank[4 + c][:, :], scalar=slot_gate[:, 0:1], in1=y_hi[:, cols],
                            op0=ALU.mult, op1=ALU.subtract).then_inc(y_ready.sem, 1)
                for t in range(NT):
                    add_scattered(turns1, [t])
                    dve.wait_ge(scat_added.sem, scat_added.at(turns1 + l, 4 * t + 4))
                    for c in range(4):
                        statistics(t, c, acc)
                    layer_norm(1, t, acc, ln2_loaded, layer_open)
                dve.wait_ge(layer_open.sem, layer_open.at(l + 1, 4))
                s.close()


_INS = ["x", "positions", "w_in", "attn_sinks", "conv_w", "a_log", "dt_bias", "dn_norm_w", "w_out", "ln1_g",
        "ln1_b", "router_w", "router_bias", "w_gate", "w_up", "w_down", "ln2_g", "ln2_b"]


def kernel(**inputs):
    import numpy as _np
    import concourse.bacc as _bacc
    from concourse import mybir as _mybir
    from concourse.bass_utils import run_bass_kernel_spmd as _run

    nc = _bacc.Bacc("TRN2", target_bir_lowering=False, num_devices=1)
    arrays, args = {}, []
    for name in _INS:
        a = _np.ascontiguousarray(inputs[name])
        arrays[f"in_{name}_dram"] = a
        args.append(nc.dram_tensor(f"in_{name}_dram", a.shape, _mybir.dt.from_np(a.dtype), kind="ExternalInput").ap())
    shape = tuple(inputs["x"].shape)
    args.append(nc.dram_tensor("out_0_dram", shape, _mybir.dt.float32, kind="ExternalOutput").ap())
    trunk(nc, *args)
    r = _run(nc, [arrays], core_ids=[0])
    return r.results[0]["out_0_dram"]
```

```python
from contextlib import ExitStack

import numpy as np

import concourse.bass as bass
from concourse import mybir

F32 = mybir.dt.float32
F32R = mybir.dt.float32r
I32 = mybir.dt.int32
ACT = mybir.ActivationFunctionType
ALU = mybir.AluOpType
AX = mybir.AxisListType

P = 128
WINDOW = 128
HEAD_DIM = 64
ROPE_THETA = 10000.0
LN_EPS = 1e-5
RMS_EPS = 1e-6
N_GROUPS = 4
SLOTS = 64
RING = 6
SIN_LIMIT = 3.1415925


class Signal:

    def __init__(self, sem, per):
        self.sem, self.per = sem, per

    def at(self, turn, n):
        return turn * self.per + n


class Steps:

    def __init__(self, eng, counted, turn):
        self.eng, self.counted, self.turn, self.n = eng, counted, turn, 0

    def do(self, ins):
        self.n += 1
        return ins.then_inc(self.counted.sem, 1)

    def sync(self):
        self.eng.wait_ge(self.counted.sem, self.counted.at(self.turn, self.n))

    def link(self, ins):
        self.do(ins)
        self.sync()

    def close(self):
        if self.counted.per != self.n:
            raise ValueError(f"{self.counted.sem.name} takes {self.n} steps a turn, not {self.counted.per}")


def bc(ap, axis, n):
    ap = ap.unsqueeze(axis)
    shape = list(ap.shape)
    shape[axis] = n
    return ap.to_broadcast(shape)


def trunk(nc, x_in, positions, w_in, attn_sinks, conv_w, a_log, dt_bias, dn_norm_w, w_out, ln1_g, ln1_b,
          router_w, router_bias, w_gate, w_up, w_down, ln2_g, ln2_b, out):
    depth, D, proj_dim = w_in.shape
    T = x_in.shape[1]
    NT = T // P
    KC = D // P
    n_q = attn_sinks.shape[1]
    q_dim = n_q * HEAD_DIM
    n_dn = a_log.shape[1]
    dk = dn_norm_w.shape[1]
    dn_dim = n_dn * dk
    kv_dim = (proj_dim - q_dim - 4 * dn_dim - 2 * n_dn) // 2
    n_kv = kv_dim // HEAD_DIM
    n_exp = router_w.shape[1]
    F = w_gate.shape[3]
    FC = F // P
    EPG = n_exp // N_GROUPS
    EXTRA = 2 * T // SLOTS
    TURNS = n_exp + EXTRA
    assert n_exp % 2 == 0 and EXTRA % 2 == 0
    ALPHA = float((2 * depth) ** 0.25)
    HALF = n_dn // 2
    PANEL = 512
    PIECE = 4 * PANEL
    assert (T, NT, KC, HALF * P, FC) == (2 * P, 2, 16, PANEL, 4) and n_kv == 2 and dk == P

    off_kv = q_dim
    off_dn = q_dim + 2 * kv_dim
    off_z = off_dn + 3 * dn_dim
    off_ab = off_z + dn_dim
    assert 2 * n_dn == 16 and n_exp == 16
    IN_PANELS = [("q", 0), ("q", PANEL), ("kv", off_kv)]
    IN_PANELS += [("dn", off_dn + which * dn_dim + half * PANEL) for half in range(2) for which in range(3)]
    IN_PANELS += [("z", off_z), ("z", off_z + PANEL)]
    N_IN = len(IN_PANELS)
    N_OUT = D // PANEL
    MIX_PIECES = 4 * (N_IN + N_OUT)
    ORDER = [(i, j) for i in range(N_IN) for j in range(4)]
    ORDER += [(i, j) for i in (N_IN, N_IN + 1) for j in range(3)] + [(N_IN, 3), (N_IN + 1, 3)]
    ORDER += [(i, j) for i in (N_IN + 2, N_IN + 3) for j in range(4)]
    assert len(ORDER) == MIX_PIECES
    SCATTER_BANKS = [4, 5, 6, 7, 1, 3, 4, 1]
    GATHER_BANKS = [2, 3, 0, 1]
    DOWN_ORDER = [1, 2, 3, 0]
    XT_BANKS = [[0, 2, 5, 6, 1, 3, 4, 7], [2, 3, 6, 7, 0, 1, 2, 3]]
    EXP_PIECES = 12
    EXP_COUNTED = EXP_PIECES - 2
    assert MIX_PIECES % RING == 0 and EXP_PIECES == 2 * RING
    MIX_USES = MIX_PIECES // RING
    LEVELS = P.bit_length() - 1
    N_FLAGS = 3 * n_exp
    AB_AT, TAPS_AT = T, T + 64

    ctx = ExitStack()
    with ctx:
        def sb(name, shape, dt=F32):
            return ctx.enter_context(nc.sbuf_tensor(name, shape, dt))

        def signal(name, per):
            return Signal(ctx.enter_context(nc.semaphore(name)), per)

        ring = sb("ring", [P, RING, PIECE])
        x_nat = sb("x_nat", [P, NT, D])
        x_t = sb("x_t", [P, KC * T])
        xT = x_t[:, :].rearrange("p (c t) -> p c t", c=KC)
        mix_acc = sb("mix_acc", [P, KC * T])
        mixT = mix_acc[:, :].rearrange("p (c t) -> p c t", c=KC)
        acc = mix_acc[:, :].rearrange("p (t d) -> p t d", t=NT)

        region_a = sb("region_a", [P, 7168])
        region_a_at = nc.sbuf_base - 4 * 7168
        probs = region_a[:, 0:6144].rearrange("p (h k) -> p h k", h=n_q)

        def dn_mat(i):
            return region_a[:, i * 1024:(i + 1) * 1024].rearrange("p (t h c) -> p t h c", t=NT, h=HALF)

        decay, l_t, a_t, inv, inv_t, masked = (dn_mat(i) for i in range(6))
        gate_part = region_a[:, 0:512]
        up_part = region_a[:, 512:1024]
        act_t = region_a[:, 1024:1280]
        hid_t = region_a[:, 1280:1536].rearrange("p (f s) -> p f s", f=FC)
        pick = region_a[:, 1536:1792].rearrange("p (t s) -> p t s", t=NT)
        y_hi = nc.alloc_sbuf_tensor_at("y_hi", [P, D], F32R, offset=region_a_at + 4 * 1792)
        y_lo = nc.alloc_sbuf_tensor_at("y_lo", [P, D], F32R, offset=region_a_at + 4 * (1792 + D))
        scat_rows = nc.alloc_sbuf_tensor_at("scat_rows", [P, NT * P], F32R,
                                            offset=region_a_at + 4 * (1792 + 2 * D))
        scat = scat_rows[:, :].rearrange("p (t c) -> p t c", t=NT)
        assert 1792 + 2 * D + NT * P <= 6144
        region_b = sb("region_b", [P, 6144])
        qkv_t = region_b[:, :].rearrange("p (f w h t) -> p f w h t", f=2, w=3, h=HALF)
        region_cd = sb("region_cd", [P, 2 * NT * q_dim])
        region_c = region_cd[:, 0:NT * q_dim]
        q_rot = region_c[:, :].rearrange("p (t n) -> p t n", t=NT)
        z_act = q_rot
        region_d = region_cd[:, NT * q_dim:]
        q_t = region_d[:, :].rearrange("p (c t) -> p c t", t=T)
        o_nat = region_d[:, :].rearrange("p (t n) -> p t n", t=NT)
        ln_par = region_cd[:, 0:2 * D].rearrange("p (g d) -> p g d", g=2)

        slot_gate = sb("slot_gate", [P, 1])
        gate_col = sb("gate_col", [P, NT])
        k_rot = sb("k_rot", [P, NT, n_kv, 2, HEAD_DIM])
        v_nat = sb("v_nat", [P, NT, n_kv * HEAD_DIM])
        k_t = sb("k_t", [P, n_kv, T])
        v_rot = sb("v_rot", [P, 2 * PANEL])
        rot_a = v_rot[:, 0:PANEL]
        rot_b = v_rot[:, PANEL:2 * PANEL]
        conv_sq = sb("conv_sq", [P, 4 * PANEL])
        conv_y = conv_sq[:, 0:2 * PANEL].rearrange("p (a c) -> p a c", a=2)
        square = conv_sq[:, 2 * PANEL:].rearrange("p (a c) -> p a c", a=2)
        prob_t = sb("prob_t", [P, 4, 3 * P])
        prob_flat = prob_t[:, :, :].rearrange("p a c -> p (a c)")
        xg_half = [region_a[:, 6144:7168], prob_flat[:, 0:1024]]
        w_ab = prob_flat[:, 0:KC * 32].rearrange("p (k n) -> p k n", k=KC)
        ab_part = prob_flat[:, KC * 32:KC * 32 + T]
        logit_part = prob_flat[:, 0:2 * P].rearrange("p (t s) -> p t s", t=NT)
        pick2 = prob_flat[:, 1024:1024 + 2 * P].rearrange("p (t s) -> p t s", t=NT)
        v_beta = v_rot[:, :].rearrange("p (t h c) -> p t h c", t=NT, h=HALF)
        k_in = conv_y[:, 0, :].rearrange("p (h c) -> p h c", h=HALF)
        k_out = conv_y[:, 1, :].rearrange("p (h c) -> p h c", h=HALF)
        v_new = square[:, :, :].rearrange("p t (h c) -> p t h c", h=HALF)

        def w_t(h):
            return prob_t[:, h // 2, (h % 2) * P:(h % 2 + 1) * P]

        def state(h):
            return prob_t[:, 2 + h // 2, (h % 2) * P:(h % 2 + 1) * P]

        ident = sb("ident", [P, P])
        tri = sb("tri", [P, P])
        tri_strict = sb("tri_strict", [P, P])
        ones = sb("ones", [P, P])
        level_mask = sb("level_mask", [P, LEVELS, P])
        pair_mask = sb("pair_mask", [P, P])
        win_mask = sb("win_mask", [P, 3 * P])
        slot_id = sb("slot_id", [P, P])
        fold = sb("fold", [P, SLOTS])
        before = sb("before", [P, EPG, EPG])
        flag_exp = sb("flag_exp", [P, N_FLAGS])
        flag_off = sb("flag_off", [P, N_FLAGS])
        extra_id = sb("extra_id", [P, EXTRA])
        iota_i = sb("iota_i", [P, P], I32)
        inv_freq = sb("inv_freq", [P, HEAD_DIM // 2])
        cos_t = sb("cos_t", [P, NT, HEAD_DIM // 2])
        sin_t = sb("sin_t", [P, NT, HEAD_DIM // 2])
        ang = v_rot[:, 0:4 * NT * HEAD_DIM // 2].rearrange("p (a t f) -> p a t f", a=4, t=NT)
        pos_i = sb("pos_i", [P, NT], I32)
        pos_f = sb("pos_f", [P, NT])
        zero = sb("zero", [P, 1])
        exp_zero = sb("exp_zero", [P, 1])
        eps_dn = sb("eps_dn", [P, 3])

        w_rout = sb("w_rout", [P, KC, 32])
        sum_groups = sb("sum_groups", [P, n_exp])
        sum_ab = sb("sum_ab", [P, 2 * n_dn])
        b_rout = sb("b_rout", [P, n_exp])
        sinks = sb("sinks", [P, n_q])
        a_log_b = sb("a_log_b", [P, n_dn])
        dt_b = sb("dt_b", [P, n_dn])
        dn_w = sb("dn_w", [P, P])
        taps_nat = sb("taps_nat", [4 * 3 * n_dn, P])
        taps = sb("taps", [P, 4 * 3 * n_dn])

        mx = sb("mx", [P, NT, n_q])
        sink_e = sb("sink_e", [P, NT, n_q])
        row_sum = sb("row_sum", [P, NT, n_q])
        gates = sb("gates", [P, 10, NT, n_dn])
        g_nat = sb("g_nat", [P, NT, n_dn])
        beta = sb("beta", [P, NT, n_dn])
        gc = sb("gc", [P, 3, n_dn])
        gfac = sb("gfac", [P, 4, n_dn])
        rms = sb("rms", [P, 4, HALF])
        stats = sb("stats", [P, NT, D // PANEL, 6])
        mean_var = sb("mean_var", [P, NT, 2])
        ln_s = sb("ln_s", [P, 3, NT])
        r = sb("r", [P, 10, NT, n_exp])
        cmp_a = sb("cmp_a", [P, NT * N_GROUPS, EPG, EPG])
        cmp_b = sb("cmp_b", [P, NT * N_GROUPS, EPG, EPG])
        gr = sb("gr", [P, 3, NT, N_GROUPS])
        cum = sb("cum", [P, 2, N_FLAGS])
        flags = sb("flags", [P, N_FLAGS])
        route_tmp = v_rot[:, 0:2 * EXTRA * N_FLAGS + EXTRA * n_exp]
        hot = route_tmp[:, 0:EXTRA * N_FLAGS].rearrange("p (j i) -> p j i", j=EXTRA)
        hot_w = route_tmp[:, EXTRA * N_FLAGS:2 * EXTRA * N_FLAGS].rearrange("p (j i) -> p j i", j=EXTRA)
        hot_e = route_tmp[:, 2 * EXTRA * N_FLAGS:].rearrange("p (j e) -> p j e", j=EXTRA)
        ext = sb("ext", [P, 3, EXTRA])
        slot_of = sb("slot_of", [P, NT, TURNS + 2])
        gate_of = sb("gate_of", [P, NT, TURNS + 2])
        pairs_f = sb("pairs_f", [P, 1])
        pairs = sb("pairs", [P, depth + 1], I32)
        last_pairs = sb("last_pairs", [P, depth], I32)
        pair_n = sb("pair_n", [P, 1], I32)
        extra_n = sb("extra_n", [P, depth], I32)
        extra_e = sb("extra_e", [P, EXTRA], I32)

        bank = [ctx.enter_context(nc.psum_tensor(f"bank{i}", [P, PANEL], F32)) for i in range(8)]

        consts = signal("consts", 0)
        pool_steps = signal("pool_steps", 0)
        once_loaded = signal("once_loaded", 0)
        pos_loaded = signal("pos_loaded", 0)
        rope_act = signal("rope_act", 0)
        rope_dve = signal("rope_dve", 0)
        dve_setup = signal("dve_setup", 0)
        ring_free = signal("ring_free", 0)
        landed = [signal(f"landed{i}", 0) for i in range(2 * RING)]
        layer_open = signal("layer_open", 4)
        small_loaded = signal("small_loaded", 96)
        ln1_loaded = signal("ln1_loaded", 32)
        ln2_loaded = signal("ln2_loaded", 32)
        xt_done = signal("xt_done", 16)
        xt_act = signal("xt_act", 10)
        xt_dve = signal("xt_dve", 6)
        proj_done = signal("proj_done", 2 * (N_IN + N_OUT))
        proj_read = signal("proj_read", N_IN + N_OUT - 2)
        z_read = signal("z_read", 2)
        ab_part_done = signal("ab_part_done", 1)
        ab_part_read = signal("ab_part_read", 1)
        ab_done = signal("ab_done", 1)
        ab_act = signal("ab_act", 3)
        ab_dve = signal("ab_dve", 2)
        g_ready = signal("g_ready", 1)
        roped = signal("roped", 3)
        tq_done = signal("tq_done", 5)
        tq_read = signal("tq_read", 5)
        score_done = signal("score_done", n_q)
        score_read = signal("score_read", n_q)
        max_ready = signal("max_ready", 1)
        exp_done = signal("exp_done", 1)
        probs_ready = signal("probs_ready", 1)
        pt_done = signal("pt_done", n_q)
        pt_read = signal("pt_read", n_q)
        pv_done = signal("pv_done", n_q)
        pv_read = signal("pv_read", n_q // 2)
        conv_ready = signal("conv_ready", 12)
        silu_done = signal("silu_done", 12)
        square_ready = signal("square_ready", 8)
        ss_done = signal("ss_done", 8)
        norm_sqrt = signal("norm_sqrt", 8)
        normed = signal("normed", 8)
        gc_done = signal("gc_done", 1)
        gc_dve = signal("gc_dve", 1)
        gc_act = signal("gc_act", 1)
        spread_ready = signal("spread_ready", 4)
        spread_done = signal("spread_done", 4)
        decay_arg = signal("decay_arg", 4)
        decay_exp = signal("decay_exp", 4)
        pair_done = signal("pair_done", 4)
        pair_read = signal("pair_read", 4)
        kv_done = signal("kv_done", 4)
        kv_read = signal("kv_read", 4)
        lt_done = signal("lt_done", 4 * LEVELS)
        masked_ready = signal("masked_ready", 4 * (LEVELS - 1))
        tlt_done = signal("tlt_done", 4 * (LEVELS - 1))
        inv_ready = signal("inv_ready", 4 * LEVELS)
        u0_done = signal("u0_done", 2)
        v0_ready = signal("v0_ready", 2)
        s_done = signal("s_done", 2)
        s_ready = signal("s_ready", 2)
        v1_done = signal("v1_done", 2)
        v1_ready = signal("v1_ready", 2)
        o1_done = signal("o1_done", 2)
        o_ready = signal("o_ready", 2)
        rms_arg = signal("rms_arg", 4)
        rms_sqrt = signal("rms_sqrt", 4)
        dn_out = signal("dn_out", 4)
        to_done = signal("to_done", 4)
        to_read = signal("to_read", 4)
        var_ready = signal("var_ready", 4)
        ln_sqrt = signal("ln_sqrt", 4)
        acc_ready = signal("acc_ready", 1)
        ln_done = signal("ln_done", 4)
        part_done = signal("part_done", 2)
        part_read = signal("part_read", 2)
        logit_done = signal("logit_done", 1)
        logit_exp = signal("logit_exp", 1)
        member_ready = signal("member_ready", 1)
        rank_done = signal("rank_done", 1)
        route_ready = signal("route_ready", 1)
        route_seen = signal("route_seen", 1)
        open_seen = signal("open_seen", 1)
        moe_open = signal("moe_open", 1)
        act_steps = signal("act_steps", 5)
        dve_steps = signal("dve_steps", 347)
        gather_done = signal("gather_done", 4)
        gather_read = signal("gather_read", 4)
        pick2_ready = signal("pick2_ready", 1)
        pick_ready = signal("pick_ready", 1)
        gateup_done = signal("gateup_done", 2)
        gate_read = signal("gate_read", 1)
        up_read = signal("up_read", 1)
        scat_put = signal("scat_put", 8)
        scat_added = signal("scat_added", 8)
        scat_ready = signal("scat_ready", 1)
        fold_done = signal("fold_done", 1)
        silu_ready = signal("silu_ready", 1)
        hid_ready = signal("hid_ready", 1)
        down_done = signal("down_done", 4)
        hi_ready = signal("hi_ready", 4)
        y_ready = signal("y_ready", 4)
        stored = signal("stored", 0)

        w_in_v = w_in.rearrange("l (k p) n -> l p k n", p=P)
        w_out_v = w_out.rearrange("l (k p) n -> l p k n", p=P)
        w_gate_v = w_gate.rearrange("l e (k p) f -> (l e) p k f", p=P)
        w_up_v = w_up.rearrange("l e (k p) f -> (l e) p k f", p=P)
        w_down_v = w_down.rearrange("l e (f p) d -> (l e) p f d", p=P)

        def piece(n):
            return ring[:, n % RING, :].rearrange("p (k n) -> p k n", k=4)

        exp_slot = [ring[:, n, :] for n in range(RING)]
        exp_slot += [region_b[:, n * PIECE:(n + 1) * PIECE] for n in range(3)]
        exp_slot += [conv_sq[:, :], x_t[:, 0:PIECE], x_t[:, PIECE:2 * PIECE]]

        block = ctx.enter_context(nc.Block())

        @block.gpsimd
        def _(pool):
            s = Steps(pool, pool_steps, 0)

            def select(ap, op, fill, base, pattern):
                s.link(pool.affine_select(out=ap, in_=ap, compare_op=op, fill=fill, base=base,
                                          pattern=pattern, channel_multiplier=1))

            s.do(pool.memset(ident[:, :], 0.0))
            s.do(pool.memset(pairs[:, :], 0))
            s.do(pool.memset(w_rout[:, :, :], 0.0))
            for i in range(HEAD_DIM // 2):
                f = np.float32(1.0) / np.power(np.float32(ROPE_THETA), np.float32(2 * i / HEAD_DIM))
                s.do(pool.memset(inv_freq[:, i:i + 1], float(f)))
            s.sync()
            select(ident[:, :], ALU.not_equal, 1.0, 0, [[-1, P]])
            pool.sem_inc(consts.sem, 1)
            s.do(pool.memset(ones[:, :], 1.0))
            s.do(pool.memset(tri[:, :], 0.0))
            s.do(pool.memset(tri_strict[:, :], 0.0))
            s.do(pool.memset(level_mask[:, :, :], 0.0))
            s.do(pool.memset(win_mask[:, :], -1e30))
            s.do(pool.memset(pair_mask[:, :], 0.0))
            s.do(pool.memset(sum_groups[:, :], 0.0))
            s.do(pool.memset(sum_ab[:, :], 0.0))
            s.do(pool.memset(fold[:, :], 0.0))
            s.do(pool.memset(before[:, :, :], 0.0))
            s.do(pool.memset(flag_off[:, :], 0.0))
            s.do(pool.memset(pairs_f[:, :], 0.0))
            s.do(pool.memset(slot_of[:, :, :], -1.0))
            s.do(pool.memset(gate_of[:, :, :], 0.0))
            s.do(pool.memset(zero[:, :], 0.0))
            s.do(pool.memset(eps_dn[:, 0:1], float(dk * RMS_EPS)))
            s.do(pool.memset(eps_dn[:, 1:2], RMS_EPS))
            s.do(pool.memset(eps_dn[:, 2:3], LN_EPS))
            s.sync()
            select(tri[:, :], ALU.is_gt, 1.0, 0, [[-1, P]])
            select(tri_strict[:, :], ALU.is_ge, 1.0, 0, [[-1, P]])
            for a in range(4):
                select(sum_groups[:, :], ALU.not_equal, 1.0, -32 * a, [[-1, n_exp]])
                select(sum_ab[:, :], ALU.not_equal, 1.0, -32 * a - 16, [[-1, 2 * n_dn]])
            select(fold[:, :], ALU.not_equal, 1.0, 0, [[-1, SLOTS]])
            select(fold[:, :], ALU.not_equal, 1.0, -SLOTS, [[-1, SLOTS]])
            for j in (0, 2):
                own = win_mask[:, j * P:(j + 1) * P]
                s.link(pool.affine_select(out=own, in_=own, compare_op=ALU.is_gt, fill=0.0, base=0,
                                          pattern=[[1, P]], channel_multiplier=-1))
            select(win_mask[:, P:2 * P], ALU.is_ge, 0.0, 0, [[-1, P]])
            for lev in range(LEVELS):
                b = 1 << lev
                m = level_mask[:, lev, :].rearrange("p (n j i) -> p n j i", j=2, i=b)[:, :, 0, :]
                nb = P // (2 * b)
                s.link(pool.memset(m, -1.0))
                s.link(pool.affine_select(out=m, in_=m, compare_op=ALU.is_ge, fill=0.0, base=-b,
                                          pattern=[[-2 * b, nb], [0, b]], channel_multiplier=1))
                s.link(pool.affine_select(out=m, in_=m, compare_op=ALU.is_ge, fill=0.0, base=2 * b - 1,
                                          pattern=[[2 * b, nb], [0, b]], channel_multiplier=-1))
            odd = pair_mask[:, :].rearrange("p (n j) -> p n j", j=2)[:, :, 1]
            s.link(pool.affine_select(out=odd, in_=odd, compare_op=ALU.not_equal, fill=-1.0, base=0,
                                      pattern=[[-2, P // 2]], channel_multiplier=1))
            s.link(pool.affine_select(out=before[:, :, :], in_=before[:, :, :], compare_op=ALU.is_ge, fill=1.0,
                                      base=0, pattern=[[-1, EPG], [1, EPG]], channel_multiplier=0))
            for tau in range(3):
                s.do(pool.memset(flag_off[:, tau * n_exp:(tau + 1) * n_exp], float(SLOTS * (tau + 1))))
            s.link(pool.iota(iota_i[:, 0:N_FLAGS], pattern=[[0, 3], [1, n_exp]], base=0, channel_multiplier=0))
            s.link(pool.tensor_copy(flag_exp[:, :], iota_i[:, 0:N_FLAGS]))
            s.link(pool.iota(iota_i[:, 0:EXTRA], pattern=[[1, EXTRA]], base=1, channel_multiplier=0))
            s.link(pool.tensor_copy(extra_id[:, :], iota_i[:, 0:EXTRA]))
            s.link(pool.iota(iota_i[:, :], pattern=[[0, 2], [1, SLOTS]], base=0, channel_multiplier=0))
            pool.tensor_copy(slot_id[:, :], iota_i[:, :]).then_inc(consts.sem, 1)

        @block.sync
        def _(sp):
            with nc.allow_non_contiguous_dma(reason="256 positions, one for each token's partition"):
                sp.dma_start(pos_i[:, :], positions.rearrange("b (t p) -> p (b t)", p=P)).then_inc(pos_loaded.sem, 16)
            for t in range(NT):
                sp.dma_start(x_nat[:, t, :], x_in[0, t * P:(t + 1) * P, :]).then_inc(once_loaded.sem, 16)
            sp.dma_start(b_rout[:, :], router_bias.partition_broadcast(P)).then_inc(once_loaded.sem, 16)
            sp.wait_ge(consts.sem, 1)
            sp.dma_start(w_rout[:, :, 0:n_exp], router_w.rearrange("(k p) e -> p k e", p=P)).then_inc(once_loaded.sem, 16)

            def load(n, counted, src):
                sp.wait_ge(ring_free.sem, counted + (n + 1 + RING if n >= RING else n + 1 + 2 * RING - EXP_COUNTED))
                dst = piece(n)
                if src.shape[-1] != PANEL:
                    dst = dst[:, :, 0:src.shape[-1]]
                sp.dma_start(dst, src).then_inc(landed[n % RING].sem, 16)

            def expert(counted, turn, le, l=None):
                for j in range(EXP_PIECES):
                    if l is None and j < EXP_COUNTED:
                        sp.wait_ge(ring_free.sem, counted + (j + 1 + 2 * RING - EXP_COUNTED))
                    elif l is None:
                        sp.wait_ge(down_done.sem, turn * 4)
                    elif j < RING - 1:
                        sp.wait_ge(ring_free.sem, counted + (j + 2 + RING))
                    elif j == RING - 1:
                        sp.wait_ge(proj_done.sem, proj_done.at(l, 2 * (N_IN + N_OUT)))
                    elif j == RING:
                        sp.wait_ge(o_ready.sem, o_ready.at(l, 2))
                    elif j == EXP_PIECES - 2:
                        sp.wait_ge(logit_done.sem, logit_done.at(l, 1))
                    dst = exp_slot[j]
                    if j < 8:
                        w = (w_gate_v, w_up_v)[j // 4]
                        dst = dst.rearrange("p (k n) -> p k n", k=4)
                        src = w[bass.ds(le, 1), :, 4 * (j % 4):4 * (j % 4) + 4, :].rearrange("a p k f -> (a p) k f")
                    else:
                        src = w_down_v[bass.ds(le, 1), :, j - 8, :].rearrange("a p d -> (a p) d")
                    sp.dma_start(dst, src).then_inc(landed[j].sem, 16)

            with sp.Fori(0, depth) as l:
                pairs0 = sp.value_load(pairs[0:1, bass.ds(l, 1)], min_val=0, max_val=depth * TURNS // 2)
                first = sp.snap(l * (MIX_PIECES - 1) + pairs0 * (2 * EXP_COUNTED))

                def row(a):
                    return a[bass.ds(l, 1)].rearrange("a n -> (a n)").partition_broadcast(P)

                for n, (i, j) in enumerate(ORDER):
                    if i < N_IN:
                        kind, c0 = IN_PANELS[i]
                        width = 2 * kv_dim if kind == "kv" else PANEL
                        load(n, first, w_in_v[bass.ds(l, 1), :, 4 * j:4 * j + 4, c0:c0 + width]
                             .rearrange("a p k n -> (a p) k n"))
                    else:
                        c0 = (i - N_IN) * PANEL
                        load(n, first, w_out_v[bass.ds(l, 1), :, 4 * j:4 * j + 4, c0:c0 + PANEL]
                             .rearrange("a p k n -> (a p) k n"))
                    if (i, j) == (0, 3):
                        sp.wait_ge(layer_open.sem, layer_open.at(l, 4))
                        sp.sem_inc(open_seen.sem, 1)
                        sp.dma_start(w_ab[:, :, :], w_in_v[bass.ds(l, 1), :, :, off_ab - 16:off_ab + 16]
                                     .rearrange("a p k n -> (a p) k n")).then_inc(small_loaded.sem, 16)
                        sp.dma_start(taps_nat[:, :], conv_w[bass.ds(l, 1)].rearrange("a w (c p) -> (a w c) p", p=P))\
                            .then_inc(small_loaded.sem, 16)
                        for dst, src in ((sinks, attn_sinks), (a_log_b, a_log), (dt_b, dt_bias), (dn_w, dn_norm_w)):
                            sp.dma_start(dst[:, :], row(src)).then_inc(small_loaded.sem, 16)
                    if (i, j) == (N_IN + 2, 0):
                        sp.wait_ge(to_done.sem, to_done.at(l, 4))
                        sp.dma_start(ln_par[:, 0, :], row(ln1_g)).then_inc(ln1_loaded.sem, 16)
                        sp.dma_start(ln_par[:, 1, :], row(ln1_b)).then_inc(ln1_loaded.sem, 16)
                first_e = sp.snap(l * (MIX_PIECES - 1) + pairs0 * (2 * EXP_COUNTED) + (MIX_PIECES - 1))
                turns0 = sp.snap(pairs0 * 2)
                expert(first_e, turns0, l * n_exp, l)
                sp.wait_ge(ln_done.sem, ln_done.at(l, 4))
                sp.dma_start(ln_par[:, 0, :], row(ln2_g)).then_inc(ln2_loaded.sem, 16)
                sp.dma_start(ln_par[:, 1, :], row(ln2_b)).then_inc(ln2_loaded.sem, 16)
                with sp.Fori(1, n_exp) as e:
                    expert(first_e + e * EXP_COUNTED, turns0 + e, l * n_exp + e)
                sp.wait_ge(route_ready.sem, l + 1)
                sp.sem_inc(route_seen.sem, 1)
                more = sp.value_load(extra_n[0:1, bass.ds(l, 1)], min_val=0, max_val=EXTRA)
                with sp.If(more > 0):
                    with sp.Fori(0, more) as j:
                        e = sp.value_load(extra_e[0:1, bass.ds(j, 1)], min_val=0, max_val=n_exp - 1)
                        expert(first_e + (n_exp + j) * EXP_COUNTED, turns0 + (n_exp + j), l * n_exp + e)

            for t in range(NT):
                for side in range(2):
                    cols = slice(side * D // 2, (side + 1) * D // 2)
                    sp.wait_ge(layer_open.sem, layer_open.at(depth, 2 * t + side + 1))
                    sp.dma_start(out[0, t * P:(t + 1) * P, cols], x_nat[:, t, cols]).then_inc(stored.sem, 16)
            sp.wait_ge(stored.sem, 16 * 2 * NT)

        @block.tensor
        def _(pe):
            pe.wait_ge(consts.sem, 1)

            def transposes(g, src, dst):
                for j in range(4):
                    last = pe.transpose(dst[:, j * P:(j + 1) * P], src(j), ident[:, :])
                return last

            def turn_x(g, rnd, dst):
                t, c = g // 4, 4 * (g % 4)
                transposes(g, lambda j: x_nat[:, t, (c + j) * P:(c + j + 1) * P], dst).then_inc(xt_done.sem, 1)

            with pe.Fori(0, depth) as l:
                pe.wait_ge(layer_open.sem, layer_open.at(l, 1))
                pairs0 = pe.value_load(pairs[0:1, bass.ds(l, 1)], min_val=0, max_val=depth * TURNS // 2)
                uses = pe.snap(l * MIX_USES + pairs0 * 2)

                def arrived(n, before_):
                    pe.wait_ge(landed[n % RING].sem, (before_ + (n // RING + 1)) * 16)

                for g in range(8):
                    pe.wait_ge(layer_open.sem, layer_open.at(l, g // 2 + 1))
                    turn_x(g, 0, bank[XT_BANKS[0][g]])
                pe.wait_ge(xt_act.sem, xt_act.at(l, 4))
                pe.wait_ge(xt_dve.sem, xt_dve.at(l, 4))

                owed = [0]

                def k_step(i, k, tiles=(0, 1)):
                    kind = IN_PANELS[i][0] if i < N_IN else "out"
                    j, kk = k // 4, k % 4
                    n = ORDER.index((i, j))
                    if k == 0 and tiles[0] == 0:
                        if 2 <= i <= 10:
                            pe.wait_ge(proj_read.sem, proj_read.at(l, i - 1))
                        if i in (11, 12):
                            pe.wait_ge(z_read.sem, z_read.at(l, i - 10))
                        if i > 12:
                            pe.wait_ge(proj_read.sem, proj_read.at(l, i - 3))
                    if i in (11, 12) and k in (8, 12) and tiles[0] == 0:
                        pe.wait_ge(to_read.sem, to_read.at(l, k // 2 - 2))
                    if kk == 0 and tiles[0] == 0:
                        arrived(n, uses)
                    b = [bank[2 * (i % 2)], bank[2 * (i % 2) + 1]]
                    width = 2 * kv_dim if kind == "kv" else PANEL
                    w = piece(n)

                    def settle(m):
                        if kk == 0 and owed[0]:
                            m.then_inc(ring_free.sem, owed[0])
                            owed[0] = 0

                    if kind == "dn":
                        for c in range(4):
                            m = pe.matmul(b[c // 2][:, (c % 2) * T:(c % 2 + 1) * T],
                                          w[:, kk, c * P:(c + 1) * P], xT[:, k, :],
                                          start=(k == 0 and c % 2 == 0), stop=(k == KC - 1),
                                          skip_group_check=True)
                            if c == 0:
                                settle(m)
                            if k == KC - 1 and c == 1:
                                m.then_inc(proj_done.sem, 1)
                    else:
                        lhs = mixT if kind == "out" else xT
                        for t in tiles:
                            m = pe.matmul(b[t][:, 0:width], lhs[:, k, t * P:(t + 1) * P],
                                          w[:, kk, 0:width], start=(k == 0), stop=(k == KC - 1))
                            if t == 0:
                                settle(m)
                            if k == KC - 1 and t == 0:
                                m.then_inc(proj_done.sem, 1)
                    if tiles[-1] == 0:
                        return
                    if k == KC - 1:
                        m.then_inc(proj_done.sem, 1)
                        owed[0] += 1
                    elif kk == 3:
                        m.then_inc(ring_free.sem, 1)

                def last_panel():
                    i = N_IN + N_OUT - 1
                    pe.wait_ge(proj_read.sem, proj_read.at(l, i - 3))
                    for t in range(NT):
                        for k in range(KC):
                            j, kk = k // 4, k % 4
                            n = ORDER.index((i, j))
                            if t == kk == 0:
                                arrived(n, uses)
                            m = pe.matmul(bank[2 * (i % 2) + t][:, :], mixT[:, k, t * P:(t + 1) * P],
                                          piece(n)[:, kk, :], start=(k == 0), stop=(k == KC - 1))
                            if t == k == 0:
                                m.then_inc(ring_free.sem, owed[0])
                            if t == 1 and kk == 3 and j < 3:
                                m.then_inc(ring_free.sem, 1)
                        m.then_inc(proj_done.sem, 1)

                def panel(i, first=0, end=KC):
                    for k in range(first, end):
                        k_step(i, k)

                panel(0)
                pe.wait_ge(consts.sem, 2)
                panel(1)
                panel(2)
                pe.wait_ge(small_loaded.sem, small_loaded.at(l, 96))
                for k in range(KC):
                    a = k % 4
                    m = pe.matmul(bank[4][32 * a:32 * a + 32, 0:T], w_ab[:, k, :], xT[:, k, :],
                                  start=(k < 4), stop=(k >= KC - 4))
                m.then_inc(ab_part_done.sem, 1)

                for g in range(4):
                    t, c = g // 2, 4 * (g % 2)
                    pe.wait_ge(roped.sem, roped.at(l, 2))
                    if g == 1:
                        pe.wait_ge(ab_part_read.sem, ab_part_read.at(l, 1))
                        for tile in range(NT):
                            pe.matmul(bank[4][:, AB_AT + tile * 16:AB_AT + (tile + 1) * 16],
                                      ab_part[:, tile * P:(tile + 1) * P],
                                      sum_ab[:, :], start=True, stop=True)
                        pe.transpose(bank[4][:, TAPS_AT:TAPS_AT + taps_nat.shape[0]], taps_nat[:, :],
                                     ident[0:taps_nat.shape[0], 0:taps_nat.shape[0]]).then_inc(ab_done.sem, 1)
                    if g == 3:
                        pe.wait_ge(tq_read.sem, tq_read.at(l, 1))
                    transposes(g, lambda j: q_rot[:, t, (c + j) * P:(c + j + 1) * P], bank[5 + g % 3])\
                        .then_inc(tq_done.sem, 1)
                pe.wait_ge(roped.sem, roped.at(l, 3))
                pe.wait_ge(tq_read.sem, tq_read.at(l, 2))
                transposes(4, lambda j: k_rot[:, j % 2, j // 2, :, :].rearrange("p a d -> p (a d)"), bank[6])\
                    .then_inc(tq_done.sem, 1)

                panel(3)
                pe.wait_ge(tq_read.sem, tq_read.at(l, 5))
                pe.wait_ge(ab_dve.sem, ab_dve.at(l, 2))
                for h in range(n_q):
                    lo = (h % 2) * HEAD_DIM
                    kv = h // (n_q // n_kv)
                    rows = slice(lo, lo + HEAD_DIM)
                    if h >= 4:
                        pe.wait_ge(score_read.sem, score_read.at(l, h - 3))
                    b = bank[4 + h % 4]
                    pe.matmul(b[:, 0:P], q_t[rows, h // 2, 0:P], k_t[rows, kv, 0:P], start=True, stop=True)
                    pe.matmul(b[:, P:3 * P], q_t[rows, h // 2, P:T], k_t[rows, kv, :], start=True, stop=True)\
                        .then_inc(score_done.sem, 1)
                    k_step(4, h)
                panel(5)

                def square_sums(half, i, k):
                    for u in range(4):
                        n = 4 * half + u
                        if u:
                            k_step(i, k + u - 1)
                        pe.wait_ge(square_ready.sem, square_ready.at(l, n + 1))
                        if u >= 2:
                            pe.wait_ge(norm_sqrt.sem, norm_sqrt.at(l, n - 1))
                        pe.matmul(bank[4 + u % 2][:, :], ones[:, :], square[:, n % 2, :], start=True, stop=True)\
                            .then_inc(ss_done.sem, 1)

                pe.wait_ge(score_read.sem, score_read.at(l, n_q))
                panel(6, 0, 4)
                pe.wait_ge(probs_ready.sem, probs_ready.at(l, 1))
                for h in range(n_q + 2):
                    if h < n_q:
                        if h >= 2:
                            pe.wait_ge(pt_read.sem, pt_read.at(l, h - 1))
                        for j in range(3):
                            m = pe.transpose(bank[4 + h % 2][:, j * P:(j + 1) * P],
                                             probs[:, h, j * P:(j + 1) * P], ident[:, :])
                        m.then_inc(pt_done.sem, 1)
                    if h >= 2:
                        hh = h - 2
                        lo = (hh % 2) * HEAD_DIM
                        kv = hh // (n_q // n_kv)
                        vs = slice(kv * HEAD_DIM, (kv + 1) * HEAD_DIM)
                        pe.wait_ge(pt_read.sem, pt_read.at(l, hh + 1))
                        if hh >= 4 and hh % 2 == 0:
                            pe.wait_ge(pv_read.sem, pv_read.at(l, hh // 2 - 1))
                        o = bank[6 + hh // 2 % 2][lo:lo + HEAD_DIM, 0:T]
                        pt = prob_t[:, hh % 4, :]
                        pe.matmul(o[:, 0:P], v_nat[:, 0, vs], pt[:, 0:P], start=True, stop=True)
                        pe.matmul(o[:, P:T], v_nat[:, 0, vs], pt[:, P:2 * P], start=True, stop=False)
                        pe.matmul(o[:, P:T], v_nat[:, 1, vs], pt[:, 2 * P:3 * P], start=False, stop=True)\
                            .then_inc(pv_done.sem, 1)
                    if 4 + h < KC:
                        k_step(6, 4 + h)
                pe.wait_ge(pt_read.sem, pt_read.at(l, n_q))
                panel(7, 0, 2)
                square_sums(0, 7, 2)
                panel(7, 5)
                pe.wait_ge(g_ready.sem, g_ready.at(l, 1))
                pe.wait_ge(norm_sqrt.sem, norm_sqrt.at(l, 4))
                pe.wait_ge(pv_read.sem, pv_read.at(l, n_q // 2))
                for t in range(NT):
                    pe.matmul(bank[4][:, t * n_dn:(t + 1) * n_dn], tri[:, :], g_nat[:, t, :], start=True, stop=True)
                pe.matmul(bank[4][:, 2 * n_dn:3 * n_dn], ones[:, :], g_nat[:, 0, :], start=True, stop=True)\
                    .then_inc(gc_done.sem, 1)
                panel(8)
                pe.wait_ge(gc_dve.sem, gc_dve.at(l, 1))
                panel(9, 0, 6)
                square_sums(1, 9, 6)
                panel(9, 9)

                between = [[(10, k) for k in range(KC)] + [(11, k) for k in range(8)],
                           [(11, k) for k in range(8, 12)] + [(12, k) for k in range(12)]]
                left = []

                def meanwhile(n):
                    for _ in range(min(n, len(left))):
                        i, k, t = left.pop(0)
                        k_step(i, k, (t,))

                def turn_out(half):
                    for t in range(NT):
                        n = 2 * half + t
                        pe.wait_ge(dn_out.sem, dn_out.at(l, n + 1))
                        transposes(0, lambda j: o_nat[:, t, (half * HALF + j) * P:(half * HALF + j + 1) * P],
                                   bank[4 + t]).then_inc(to_done.sem, 1)

                for half in range(2):
                    q_h, k_h, v_h = (qkv_t[:, half, w] for w in range(3))
                    pe.wait_ge(normed.sem, normed.at(l, 4 * half + 4))
                    pe.wait_ge(silu_done.sem, silu_done.at(l, 6 * half + 6))
                    left += [(i, k, t) for i, k in between[half] for t in range(NT)]
                    for t in range(NT):
                        n = 2 * half + t
                        tok = slice(t * P, (t + 1) * P)
                        pe.wait_ge(spread_ready.sem, spread_ready.at(l, n + 1))
                        if t == 1 or half == 1:
                            pe.wait_ge(kv_read.sem, kv_read.at(l, n))
                        if t == 0 and half == 1:
                            pe.wait_ge(o_ready.sem, o_ready.at(l, 1))
                            pe.wait_ge(to_read.sem, to_read.at(l, 2))
                        pe.matmul(bank[4][:, :], ones[:, :], decay[:, t].rearrange("p h c -> p (h c)"),
                                  start=True, stop=True)
                        pe.matmul(bank[5][:, :], ones[:, :], l_t[:, t].rearrange("p h c -> p (h c)"),
                                  start=True, stop=True).then_inc(spread_done.sem, 1)
                        for h in range(HALF):
                            pe.matmul(bank[6][:, h * P:(h + 1) * P], k_h[:, h, tok], k_h[:, h, tok],
                                      start=True, stop=True)
                        for h in range(HALF):
                            m = pe.matmul(bank[7][:, h * P:(h + 1) * P], k_h[:, h, tok], q_h[:, h, tok],
                                          start=True, stop=True)
                        m.then_inc(pair_done.sem, 1)
                        meanwhile(4 if half == 0 else 2)
                        pe.wait_ge(pair_read.sem, pair_read.at(l, n + 1))
                        transposes(0, lambda j: k_h[:, j, tok], bank[6])
                        transposes(0, lambda j: v_h[:, j, tok], bank[7]).then_inc(kv_done.sem, 1)
                        meanwhile(2 - half)
                    pe.wait_ge(kv_read.sem, kv_read.at(l, 2 * half + 2))
                    for lev in range(LEVELS):
                        for t in range(NT):
                            n = (half * LEVELS + lev) * NT + t
                            if lev:
                                pe.wait_ge(inv_ready.sem, inv_ready.at(l, n - 1))
                            for h in range(HALF):
                                m = pe.matmul(bank[4 + 2 * t][:, h * P:(h + 1) * P], l_t[:, t, h],
                                              inv[:, t, h] if lev else ident[:, :],
                                              start=True, stop=True)
                            m.then_inc(lt_done.sem, 1)
                        meanwhile(2 - half)
                        for t in range(NT if lev else 0):
                            n = (half * LEVELS + lev) * NT + t
                            pe.wait_ge(masked_ready.sem, masked_ready.at(l, n - NT * half - 1))
                            for h in range(HALF):
                                pe.matmul(bank[5 + 2 * t][:, h * P:(h + 1) * P], inv_t[:, t, h], masked[:, t, h],
                                          start=True, stop=True)
                            for h in range(HALF):
                                m = pe.matmul(bank[4 + 2 * t][:, h * P:(h + 1) * P], masked[:, t, h],
                                              inv_t[:, t, h], start=True, stop=True)
                            m.then_inc(tlt_done.sem, 1)
                        meanwhile(2 - half)
                    assert not left or left[0][0] > 10
                    pe.wait_ge(inv_ready.sem, inv_ready.at(l, (half + 1) * LEVELS * NT))
                    for h in range(HALF):
                        pe.matmul(bank[4][:, h * P:(h + 1) * P], inv_t[:, 0, h], v_beta[:, 0, h], start=True, stop=True)
                    for h in range(HALF):
                        m = pe.matmul(bank[7][:, h * P:(h + 1) * P], k_in[:, h], inv_t[:, 1, h], start=True, stop=True)
                    m.then_inc(u0_done.sem, 1)
                    meanwhile(2)
                    pe.wait_ge(v0_ready.sem, v0_ready.at(l, half + 1))
                    for h in range(HALF):
                        pe.matmul(bank[6][:, h * P:(h + 1) * P], k_out[:, h], v_new[:, 0, h], start=True, stop=True)
                    for h in range(HALF):
                        m = pe.matmul(bank[5][:, h * P:(h + 1) * P], a_t[:, 0, h], v_new[:, 0, h], start=True, stop=True)
                    m.then_inc(s_done.sem, 1)
                    meanwhile(2)
                    pe.wait_ge(s_ready.sem, s_ready.at(l, half + 1))
                    for h in range(HALF):
                        pe.matmul(bank[4][:, h * P:(h + 1) * P], inv_t[:, 1, h], v_beta[:, 1, h], start=True, stop=False)
                        m = pe.matmul(bank[4][:, h * P:(h + 1) * P], w_t(h), state(h), start=False, stop=True)
                    m.then_inc(v1_done.sem, 1)
                    for h in range(HALF):
                        pe.matmul(bank[6][:, h * P:(h + 1) * P], q_h[:, h, P:T], state(h), start=True, stop=True)
                    meanwhile(2)
                    pe.wait_ge(v1_ready.sem, v1_ready.at(l, half + 1))
                    for h in range(HALF):
                        m = pe.matmul(bank[7][:, h * P:(h + 1) * P], a_t[:, 1, h], v_new[:, 1, h], start=True, stop=True)
                    m.then_inc(o1_done.sem, 1)

                    meanwhile(len(left))
                    if half == 1:
                        pe.wait_ge(o_ready.sem, o_ready.at(l, 2))
                    turn_out(half)
                panel(11, 12)
                panel(12, 12)
                panel(13)
                last_panel()

                for t in range(NT):
                    for g in range(4 * t, 4 * t + 4):
                        pe.wait_ge(ln_done.sem, ln_done.at(l, g // 2 + 1))
                        if g >= 6:
                            pe.wait_ge(xt_act.sem, xt_act.at(l, 4 + g - 5))
                        turn_x(g, 1, bank[XT_BANKS[1][g]])
                    pe.wait_ge(xt_act.sem, xt_act.at(l, 8 + 2 * t))
                    if t:
                        pe.wait_ge(xt_dve.sem, xt_dve.at(l, 6))
                    if t:
                        pe.wait_ge(part_read.sem, part_read.at(l, 1))
                    for k in range(KC):
                        a = k % 4
                        m = pe.matmul(bank[4][32 * a:32 * a + 32, t * P:(t + 1) * P], w_rout[:, k, :],
                                      xT[:, k, t * P:(t + 1) * P], start=(k < 4), stop=(k >= KC - 4))
                    m.then_inc(part_done.sem, 1)
                for t in range(NT):
                    pe.wait_ge(part_read.sem, part_read.at(l, t + 1))
                    m = pe.matmul(bank[5][:, 64 + t * n_exp:64 + (t + 1) * n_exp], logit_part[:, t, :],
                                  sum_groups[:, :], start=True, stop=True)
                m.then_inc(logit_done.sem, 1)
                pe.wait_ge(member_ready.sem, member_ready.at(l, 1))
                member = r[:, 4]
                pe.matmul(bank[5][:, 0:n_exp], tri_strict[:, :], member[:, 0, :], start=True, stop=True)
                pe.matmul(bank[5][:, n_exp:2 * n_exp], tri_strict[:, :], member[:, 1, :], start=True, stop=False)
                pe.matmul(bank[5][:, n_exp:2 * n_exp], ones[:, :], member[:, 0, :], start=False, stop=True)
                pe.matmul(bank[5][:, 2 * n_exp:3 * n_exp], ones[:, :], member[:, 0, :], start=True, stop=False)
                pe.matmul(bank[5][:, 2 * n_exp:3 * n_exp], ones[:, :], member[:, 1, :], start=False, stop=True)\
                    .then_inc(rank_done.sem, 1)

                def gather():
                    for b in range(4):
                        for j in range(4):
                            for t in range(NT):
                                c = 4 * b + j
                                m = pe.matmul(bank[GATHER_BANKS[b]][:, j * P:(j + 1) * P],
                                              x_nat[:, t, c * P:(c + 1) * P], pick2[:, t, :],
                                              start=(t == 0), stop=(t == NT - 1))
                        m.then_inc(gather_done.sem, 1)

                def scatter(i):
                    for n in range(8):
                        t, c = n // 4, n % 4
                        if n >= 6:
                            pe.wait_ge(scat_added.sem, scat_added.at(i + l, 1 if n == 6 else 5))
                        pe.matmul(bank[SCATTER_BANKS[n]][:, :], scat[:, t, :], y_hi[:, c * PANEL:(c + 1) * PANEL],
                                  start=True, stop=False)
                        pe.matmul(bank[SCATTER_BANKS[n]][:, :], scat[:, t, :], y_lo[:, c * PANEL:(c + 1) * PANEL],
                                  start=False, stop=True).then_inc(scat_put.sem, 1)

                pe.wait_ge(pick2_ready.sem, pairs0 + (l + 1))
                gather()
                pe.wait_ge(moe_open.sem, l + 1)
                pairs1 = pe.value_load(pairs[0:1, bass.ds(l + 1, 1)], min_val=n_exp // 2, max_val=depth * TURNS // 2)

                def expert_turn(i, q, second, last):
                    uses_e = pe.snap((l + 1) * MIX_USES + i)

                    def here(j):
                        pe.wait_ge(landed[j].sem, ((uses_e if j < RING else i) + 1) * 16)

                    slots = slice(second * SLOTS, (second + 1) * SLOTS)
                    for w in range(2):
                        for j in range(4):
                            n = 4 * w + j
                            here(n)
                            if w == second == 0:
                                pe.wait_ge(gather_read.sem, gather_read.at(q, j + 1))
                            for kk in range(4):
                                k = 4 * j + kk
                                side = k % 2
                                m = pe.matmul(bank[2 + w][side * SLOTS:(side + 1) * SLOTS, :],
                                              xg_half[k // 8][:, k % 8 * P + slots.start:k % 8 * P + slots.stop],
                                              exp_slot[n][:, kk * PANEL:(kk + 1) * PANEL], start=(k < 2), stop=(k >= KC - 2))
                                if k == 0 and w == 1:
                                    m.then_inc(ring_free.sem, 1)
                            m.then_inc(*((ring_free.sem, 1) if j < 3 else (gateup_done.sem, 1)))
                    pe.wait_ge(scat_ready.sem, i + (l + 1))
                    pe.wait_ge(pick_ready.sem, i + (l + 1))
                    for t in range(NT):
                        pe.transpose(bank[0][:, t * P:(t + 1) * P], pick[:, t, :], ident[:, :])
                    for t in range(NT):
                        pe.matmul(bank[0][:, NT * P:NT * P + 1], pick[:, t, :], gate_col[:, t:t + 1],
                                  start=(t == 0), stop=(t == NT - 1))
                    pe.wait_ge(gate_read.sem, i + 1)
                    for w, part in enumerate((gate_part, up_part)):
                        if w:
                            pe.wait_ge(up_read.sem, i + 1)
                        for f in range(FC):
                            m = pe.matmul(bank[2][:, (w * FC + f) * SLOTS:(w * FC + f + 1) * SLOTS],
                                          part[:, f * P:(f + 1) * P], fold[:, :], start=True, stop=True)
                            if w == f == 0:
                                m.then_inc(ring_free.sem, 1)
                    m.then_inc(fold_done.sem, 1)
                    pe.wait_ge(y_ready.sem, (i + (l + 1)) * 4)
                    scatter(i)
                    pe.wait_ge(hid_ready.sem, i + 1)
                    for pair in range(2):
                        for c in DOWN_ORDER:
                            if pair == 0:
                                pe.wait_ge(scat_added.sem, scat_added.at(i + l, c + 1 if c else 7))
                            for side in range(2):
                                f = 2 * pair + side
                                if c == DOWN_ORDER[0]:
                                    here(8 + f)
                                m = pe.matmul(bank[4 + c][side * SLOTS:(side + 1) * SLOTS, :], hid_t[:, f, :],
                                              exp_slot[8 + f][:, c * PANEL:(c + 1) * PANEL],
                                              start=(pair == 0), stop=(pair == 1))
                                if pair == 1 and c == DOWN_ORDER[0] and side == 0:
                                    m.then_inc(ring_free.sem, 2)
                            if pair == 1:
                                m.then_inc(down_done.sem, 1)
                    if second:
                        pe.wait_ge(scat_ready.sem, i + (l + 2))
                        pe.wait_ge(scat_added.sem, scat_added.at(i + l, 8))
                        if not last:
                            pe.wait_ge(pick2_ready.sem, q + (l + 2))
                            gather()

                last_pair = pe.value_load(last_pairs[0:1, bass.ds(l, 1)], min_val=n_exp // 2 - 1,
                                          max_val=depth * TURNS // 2)
                with pe.Fori(pairs0, last_pair) as q:
                    for second in range(2):
                        expert_turn(pe.snap(q * 2 + second), q, second, False)
                for second in range(2):
                    expert_turn(pe.snap(last_pair * 2 + second), last_pair, second, True)
                turns1 = pe.snap(pairs1 * 2)
                pe.wait_ge(scat_ready.sem, turns1 + (l + 1))
                pe.wait_ge(y_ready.sem, (turns1 + (l + 1)) * 4)
                scatter(turns1)

        @block.scalar
        def _(act):
            act.wait_ge(consts.sem, 1)
            act.wait_ge(rope_dve.sem, 1)
            act.activation(sin_t[:, :, :], ang[:, 1], ACT.Sin).then_inc(rope_act.sem, 1)
            act.activation(cos_t[:, :, :], ang[:, 2], ACT.Sin).then_inc(rope_act.sem, 1)

            with act.Fori(0, depth) as l:
                act.wait_ge(layer_open.sem, layer_open.at(l, 4))
                s = Steps(act, act_steps, l)

                def read_x(g, rnd, src):
                    t, c = g // 4, 4 * (g % 4)
                    act.wait_ge(xt_done.sem, xt_done.at(l, 8 * rnd + g + 1))
                    act.activation(xT[:, c:c + 4, t * P:(t + 1) * P],
                                   src[:, :].rearrange("p (c t) -> p c t", c=4), ACT.Copy).then_inc(xt_act.sem, 1)

                for g in range(0, 8, 2):
                    read_x(g, 0, bank[XT_BANKS[0][g]])
                act.wait_ge(consts.sem, 2)
                act.wait_ge(ab_part_done.sem, ab_part_done.at(l, 1))
                act.activation(ab_part, bank[4][:, 0:T], ACT.Copy).then_inc(ab_part_read.sem, 1)
                act.wait_ge(ab_dve.sem, ab_dve.at(l, 1))
                act.activation(gates[:, 1], gates[:, 0], ACT.Exp, scale=-1.0).then_inc(ab_act.sem, 1)
                s.do(act.activation(gates[:, 7, 0], a_log_b[:, :], ACT.Exp))
                act.activation(gates[:, 8], gates[:, 9], ACT.Exp, scale=-1.0).then_inc(ab_act.sem, 1)
                act.wait_ge(ab_dve.sem, ab_dve.at(l, 2))
                act.activation(gates[:, 3], gates[:, 2], ACT.Ln).then_inc(ab_act.sem, 1)
                for g in range(4):
                    t, c = g // 2, 4 * (g % 2)
                    act.wait_ge(tq_done.sem, tq_done.at(l, g + 1))
                    act.activation(q_t[:, c:c + 4, t * P:(t + 1) * P],
                                   bank[5 + g % 3][:, :].rearrange("p (c t) -> p c t", c=4), ACT.Copy)\
                        .then_inc(tq_read.sem, 1)
                act.wait_ge(tq_done.sem, tq_done.at(l, 5))
                act.activation(k_t[:, :, :].rearrange("p v t -> p (v t)"), bank[6][:, :], ACT.Copy)\
                    .then_inc(tq_read.sem, 1)

                def silu(n):
                    p, b = n // 2, n % 2
                    half, w = p // 3, p % 3
                    act.wait_ge(conv_ready.sem, conv_ready.at(l, n + 1))
                    act.activation(qkv_t[:, half, w, 2 * b:2 * b + 2, :].rearrange("p h t -> p (h t)"),
                                   conv_y[:, n % 2, :], ACT.Silu).then_inc(silu_done.sem, 1)

                def norms(half):
                    act.wait_ge(silu_done.sem, silu_done.at(l, 6 * half + 6))
                    for u in range(6):
                        n = 4 * half + u
                        if u < 4:
                            w, b = u // 2, u % 2
                            if n >= 2:
                                act.wait_ge(ss_done.sem, ss_done.at(l, n - 1))
                            act.activation(square[:, n % 2, :],
                                           qkv_t[:, half, w, 2 * b:2 * b + 2, :].rearrange("p h t -> p (h t)"),
                                           ACT.Square).then_inc(square_ready.sem, 1)
                        if u >= 2:
                            n = 4 * half + u - 2
                            w = (u - 2) // 2
                            act.wait_ge(ss_done.sem, ss_done.at(l, n + 1))
                            if n >= 2:
                                act.wait_ge(normed.sem, normed.at(l, n - 1))
                            act.activation(rot_ab[n % 2], bank[4 + n % 2][:, :], ACT.Sqrt,
                                           bias=eps_dn[:, w:w + 1], scale=float(dk) if w == 0 else 1.0)\
                                .then_inc(norm_sqrt.sem, 1)

                rot_ab = [rot_a[:, :], rot_b[:, :]]
                silu(0)
                silu(1)
                act.wait_ge(max_ready.sem, max_ready.at(l, 1))
                for h in range(n_q):
                    act.activation(probs[:, h, 0:P], probs[:, h, 0:P], ACT.Exp, bias=mx[:, 0, h:h + 1],
                                   accum_out=row_sum[:, 0, h:h + 1])
                    act.activation(probs[:, h, P:3 * P], probs[:, h, P:3 * P], ACT.Exp, bias=mx[:, 1, h:h + 1],
                                   accum_out=row_sum[:, 1, h:h + 1])
                act.activation(sink_e[:, :, :], sink_e[:, :, :], ACT.Exp).then_inc(exp_done.sem, 1)
                for n in range(2, 6):
                    silu(n)
                for h in range(n_q):
                    act.wait_ge(pt_done.sem, pt_done.at(l, h + 1))
                    if h >= 4:
                        act.wait_ge(pv_done.sem, pv_done.at(l, h - 3))
                    act.activation(prob_t[:, h % 4, :], bank[4 + h % 2][:, 0:3 * P], ACT.Copy)\
                        .then_inc(pt_read.sem, 1)
                norms(0)
                silu(6)
                silu(7)
                silu(8)
                silu(9)
                act.wait_ge(gc_dve.sem, gc_dve.at(l, 1))
                act.activation(gfac[:, 0:2, :], gfac[:, 0:2, :], ACT.Exp).then_inc(gc_act.sem, 1)
                silu(10)
                silu(11)
                norms(1)

                def silu_z(i):
                    for t in range(NT):
                        act.wait_ge(proj_done.sem, proj_done.at(l, 2 * (9 + i) + t + 1))
                        z = act.activation(z_act[:, t, i * PANEL:(i + 1) * PANEL], bank[2 * ((9 + i) % 2) + t][:, :],
                                           ACT.Silu)
                    z.then_inc(z_read.sem, 1)

                def rms_root(half, t):
                    act.wait_ge(rms_arg.sem, rms_arg.at(l, 2 * half + t + 1))
                    act.activation(rms[:, 1], rms[:, 0], ACT.Sqrt, bias=eps_dn[:, 1:2], scale=1.0 / dk)\
                        .then_inc(rms_sqrt.sem, 1)

                silu_z(0)
                for half in range(2):
                    for t in range(NT):
                        n = 2 * half + t
                        act.wait_ge(decay_arg.sem, decay_arg.at(l, n + 1))
                        d = decay[:, t].rearrange("p h c -> p (h c)")
                        act.activation(d, d, ACT.Exp).then_inc(decay_exp.sem, 1)
                    if half == 0:
                        silu_z(1)
                    act.wait_ge(u0_done.sem, u0_done.at(l, half + 1))
                    s.do(act.activation(prob_t[:, 0:2, 0:2 * P], bank[7][:, :].rearrange("p (a c) -> p a c", a=2), ACT.Copy))
                    act.activation(v_new[:, 0].rearrange("p h c -> p (h c)"), bank[4][:, :], ACT.Copy)\
                        .then_inc(v0_ready.sem, 1)
                    act.wait_ge(s_done.sem, s_done.at(l, half + 1))
                    s.do(act.activation(o_nat[:, 0, half * PANEL:(half + 1) * PANEL], bank[5][:, :], ACT.Copy))
                    act.activation(prob_t[:, 2:4, 0:2 * P], bank[6][:, :].rearrange("p (a c) -> p a c", a=2), ACT.Copy)\
                        .then_inc(s_ready.sem, 1)
                    rms_root(half, 0)
                    act.wait_ge(v1_done.sem, v1_done.at(l, half + 1))
                    act.activation(v_new[:, 1].rearrange("p h c -> p (h c)"), bank[4][:, :], ACT.Copy)\
                        .then_inc(v1_ready.sem, 1)
                    rms_root(half, 1)
                    for t in range(NT):
                        act.wait_ge(to_done.sem, to_done.at(l, 2 * half + t + 1))
                        c = q_dim // P + half * HALF
                        act.activation(mixT[:, c:c + HALF, t * P:(t + 1) * P],
                                       bank[4 + t][:, :].rearrange("p (c t) -> p c t", c=4), ACT.Copy)\
                            .then_inc(to_read.sem, 1)

                def deviations(rnd):
                    for t in range(NT):
                        n = 2 * rnd + t
                        act.wait_ge(var_ready.sem, var_ready.at(l, n + 1))
                        act.activation(ln_s[:, 0, t:t + 1], mean_var[:, t, 1:2], ACT.Sqrt, bias=eps_dn[:, 2:3])\
                            .then_inc(ln_sqrt.sem, 1)

                deviations(0)
                for g in (0, 1, 2, 3, 4, 6):
                    read_x(g, 1, bank[XT_BANKS[1][g]])
                    if g in (3, 6):
                        if g == 6:
                            act.activation(exp_zero[:, :], zero[:, :], ACT.Exp)
                        act.wait_ge(part_done.sem, part_done.at(l, g // 4 + 1))
                        act.activation(logit_part[:, g // 4, :], bank[4][:, g // 4 * P:(g // 4 + 1) * P], ACT.Copy)\
                            .then_inc(part_read.sem, 1)
                act.wait_ge(logit_done.sem, logit_done.at(l, 1))
                act.activation(r[:, 0].rearrange("p t e -> p (t e)"), bank[5][:, 64:64 + NT * n_exp],
                               ACT.Exp, scale=-1.0)\
                    .then_inc(logit_exp.sem, 1)
                act.activation(scat_rows[:, :], zero[:, 0:1].to_broadcast([P, NT * P]), ACT.Copy)\
                    .then_inc(scat_ready.sem, 1)
                act.activation(y_hi[:, :], zero[:, 0:1].to_broadcast([P, D]), ACT.Copy)
                act.activation(y_lo[:, :], zero[:, 0:1].to_broadcast([P, D]), ACT.Copy).then_inc(y_ready.sem, 4)
                for t in range(NT):
                    m = act.activation(acc[:, t, :], x_nat[:, t, :], ACT.Copy, scale=ALPHA)
                m.then_inc(acc_ready.sem, 1)

                pairs0 = act.value_load(pairs[0:1, bass.ds(l, 1)], min_val=0, max_val=depth * TURNS // 2)

                def gather_out(n):
                    for b in range(4):
                        act.wait_ge(gather_done.sem, gather_done.at(n, b + 1))
                        act.activation(xg_half[b // 2][:, b % 2 * PANEL:(b % 2 + 1) * PANEL],
                                       bank[GATHER_BANKS[b]][:, :], ACT.Copy).then_inc(gather_read.sem, 1)

                gather_out(pairs0)
                act.wait_ge(moe_open.sem, l + 1)
                pairs1 = act.value_load(pairs[0:1, bass.ds(l + 1, 1)], min_val=n_exp // 2, max_val=depth * TURNS // 2)

                def expert_turn(i, q, second, last):
                    act.wait_ge(gateup_done.sem, i * 2 + 1)
                    act.activation(gate_part, bank[2][:, :], ACT.Copy).then_inc(gate_read.sem, 1)
                    act.wait_ge(fold_done.sem, i + 1)
                    act.activation(act_t, bank[2][:, 0:FC * SLOTS], ACT.Silu).then_inc(silu_ready.sem, 1)
                    act.wait_ge(scat_put.sem, scat_put.at(i + l, 8))
                    act.activation(slot_gate[:, :], bank[0][:, NT * P:NT * P + 1], ACT.Copy)
                    act.activation(scat_rows[:, :], bank[0][:, 0:NT * P], ACT.Copy).then_inc(scat_ready.sem, 1)
                    act.wait_ge(scat_ready.sem, i + (l + 2))
                    for n, c in enumerate(DOWN_ORDER):
                        act.wait_ge(down_done.sem, i * 4 + (n + 1))
                        act.activation(y_hi[:, c * PANEL:(c + 1) * PANEL], bank[4 + c][:, :], ACT.Copy,
                                       scale=slot_gate[:, 0:1]).then_inc(hi_ready.sem, 1)
                    if second and not last:
                        gather_out(q + 1)

                last_pair = act.value_load(last_pairs[0:1, bass.ds(l, 1)], min_val=n_exp // 2 - 1,
                                           max_val=depth * TURNS // 2)
                with act.Fori(pairs0, last_pair) as q:
                    for second in range(2):
                        expert_turn(act.snap(q * 2 + second), q, second, False)
                for second in range(2):
                    expert_turn(act.snap(last_pair * 2 + second), last_pair, second, True)
                deviations(1)
                s.close()

        @block.vector
        def _(dve):
            tt, ts, stt = dve.tensor_tensor, dve.tensor_scalar, dve.scalar_tensor_tensor
            s = Steps(dve, dve_setup, 0)
            dve.wait_ge(consts.sem, 1)
            dve.wait_ge(pos_loaded.sem, 16)
            s.link(dve.tensor_copy(pos_f[:, :], pos_i[:, :]))
            for t in range(NT):
                s.link(ts(ang[:, 0, t, :], inv_freq[:, :], pos_f[:, t:t + 1], None, ALU.mult))
            big = 1.5 * 2.0 ** 23
            parts = (6.28125, 1.93500518798828125e-3, 3.0199159819e-07)
            for j, shift in ((1, 0.0), (2, 0.25)):
                s.link(ts(ang[:, 3], ang[:, 0], 1.0 / (2.0 * np.pi), shift, ALU.mult, ALU.add))
                s.link(ts(ang[:, 3], ang[:, 3], big, -big, ALU.add, ALU.add))
                src = ang[:, 0]
                for part in parts:
                    s.link(stt(out=ang[:, j], in0=ang[:, 3], scalar=-part, in1=src, op0=ALU.mult, op1=ALU.add))
                    src = ang[:, j]
                if j == 2:
                    s.link(ts(ang[:, j], ang[:, j], float(np.pi / 2), None, ALU.add))
                s.link(ts(ang[:, j], ang[:, j], SIN_LIMIT, -SIN_LIMIT, ALU.min, ALU.max))
            dve.sem_inc(rope_dve.sem, 1)
            dve.wait_ge(rope_act.sem, 2)
            dve.sem_inc(ring_free.sem, 2 * RING)
            dve.wait_ge(once_loaded.sem, 16 * 4)
            dve.sem_inc(layer_open.sem, 4)

            with dve.Fori(0, depth) as l:
                s = Steps(dve, dve_steps, l)

                def read_x(g, rnd, src):
                    t, c = g // 4, 4 * (g % 4)
                    dve.wait_ge(xt_done.sem, xt_done.at(l, 8 * rnd + g + 1))
                    dve.tensor_copy(xT[:, c:c + 4, t * P:(t + 1) * P],
                                    src[:, :].rearrange("p (c t) -> p c t", c=4)).then_inc(xt_dve.sem, 1)

                for g in range(1, 8, 2):
                    read_x(g, 0, bank[XT_BANKS[0][g]])
                dve.wait_ge(consts.sem, 2)

                def rope(ps, t, heads, out_ap):
                    v = ps.rearrange("p (h r d) -> p h r d", h=heads, r=2)
                    n = heads * HEAD_DIM
                    a = rot_a[:, 0:n].rearrange("p (h d) -> p h d", h=2 * heads)
                    b = rot_b[:, 0:n].rearrange("p (h d) -> p h d", h=2 * heads)
                    src = ps.rearrange("p (h d) -> p h d", h=2 * heads)
                    s.do(tt(a, src, bc(cos_t[:, t, :], 1, 2 * heads), ALU.mult))
                    s.do(tt(b, src, bc(sin_t[:, t, :], 1, 2 * heads), ALU.mult))
                    s.sync()
                    a2 = rot_a[:, 0:n].rearrange("p (h r d) -> p h r d", h=heads, r=2)
                    b2 = rot_b[:, 0:n].rearrange("p (h r d) -> p h r d", h=heads, r=2)
                    return [(tt, out_ap(0), a2[:, :, 0, :], b2[:, :, 1, :], ALU.subtract),
                            (tt, out_ap(1), a2[:, :, 1, :], b2[:, :, 0, :], ALU.add)]

                for i in range(2):
                    for t in range(NT):
                        dve.wait_ge(proj_done.sem, proj_done.at(l, 2 * i + t + 1))
                        o = q_rot[:, t, i * PANEL:(i + 1) * PANEL].rearrange("p (h r d) -> p h r d", h=8, r=2)
                        ops = rope(bank[2 * i + t][:, :], t, 8, lambda half: o[:, :, half, :])
                        for f, *args in ops:
                            s.do(f(*args))
                        s.sync()
                    dve.sem_inc(proj_read.sem, 1)
                    dve.sem_inc(roped.sem, 1)
                for t in range(NT):
                    dve.wait_ge(proj_done.sem, proj_done.at(l, 4 + t + 1))
                    for dup in range(2):
                        ops = rope(bank[t][:, 0:kv_dim], t, n_kv,
                                   lambda half: k_rot[:, t, :, dup, half * 32:(half + 1) * 32])
                        for f, *args in ops:
                            s.do(f(*args))
                        s.sync()
                    s.do(dve.tensor_copy(v_nat[:, t, :], bank[t][:, kv_dim:2 * kv_dim]))
                s.sync()
                dve.sem_inc(proj_read.sem, 1)
                dve.sem_inc(roped.sem, 1)

                dve.wait_ge(ab_done.sem, ab_done.at(l, 1))
                dve.wait_ge(small_loaded.sem, small_loaded.at(l, 96))
                ab = bank[4][:, AB_AT:AB_AT + 4 * n_dn].rearrange("p (t w h) -> p t w h", t=NT, w=2)
                s.do(tt(gates[:, 4], ab[:, :, 0, :], bc(dt_b[:, :], 1, NT), ALU.add))
                s.do(dve.tensor_copy(gates[:, 9], ab[:, :, 1, :]))
                s.do(dve.tensor_copy(taps[:, :], bank[4][:, TAPS_AT:TAPS_AT + taps_nat.shape[0]]))
                s.sync()
                stt(out=gates[:, 0], in0=gates[:, 4], scalar=-1.0, in1=gates[:, 4], op0=ALU.mult, op1=ALU.max)\
                    .then_inc(ab_dve.sem, 1)
                dve.wait_ge(ab_act.sem, ab_act.at(l, 1))
                s.do(ts(gates[:, 5], gates[:, 4], 0.0, None, ALU.max))
                ts(gates[:, 2], gates[:, 1], 1.0, None, ALU.add).then_inc(ab_dve.sem, 1)
                dve.wait_ge(ab_act.sem, ab_act.at(l, 3))
                s.do(ts(gates[:, 8], gates[:, 8], 1.0, None, ALU.add))
                s.do(ts(gates[:, 2], gates[:, 2], -1.0, None, ALU.add))
                s.do(tt(gates[:, 3], gates[:, 3], gates[:, 1], ALU.mult))
                s.sync()
                s.link(ts(gates[:, 6], gates[:, 2], 0.0, None, ALU.is_equal))
                s.do(dve.reciprocal(beta[:, :, :], gates[:, 8]))
                s.do(tt(gates[:, 2], gates[:, 2], gates[:, 6], ALU.add))
                s.do(tt(gates[:, 6], gates[:, 6], gates[:, 1], ALU.mult))
                s.sync()
                s.do(tt(gates[:, 3], gates[:, 3], gates[:, 6], ALU.add))
                s.do(dve.reciprocal(gates[:, 2], gates[:, 2]))
                s.sync()
                s.link(tt(gates[:, 3], gates[:, 3], gates[:, 2], ALU.mult))
                s.link(tt(gates[:, 3], gates[:, 3], gates[:, 5], ALU.add))
                s.link(tt(gates[:, 3], gates[:, 3], bc(gates[:, 7, 0, :], 1, NT), ALU.mult))
                ts(g_nat[:, :, :], gates[:, 3], -1.0, None, ALU.mult).then_inc(g_ready.sem, 1)

                def conv(p):
                    half, w = p // 3, p % 3
                    i = 3 + p
                    for b in range(2):
                        n = 2 * p + b
                        dve.wait_ge(proj_done.sem, proj_done.at(l, 2 * i + b + 1))
                        if n >= 2:
                            dve.wait_ge(silu_done.sem, silu_done.at(l, n - 1))
                        chunk = w * n_dn + half * HALF + 2 * b
                        ps = bank[2 * (i % 2) + b]
                        for tap in range(4):
                            back = 3 - tap
                            for c in range(2):
                                w_c = taps[:, tap * 3 * n_dn + chunk + c:tap * 3 * n_dn + chunk + c + 1]
                                o = conv_y[:, n % 2, c * T:(c + 1) * T]
                                src = ps[:, c * T:(c + 1) * T]
                                if tap == 0:
                                    w_c = taps[:, 3 * 3 * n_dn + chunk + c:3 * 3 * n_dn + chunk + c + 1]
                                    s.do(ts(o, src, w_c, None, ALU.mult))
                                else:
                                    back = tap
                                    w_c = taps[:, (3 - tap) * 3 * n_dn + chunk + c:(3 - tap) * 3 * n_dn + chunk + c + 1]
                                    s.do(stt(out=o[:, back:T], in0=src[:, 0:T - back], scalar=w_c,
                                             in1=o[:, back:T], op0=ALU.mult, op1=ALU.add))
                            s.sync()
                        dve.sem_inc(conv_ready.sem, 1)
                    dve.sem_inc(proj_read.sem, 1)

                def normalise(half):
                    for u in range(4):
                        n = 4 * half + u
                        w, b = u // 2, u % 2
                        dve.wait_ge(norm_sqrt.sem, norm_sqrt.at(l, n + 1))
                        ra = (rot_a, rot_b)[n % 2]
                        s.link(dve.reciprocal(ra[:, :], ra[:, :]))
                        v = qkv_t[:, half, w, 2 * b:2 * b + 2, :].rearrange("p h t -> p (h t)")
                        tt(v, v, ra[:, :], ALU.mult).then_inc(normed.sem, 1)

                conv(0)
                for h in range(n_q):
                    dve.wait_ge(score_done.sem, score_done.at(l, h + 1))
                    stt(out=probs[:, h, :], in0=bank[4 + h % 4][:, 0:3 * P], scalar=HEAD_DIM ** -0.5,
                        in1=win_mask[:, :], op0=ALU.mult, op1=ALU.add).then_inc(score_read.sem, 1)
                dve.wait_ge(score_read.sem, score_read.at(l, n_q))
                s.do(dve.tensor_reduce(mx[:, 0, :], probs[:, :, 0:P], AX.X, ALU.max))
                s.do(dve.tensor_reduce(mx[:, 1, :], probs[:, :, P:3 * P], AX.X, ALU.max))
                s.sync()
                s.link(tt(mx[:, :, :], mx[:, :, :], bc(sinks[:, :], 1, NT), ALU.max))
                s.do(tt(sink_e[:, :, :], bc(sinks[:, :], 1, NT), mx[:, :, :], ALU.subtract))
                ts(mx[:, :, :], mx[:, :, :], -1.0, None, ALU.mult).then_inc(max_ready.sem, 1)
                conv(1)
                dve.wait_ge(exp_done.sem, exp_done.at(l, 1))
                s.link(tt(row_sum[:, :, :], row_sum[:, :, :], sink_e[:, :, :], ALU.add))
                s.link(dve.reciprocal(row_sum[:, :, :], row_sum[:, :, :]))
                s.do(tt(probs[:, :, 0:P], probs[:, :, 0:P], bc(row_sum[:, 0, :], 2, P), ALU.mult))
                tt(probs[:, :, P:3 * P], probs[:, :, P:3 * P], bc(row_sum[:, 1, :], 2, 2 * P), ALU.mult)\
                    .then_inc(probs_ready.sem, 1)
                conv(2)
                for j in range(n_q // 2):
                    dve.wait_ge(pv_done.sem, pv_done.at(l, 2 * j + 2))
                    dve.tensor_copy(mixT[:, j, :], bank[6 + j % 2][:, 0:T]).then_inc(pv_read.sem, 1)
                conv(3)
                normalise(0)
                conv(4)
                dve.wait_ge(gc_done.sem, gc_done.at(l, 1))
                s.link(dve.tensor_copy(gc[:, :, :].rearrange("p t h -> p (t h)"), bank[4][:, 0:3 * n_dn]))
                s.do(dve.tensor_copy(gfac[:, 1, :], gc[:, 1, :]))
                tt(gfac[:, 0, :], gc[:, 2, :], gc[:, 0, :], ALU.subtract).then_inc(gc_dve.sem, 1)
                conv(5)
                dve.wait_ge(gc_act.sem, gc_act.at(l, 1))
                s.link(tt(gfac[:, 2, :], gfac[:, 1, :], beta[:, 1, :], ALU.mult))
                s.link(ts(gfac[:, 2, :], gfac[:, 2, :], -1.0, None, ALU.mult))
                normalise(1)

                def heads(ap, half):
                    return ap[:, half * HALF:(half + 1) * HALF]

                def spread(half, t):
                    s.do(tt(decay[:, t], bc(tri[:, :], 1, HALF), bc(heads(g_nat[:, t, :], half), 2, P), ALU.mult))
                    tt(l_t[:, t], bc(ident[:, :], 1, HALF), bc(heads(beta[:, t, :], half), 2, P), ALU.mult)\
                        .then_inc(spread_ready.sem, 1)

                for half in range(2):
                    if half == 0:
                        dve.wait_ge(pt_done.sem, pt_done.at(l, n_q))
                    else:
                        dve.wait_ge(o1_done.sem, o1_done.at(l, 1))
                    spread(half, 0)
                    spread(half, 1)
                    for t in range(NT):
                        n = 2 * half + t
                        dve.wait_ge(spread_done.sem, spread_done.at(l, n + 1))
                        v4 = bank[4][:, :].rearrange("p (h c) -> p h c", h=HALF)
                        s.link(tt(decay[:, t], v4, bc(heads(gc[:, t, :], half), 2, P), ALU.subtract))
                        ts(decay[:, t], decay[:, t], 0.0, None, ALU.min).then_inc(decay_arg.sem, 1)
                        dve.wait_ge(pair_done.sem, pair_done.at(l, n + 1))
                        dve.wait_ge(decay_exp.sem, decay_exp.at(l, n + 1))
                        kk = bank[6][:, :].rearrange("p (h c) -> p h c", h=HALF)
                        qk = bank[7][:, :].rearrange("p (h c) -> p h c", h=HALF)
                        bb = bank[5][:, :].rearrange("p (h c) -> p h c", h=HALF)
                        s.link(tt(l_t[:, t], kk, decay[:, t], ALU.mult))
                        s.do(tt(l_t[:, t], bb, l_t[:, t], ALU.mult))
                        s.link(tt(decay[:, t], decay[:, t], bc(tri[:, :], 1, HALF), ALU.mult))
                        tt(a_t[:, t], qk, decay[:, t], ALU.mult).then_inc(pair_read.sem, 1)
                        dve.wait_ge(kv_done.sem, kv_done.at(l, n + 1))
                        if t == 0:
                            s.do(tt(k_out[:, :, :], kk, bc(heads(gfac[:, 0, :], half), 2, P), ALU.mult))
                        else:
                            s.do(tt(k_in[:, :, :], kk, bc(heads(gfac[:, 2, :], half), 2, P), ALU.mult))
                        tt(v_beta[:, t], qk, bc(heads(beta[:, t, :], half), 2, P), ALU.mult).then_inc(kv_read.sem, 1)
                    for lev in range(LEVELS):
                        for t in range(NT):
                            n = (half * LEVELS + lev) * NT + t
                            if lev == 0:
                                s.link(tt(inv_t[:, t], l_t[:, t], bc(pair_mask[:, :], 1, HALF), ALU.mult))
                                s.do(tt(inv_t[:, t], inv_t[:, t], bc(ident[:, :], 1, HALF), ALU.add))
                            dve.wait_ge(lt_done.sem, lt_done.at(l, n + 1))
                            m = tt(masked[:, t], bank[4 + 2 * t][:, :].rearrange("p (h c) -> p h c", h=HALF),
                                   bc(level_mask[:, lev, :], 1, HALF), ALU.mult)
                            if lev == 0:
                                s.link(m)
                                tt(inv[:, t], masked[:, t], bc(ident[:, :], 1, HALF), ALU.add)\
                                    .then_inc(inv_ready.sem, 1)
                            else:
                                m.then_inc(masked_ready.sem, 1)
                        for t in range(NT if lev else 0):
                            n = (half * LEVELS + lev) * NT + t
                            dve.wait_ge(tlt_done.sem, tlt_done.at(l, n - NT * half - 1))
                            s.do(tt(inv[:, t], bank[5 + 2 * t][:, :].rearrange("p (h c) -> p h c", h=HALF),
                                    inv[:, t], ALU.add))
                            tt(inv_t[:, t], bank[4 + 2 * t][:, :].rearrange("p (h c) -> p h c", h=HALF),
                               inv_t[:, t], ALU.add).then_inc(inv_ready.sem, 1)
                    if half == 0:
                        dve.wait_ge(z_read.sem, z_read.at(l, 2))
                        for t in range(NT):
                            zz = z_act[:, t, :].rearrange("p (h c) -> p h c", h=n_dn)
                            s.do(tt(zz, zz, bc(dn_w[:, :], 1, n_dn), ALU.mult))
                    o = o_nat[:, :, half * PANEL:(half + 1) * PANEL].rearrange("p t (h c) -> p t h c", h=HALF)

                    def head_norm(t):
                        n = 2 * half + t
                        sq = decay[:, t]
                        s.link(tt(sq, o[:, t], o[:, t], ALU.mult))
                        dve.tensor_reduce(rms[:, 0], sq, AX.X, ALU.add).then_inc(rms_arg.sem, 1)
                        dve.wait_ge(rms_sqrt.sem, rms_sqrt.at(l, n + 1))
                        s.link(dve.reciprocal(rms[:, 2], rms[:, 1]))
                        s.link(tt(o[:, t], o[:, t], bc(rms[:, 2], 2, P), ALU.mult))
                        zz = z_act[:, t, half * PANEL:(half + 1) * PANEL].rearrange("p (h c) -> p h c", h=HALF)
                        tt(o[:, t], o[:, t], zz, ALU.mult).then_inc(dn_out.sem, 1)

                    dve.wait_ge(s_ready.sem, s_ready.at(l, half + 1))
                    head_norm(0)
                    dve.wait_ge(o1_done.sem, o1_done.at(l, half + 1))
                    s.link(tt(o[:, 1], bank[6][:, :].rearrange("p (h c) -> p h c", h=HALF),
                              bc(heads(gfac[:, 1, :], half), 2, P), ALU.mult))
                    tt(o[:, 1], bank[7][:, :].rearrange("p (h c) -> p h c", h=HALF), o[:, 1], ALU.add)\
                        .then_inc(o_ready.sem, 1)
                    dve.wait_ge(o_ready.sem, o_ready.at(l, half + 1))
                    head_norm(1)

                def statistics(t, c, src):
                    s.do(dve.bn_stats(stats[:, t, c, :], src[:, t, c * PANEL:(c + 1) * PANEL]))

                def add_panel(i, t):
                    dve.wait_ge(proj_done.sem, proj_done.at(l, 2 * (N_IN + i) + t + 1))
                    xs = x_nat[:, t, i * PANEL:(i + 1) * PANEL]
                    s.do(stt(out=xs, in0=xs, scalar=ALPHA, in1=bank[2 * ((N_IN + i) % 2) + t][:, :],
                             op0=ALU.mult, op1=ALU.add))

                def layer_norm(rnd, t, src, loaded, signal_to):
                    s.sync()
                    s.do(dve.memset(ln_s[:, :, t], 0.0))
                    dve.bn_aggr(mean_var[:, t, :], stats[:, t, :, :]).then_inc(var_ready.sem, 1)
                    dve.wait_ge(var_ready.sem, var_ready.at(l, 2 * rnd + t + 1))
                    dve.wait_ge(loaded.sem, loaded.at(l, 32))
                    s.do(stt(out=x_nat[:, t, :], in0=src[:, t, :], scalar=mean_var[:, t, 0:1], in1=ln_par[:, 0, :],
                             op0=ALU.subtract, op1=ALU.mult))
                    dve.wait_ge(ln_sqrt.sem, ln_sqrt.at(l, 2 * rnd + t + 1))
                    s.link(dve.reciprocal(ln_s[:, 1, t:t + 1], ln_s[:, 0, t:t + 1]))
                    for side in range(2):
                        cols = slice(side * D // 2, (side + 1) * D // 2)
                        stt(out=x_nat[:, t, cols], in0=x_nat[:, t, cols], scalar=ln_s[:, 1, t:t + 1],
                            in1=ln_par[:, 1, cols], op0=ALU.mult, op1=ALU.add).then_inc(signal_to.sem, 1)

                for i in range(N_OUT - 1):
                    for t in range(NT):
                        add_panel(i, t)
                    s.sync()
                    dve.sem_inc(proj_read.sem, 1)
                    for t in range(NT):
                        statistics(t, i, x_nat)
                for t in range(NT):
                    add_panel(N_OUT - 1, t)
                    s.sync()
                    statistics(t, N_OUT - 1, x_nat)
                    layer_norm(0, t, x_nat, ln1_loaded, ln_done)
                dve.sem_inc(proj_read.sem, 1)
                for g in (5, 7):
                    read_x(g, 1, bank[XT_BANKS[1][g]])

                score, sel, rank, top, member, wsel = (r[:, i] for i in range(6))
                gate = r[:, 6]
                dve.wait_ge(logit_exp.sem, logit_exp.at(l, 1))
                s.link(ts(r[:, 0], r[:, 0], 1.0, None, ALU.add))
                s.link(dve.reciprocal(r[:, 0], r[:, 0]))
                s.link(tt(sel, score, bc(b_rout[:, :], 1, NT), ALU.add))
                tg = NT * N_GROUPS

                def ranks(values, n, m, out_ap):
                    mine, other = bc(values, 3, m), bc(values, 2, m)
                    ca, cb = cmp_a[:, 0:n], cmp_b[:, 0:n]
                    s.do(tt(ca, other, mine, ALU.is_gt))
                    s.link(tt(cb, other, mine, ALU.is_equal))
                    s.link(tt(cb, cb, bc(before[:, :, :], 1, n), ALU.mult))
                    s.link(tt(ca, ca, cb, ALU.add))
                    s.link(dve.tensor_reduce(out_ap, ca, AX.X, ALU.add))

                def grouped(ap):
                    return ap.rearrange("p t (g e) -> p (t g) e", e=EPG)

                ranks(grouped(sel), tg, EPG, grouped(rank))
                s.link(ts(top, rank, 1.5, None, ALU.is_lt))
                s.link(tt(wsel, top, sel, ALU.mult))
                s.link(dve.tensor_reduce(gr[:, 0].rearrange("p t g -> p (t g)"), grouped(wsel), AX.X, ALU.add))
                ranks(gr[:, 0], NT, N_GROUPS, gr[:, 1])
                s.link(ts(gr[:, 2], gr[:, 1], 0.5, None, ALU.is_lt))
                tt(grouped(member), grouped(top), bc(gr[:, 2].rearrange("p t g -> p (t g)"), 2, EPG), ALU.mult)\
                    .then_inc(member_ready.sem, 1)
                dve.wait_ge(member_ready.sem, member_ready.at(l, 1))
                s.link(tt(wsel, member, score, ALU.mult))
                s.link(dve.tensor_reduce(gr[:, 0, :, 0], wsel, AX.X, ALU.add))
                s.link(dve.reciprocal(gr[:, 0, :, 1], gr[:, 0, :, 0]))
                s.link(tt(gate, wsel, bc(gr[:, 0, :, 1], 2, n_exp), ALU.mult))
                dve.wait_ge(rank_done.sem, rank_done.at(l, 1))
                slot1 = r[:, 7]
                pos = bank[5][:, 0:2 * n_exp].rearrange("p (t e) -> p t e", t=NT)
                s.link(ts(slot1, pos, 1.0, None, ALU.add))
                s.link(tt(slot1, slot1, member, ALU.mult))
                s.do(ts(slot_of[:, :, 0:n_exp], slot1, -1.0, None, ALU.add))
                s.do(dve.tensor_copy(gate_of[:, :, 0:n_exp], gate))
                s.sync()

                def pick_tokens(col):
                    dve.tensor_copy(gate_col[:, :], gate_of[:, :, bass.ds(col, 1)].rearrange("p t a -> p (t a)"))
                    for t in range(NT):
                        m = ts(pick[:, t, :], slot_id[:, :], slot_of[:, t, bass.ds(col, 1)], None, ALU.is_equal)
                    return m

                def pick_pair(col):
                    return tt(pick2[:, :, :].rearrange("p t (a s) -> p t a s", a=2),
                              bc(slot_id[:, :].rearrange("p (a s) -> p a s", a=2), 1, NT),
                              bc(slot_of[:, :, bass.ds(col, 2)], 3, SLOTS), ALU.is_equal)

                pick_pair(0).then_inc(pick2_ready.sem, 1)
                pick_tokens(0).then_inc(pick_ready.sem, 1)
                for tau in range(3):
                    s.do(ts(flags[:, tau * n_exp:(tau + 1) * n_exp], bank[5][:, 2 * n_exp:3 * n_exp],
                            SLOTS * (tau + 1) + 0.5, None, ALU.is_gt))
                s.sync()
                s.link(dve.tensor_copy(cum[:, 0, :], flags[:, :]))
                side, step = 0, 1
                while step < N_FLAGS:
                    s.do(dve.tensor_copy(cum[:, 1 - side, 0:step], cum[:, side, 0:step]))
                    s.link(tt(cum[:, 1 - side, step:], cum[:, side, step:], cum[:, side, 0:N_FLAGS - step], ALU.add))
                    side, step = 1 - side, 2 * step
                s.link(ts(ext[:, 2, 0:EXTRA // 2], extra_id[:, ::2], cum[:, side, N_FLAGS - 1:N_FLAGS], None,
                          ALU.is_le))
                s.link(dve.tensor_reduce(ext[:, 2, EXTRA - 1:EXTRA], ext[:, 2, 0:EXTRA // 2], AX.X, ALU.add))
                s.do(ts(extra_n[:, bass.ds(l, 1)], ext[:, 2, EXTRA - 1:EXTRA], 2.0, None, ALU.mult))
                n_pairs_f = ext[:, 2, EXTRA - 1:EXTRA]
                s.link(ts(pair_n[:, :], n_pairs_f, float(n_exp // 2), None, ALU.add))
                s.link(ts(ext[:, 2, 0:1], n_pairs_f, pairs_f[:, 0:1], float(n_exp // 2), ALU.add, ALU.add))
                s.do(dve.tensor_copy(pairs_f[:, 0:1], ext[:, 2, 0:1]))
                s.do(ts(last_pairs[:, bass.ds(l, 1)], ext[:, 2, 0:1], -1.0, None, ALU.add))
                s.link(dve.tensor_copy(pairs[:, bass.ds(l + 1, 1)], ext[:, 2, 0:1]))
                dve.sem_inc(moe_open.sem, 1)
                s.link(tt(hot[:, :, :], bc(cum[:, side, :], 1, EXTRA), bc(extra_id[:, :], 2, N_FLAGS), ALU.is_equal))
                s.link(tt(hot[:, :, :], hot[:, :, :], bc(flags[:, :], 1, EXTRA), ALU.mult))
                s.link(tt(hot_w[:, :, :], hot[:, :, :], bc(flag_exp[:, :], 1, EXTRA), ALU.mult))
                s.link(dve.tensor_reduce(ext[:, 0, :], hot_w[:, :, :], AX.X, ALU.add))
                s.link(tt(hot_w[:, :, :], hot[:, :, :], bc(flag_off[:, :], 1, EXTRA), ALU.mult))
                s.link(dve.tensor_reduce(ext[:, 1, :], hot_w[:, :, :], AX.X, ALU.add))
                s.do(dve.tensor_copy(extra_e[:, :], ext[:, 0, :]))
                s.link(tt(hot_e[:, :, :], hot[:, :, 0:n_exp], hot[:, :, n_exp:2 * n_exp], ALU.add))
                s.link(tt(hot_e[:, :, :], hot_e[:, :, :], hot[:, :, 2 * n_exp:3 * n_exp], ALU.add))
                for t in range(NT):
                    h1 = hot_w[:, :, 0:n_exp]
                    s.link(tt(h1, hot_e[:, :, :], bc(slot1[:, t, :], 1, EXTRA), ALU.mult))
                    s.link(dve.tensor_reduce(slot_of[:, t, n_exp:TURNS], h1, AX.X, ALU.add))
                    s.link(tt(h1, hot_e[:, :, :], bc(gate[:, t, :], 1, EXTRA), ALU.mult))
                    s.link(dve.tensor_reduce(gate_of[:, t, n_exp:TURNS], h1, AX.X, ALU.add))
                    s.link(tt(slot_of[:, t, n_exp:TURNS], slot_of[:, t, n_exp:TURNS], ext[:, 1, :], ALU.subtract))
                    s.link(ts(slot_of[:, t, n_exp:TURNS], slot_of[:, t, n_exp:TURNS], -1.0, None, ALU.add))
                dve.wait_ge(acc_ready.sem, acc_ready.at(l, 1))
                dve.sem_inc(route_ready.sem, 1)

                pairs0 = dve.value_load(pairs[0:1, bass.ds(l, 1)], min_val=0, max_val=depth * TURNS // 2)
                pairs1 = dve.value_load(pairs[0:1, bass.ds(l + 1, 1)], min_val=n_exp // 2, max_val=depth * TURNS // 2)
                n_pairs = dve.value_load(pair_n[0:1, 0:1], min_val=n_exp // 2, max_val=TURNS // 2)

                def add_scattered(i, tiles=range(NT)):
                    for n in range(4 * tiles[0], 4 * tiles[-1] + 4):
                        t, c = n // 4, n % 4
                        dve.wait_ge(scat_put.sem, scat_put.at(i + l, n + 1))
                        a = acc[:, t, c * PANEL:(c + 1) * PANEL]
                        tt(a, bank[SCATTER_BANKS[n]][:, :], a, ALU.add).then_inc(scat_added.sem, 1)

                def expert_turn(pair, i, second):
                    dve.wait_ge(gateup_done.sem, i * 2 + 2)
                    dve.tensor_copy(up_part, bank[3][:, :]).then_inc(up_read.sem, 1)
                    dve.wait_ge(fold_done.sem, i + 1)
                    dve.wait_ge(silu_ready.sem, i + 1)
                    tt(hid_t[:, :, :].rearrange("p f s -> p (f s)"), bank[2][:, FC * SLOTS:2 * FC * SLOTS], act_t,
                       ALU.mult).then_inc(hid_ready.sem, 1)
                    add_scattered(i)
                    pick_tokens(pair * 2 + (second + 1)).then_inc(pick_ready.sem, 1)
                    if not second:
                        pick_pair(pair * 2 + 2).then_inc(pick2_ready.sem, 1)
                    for n, c in enumerate(DOWN_ORDER):
                        dve.wait_ge(hi_ready.sem, i * 4 + (n + 1))
                        cols = slice(c * PANEL, (c + 1) * PANEL)
                        stt(out=y_lo[:, cols], in0=bank[4 + c][:, :], scalar=slot_gate[:, 0:1], in1=y_hi[:, cols],
                            op0=ALU.mult, op1=ALU.subtract).then_inc(y_ready.sem, 1)

                with dve.Fori(0, n_pairs) as pair:
                    for second in range(2):
                        expert_turn(pair, dve.snap(pairs0 * 2 + pair * 2 + second), second)
                turns1 = dve.snap(pairs1 * 2)
                for t in range(NT):
                    add_scattered(turns1, [t])
                    dve.wait_ge(scat_added.sem, scat_added.at(turns1 + l, 4 * t + 4))
                    for c in range(4):
                        statistics(t, c, acc)
                    layer_norm(1, t, acc, ln2_loaded, layer_open)
                dve.wait_ge(layer_open.sem, layer_open.at(l + 1, 4))
                s.close()


_INS = ["x", "positions", "w_in", "attn_sinks", "conv_w", "a_log", "dt_bias", "dn_norm_w", "w_out", "ln1_g",
        "ln1_b", "router_w", "router_bias", "w_gate", "w_up", "w_down", "ln2_g", "ln2_b"]


def kernel(**inputs):
    import numpy as _np
    import concourse.bacc as _bacc
    from concourse import mybir as _mybir
    from concourse.bass_utils import run_bass_kernel_spmd as _run

    nc = _bacc.Bacc("TRN2", target_bir_lowering=False, num_devices=1)
    arrays, args = {}, []
    for name in _INS:
        a = _np.ascontiguousarray(inputs[name])
        arrays[f"in_{name}_dram"] = a
        args.append(nc.dram_tensor(f"in_{name}_dram", a.shape, _mybir.dt.from_np(a.dtype), kind="ExternalInput").ap())
    shape = tuple(inputs["x"].shape)
    args.append(nc.dram_tensor("out_0_dram", shape, _mybir.dt.float32, kind="ExternalOutput").ap())
    trunk(nc, *args)
    r = _run(nc, [arrays], core_ids=[0])
    return r.results[0]["out_0_dram"]
```
